# Optimizing a Trainium2 kernel written in Bass

```python
import jax, jax.numpy as jnp
from jax import lax
import numpy as np

D_MODEL = 1024
BATCH = 1
SEQ = 256
DEPTH = 2
DEC_BATCH = 8
DEC_SEQ = 1
PAST_LEN = 1024
PAGE_SIZE = 128

N_EVEN = (DEPTH + 1) // 2
N_ODD = DEPTH // 2
MIX_WIDTH = D_MODEL
CONV_CH = MIX_WIDTH // 2
CONV_GROUPS = 8
CONV_W = 3
SGU_CH = MIX_WIDTH // 2
SGU_GROUPS = 4
SGU_GROUP_CH = SGU_CH // SGU_GROUPS
CHUNK = 128
N_HEADS = 16
HEAD_DIM = MIX_WIDTH // N_HEADS
N_KV_HEADS = 4
GROUP = N_HEADS // N_KV_HEADS
ROPE_DIM = HEAD_DIM // 4
ROPE_THETA = 500000.0
IDX_HEADS = 8
IDX_DIM = 64
IDX_ROPE_DIM = IDX_DIM // 4
TOPK_MAX = 256
Q_BLOCK = 64
D_FF = 256 * ((8 * D_MODEL // 3 + 255) // 256)
N_EXPERTS = 8
TOP_K = 2
D_EXPERT = D_MODEL
ALPHA = (2 * DEPTH) ** 0.25
BETA = (8 * DEPTH) ** -0.25
LN_EPS = 1e-5

EVEN_IN = 3 * CONV_CH + 2 * SGU_CH
EVEN_SPLITS = [CONV_CH, 2 * CONV_CH, 3 * CONV_CH, 3 * CONV_CH + SGU_CH]
Q_END = N_HEADS * HEAD_DIM
K_END = Q_END + N_KV_HEADS * HEAD_DIM
V_END = K_END + N_KV_HEADS * HEAD_DIM
QI_END = V_END + IDX_HEADS * IDX_DIM
KI_END = QI_END + IDX_DIM
ODD_IN = KI_END + IDX_HEADS
ODD_SPLITS = [Q_END, K_END, V_END, QI_END, KI_END]

kernel_name = 'hybrid_conv_sgu_dsa_moe_decoder_step'

def layer_norm(x, g, b):
    xf = x.astype(jnp.float32)
    mu = jnp.mean(xf, axis=-1, keepdims=True)
    var = jnp.mean(jnp.square(xf - mu), axis=-1, keepdims=True)
    return ((xf - mu) * lax.rsqrt(var + LN_EPS) * g.astype(jnp.float32) + b.astype(jnp.float32)).astype(x.dtype)

def deepnorm(x, f, g, b):
    return layer_norm(ALPHA * x + f, g, b)

def rope_partial(x, pos, rot_dim):
    half = rot_dim // 2
    inv = ROPE_THETA ** (-jnp.arange(half, dtype=jnp.float32) / half)
    ang = pos.astype(jnp.float32)[:, None] * inv[None, :]
    cos = jnp.cos(ang)[:, None, :]
    sin = jnp.sin(ang)[:, None, :]
    xf = x.astype(jnp.float32)
    x1, x2, rest = xf[..., :half], xf[..., half:rot_dim], xf[..., rot_dim:]
    out = jnp.concatenate([x1 * cos - x2 * sin, x1 * sin + x2 * cos, rest], axis=-1)
    return out.astype(x.dtype)

def short_conv(z, prev, w):
    t = z.shape[1]
    ext = jnp.concatenate([prev.astype(z.dtype), z], axis=1)
    y = sum(w[j] * ext[:, j:j + t] for j in range(CONV_W))
    return y, ext[:, -(CONV_W - 1):]

def chunk_mix(v, w_s, b_s):
    bsz, t = v.shape[:2]
    pad = (-t) % CHUNK
    vp = jnp.pad(v, ((0, 0), (0, pad), (0, 0), (0, 0)))
    n = (t + pad) // CHUNK
    vc = vp.reshape(bsz, n, CHUNK, SGU_GROUPS, SGU_GROUP_CH)
    causal = jnp.tril(jnp.ones((CHUNK, CHUNK), dtype=bool))
    wm = jnp.where(causal[None], w_s, 0.0).astype(v.dtype)
    s = jnp.einsum('gij,bnjgc->bnigc', wm, vc) + b_s.T[None, None, :, :, None].astype(v.dtype)
    return s.reshape(bsz, n * CHUNK, SGU_GROUPS, SGU_GROUP_CH)[:, :t]

def even_mixer(x, conv_prev, w_in, conv_w, sgu_g, sgu_bn, sgu_w, sgu_b, w_out):
    bsz, t, _ = x.shape
    h = x @ w_in
    gate_b, gate_c, h_in, u, v = jnp.split(h, EVEN_SPLITS, axis=-1)
    conv_out, conv_state = short_conv(gate_c * h_in, conv_prev, conv_w)
    y_a = gate_b * conv_out
    v_n = layer_norm(v, sgu_g, sgu_bn)
    s = chunk_mix(v_n.reshape(bsz, t, SGU_GROUPS, SGU_GROUP_CH), sgu_w, sgu_b).reshape(bsz, t, SGU_CH)
    y_b = u * s
    return jnp.concatenate([y_a, y_b], axis=-1) @ w_out, conv_state, v_n

def odd_project(x, w_in, pos):
    bsz, t, _ = x.shape
    h = x @ w_in
    q, k, v, qi, ki, wi = jnp.split(h, ODD_SPLITS, axis=-1)
    q = rope_partial(q.reshape(bsz, t, N_HEADS, HEAD_DIM), pos, ROPE_DIM)
    k = rope_partial(k.reshape(bsz, t, N_KV_HEADS, HEAD_DIM), pos, ROPE_DIM)
    v = v.reshape(bsz, t, N_KV_HEADS, HEAD_DIM)
    qi = rope_partial(qi.reshape(bsz, t, IDX_HEADS, IDX_DIM), pos, IDX_ROPE_DIM)
    ki = rope_partial(ki.reshape(bsz, t, 1, IDX_DIM), pos, IDX_ROPE_DIM)[:, :, 0]
    wi = wi.astype(jnp.float32) * (IDX_HEADS ** -0.5)
    return q, k, v, qi, ki, wi

def dsa_attend(q, qi, wi, qpos, kidx, gather_kv, topk):
    bsz, tq = q.shape[:2]
    n_keys = kidx.shape[1]
    dots = jnp.einsum('bthd,bsd->bths', qi.astype(jnp.float32), kidx.astype(jnp.float32)) * (IDX_DIM ** -0.5)
    score = jnp.einsum('bth,bths->bts', wi, jax.nn.relu(dots))
    admissible = jnp.arange(n_keys)[None, None, :] <= qpos[None, :, None]
    score = jnp.where(admissible, score, -jnp.inf)
    top_val, sel = lax.top_k(score, topk)
    valid = jnp.isfinite(top_val)
    k_sel, v_sel = gather_kv(sel)
    qg = q.reshape(bsz, tq, N_KV_HEADS, GROUP, HEAD_DIM).astype(jnp.float32)
    logits = jnp.einsum('btkgd,btskd->btkgs', qg, k_sel.astype(jnp.float32)) * (HEAD_DIM ** -0.5)
    logits = jnp.where(valid[:, :, None, None, :], logits, -jnp.inf)
    p = jax.nn.softmax(logits, axis=-1)
    out = jnp.einsum('btkgs,btskd->btkgd', p, v_sel.astype(jnp.float32))
    return out.reshape(bsz, tq, N_HEADS * HEAD_DIM).astype(q.dtype)

def dsa_prompt(q, k, v, qi, ki, wi):
    bsz, t = q.shape[:2]
    topk = min(TOPK_MAX, t // 4)
    bidx = jnp.arange(bsz)[:, None, None]

    def gather(sel):
        return k[bidx, sel], v[bidx, sel]

    def block(start):
        sl = lambda a: lax.dynamic_slice_in_dim(a, start, Q_BLOCK, axis=1)
        qpos = start + jnp.arange(Q_BLOCK)
        return dsa_attend(sl(q), sl(qi), sl(wi), qpos, ki, gather, topk)

    outs = lax.map(block, jnp.arange(0, t, Q_BLOCK))
    return jnp.moveaxis(outs, 0, 1).reshape(bsz, t, N_HEADS * HEAD_DIM)

def dsa_sample(q, k, v, qi, ki, wi, ck, cv, cki, page_table):
    bsz, t = q.shape[:2]
    past = page_table.shape[1] * PAGE_SIZE
    topk = min(TOPK_MAX, (past + t) // 4)
    ki_past = cki[page_table].reshape(bsz, past, IDX_DIM)
    ki_all = jnp.concatenate([ki_past.astype(ki.dtype), ki], axis=1)
    bidx = jnp.arange(bsz)[:, None, None]

    def gather(sel):
        in_past = (sel < past)[..., None, None]
        sp = jnp.minimum(sel, past - 1)
        phys = page_table[bidx, sp // PAGE_SIZE]
        slot = sp % PAGE_SIZE
        sn = jnp.clip(sel - past, 0, t - 1)
        k_g = jnp.where(in_past, ck[phys, slot].astype(k.dtype), k[bidx, sn])
        v_g = jnp.where(in_past, cv[phys, slot].astype(v.dtype), v[bidx, sn])
        return k_g, v_g

    qpos = past + jnp.arange(t)
    return dsa_attend(q, qi, wi, qpos, ki_all, gather, topk)

def swiglu(x, w1, w3, w2):
    return (jax.nn.silu(x @ w1) * (x @ w3)) @ w2

def moe_swiglu(x, wr, br, w1, w3, w2):
    logits = (x @ wr).astype(jnp.float32) + br.astype(jnp.float32)
    top_val, top_idx = lax.top_k(logits, TOP_K)
    gates = jax.nn.softmax(top_val, axis=-1)
    combine = jnp.einsum('btk,btke->bte', gates, jax.nn.one_hot(top_idx, N_EXPERTS, dtype=jnp.float32))
    y = jnp.zeros_like(x)
    for e in range(N_EXPERTS):
        h = jax.nn.silu(x @ w1[e]) * (x @ w3[e])
        y = y + (combine[..., e:e + 1].astype(x.dtype) * h) @ w2[e]
    return y

def setup_inputs(seed: int = 0) -> dict:
    key = jax.random.key(seed)
    ks = jax.random.split(key, 32)
    nrm = lambda k, shape, s: jax.random.normal(k, shape, jnp.float32) * s
    n_pages = PAST_LEN // PAGE_SIZE
    used = DEC_BATCH * n_pages
    n_pool = used + max(1, used // 4)
    page_table = jax.random.permutation(ks[6], n_pool)[:used].reshape(DEC_BATCH, n_pages).astype(jnp.int32)
    return {
        'x_prompt': nrm(ks[0], (BATCH, SEQ, D_MODEL), 1.0),
        'x_sample': nrm(ks[1], (DEC_BATCH, DEC_SEQ, D_MODEL), 1.0),
        'cache_k': nrm(ks[2], (N_ODD, n_pool, PAGE_SIZE, N_KV_HEADS, HEAD_DIM), 1.0),
        'cache_v': nrm(ks[3], (N_ODD, n_pool, PAGE_SIZE, N_KV_HEADS, HEAD_DIM), 1.0),
        'cache_kidx': nrm(ks[4], (N_ODD, n_pool, PAGE_SIZE, IDX_DIM), 1.0),
        'state_conv': nrm(ks[5], (N_EVEN, DEC_BATCH, CONV_W - 1, CONV_CH), 1.0),
        'page_table': page_table,
        'ln1_g': 1.0 + nrm(ks[7], (DEPTH, D_MODEL), 0.05),
        'ln1_b': nrm(ks[8], (DEPTH, D_MODEL), 0.02),
        'ln2_g': 1.0 + nrm(ks[9], (DEPTH, D_MODEL), 0.05),
        'ln2_b': nrm(ks[10], (DEPTH, D_MODEL), 0.02),
        'w_in_even': nrm(ks[11], (N_EVEN, D_MODEL, EVEN_IN), D_MODEL ** -0.5),
        'conv_w': nrm(ks[12], (N_EVEN, CONV_W, CONV_CH), CONV_W ** -0.5),
        'sgu_ln_g': 1.0 + nrm(ks[13], (N_EVEN, SGU_CH), 0.05),
        'sgu_ln_b': nrm(ks[14], (N_EVEN, SGU_CH), 0.02),
        'sgu_w': nrm(ks[15], (N_EVEN, SGU_GROUPS, CHUNK, CHUNK), CHUNK ** -0.5),
        'sgu_b': 1.0 + nrm(ks[16], (N_EVEN, SGU_GROUPS, CHUNK), 0.1),
        'w_out_even': nrm(ks[17], (N_EVEN, MIX_WIDTH, D_MODEL), BETA * MIX_WIDTH ** -0.5),
        'ffn_w1': nrm(ks[18], (N_EVEN, D_MODEL, D_FF), D_MODEL ** -0.5),
        'ffn_w3': nrm(ks[19], (N_EVEN, D_MODEL, D_FF), D_MODEL ** -0.5),
        'ffn_w2': nrm(ks[20], (N_EVEN, D_FF, D_MODEL), BETA * D_FF ** -0.5),
        'w_in_odd': nrm(ks[21], (N_ODD, D_MODEL, ODD_IN), D_MODEL ** -0.5),
        'w_out_odd': nrm(ks[22], (N_ODD, N_HEADS * HEAD_DIM, D_MODEL), BETA * (N_HEADS * HEAD_DIM) ** -0.5),
        'router_w': nrm(ks[23], (N_ODD, D_MODEL, N_EXPERTS), D_MODEL ** -0.5),
        'router_b': nrm(ks[24], (N_ODD, N_EXPERTS), 0.01),
        'moe_w1': nrm(ks[25], (N_ODD, N_EXPERTS, D_MODEL, D_EXPERT), D_MODEL ** -0.5),
        'moe_w3': nrm(ks[26], (N_ODD, N_EXPERTS, D_MODEL, D_EXPERT), D_MODEL ** -0.5),
        'moe_w2': nrm(ks[27], (N_ODD, N_EXPERTS, D_EXPERT, D_MODEL), BETA * D_EXPERT ** -0.5),
    }

def reference(x_prompt, x_sample, cache_k, cache_v, cache_kidx, state_conv, page_table,
              ln1_g, ln1_b, ln2_g, ln2_b, w_in_even, conv_w, sgu_ln_g, sgu_ln_b, sgu_w, sgu_b,
              w_out_even, ffn_w1, ffn_w3, ffn_w2, w_in_odd, w_out_odd, router_w, router_b,
              moe_w1, moe_w3, moe_w2):
    bp, tp, _ = x_prompt.shape
    past = page_table.shape[1] * PAGE_SIZE
    pos_p = jnp.arange(tp)
    pos_s = past + jnp.arange(x_sample.shape[1])
    xp, xs = x_prompt, x_sample
    k_p, v_p, ki_p, conv_p = [], [], [], []
    k_s, v_s, ki_s, conv_s, chunk_s = [], [], [], [], []
    for layer in range(DEPTH):
        i = layer // 2
        if layer % 2 == 0:
            ew = (w_in_even[i], conv_w[i], sgu_ln_g[i], sgu_ln_b[i], sgu_w[i], sgu_b[i], w_out_even[i])
            zero_prev = jnp.zeros((bp, CONV_W - 1, CONV_CH), xp.dtype)
            mp, cp, _ = even_mixer(xp, zero_prev, *ew)
            ms, cs, vs = even_mixer(xs, state_conv[i], *ew)
            conv_p.append(cp)
            conv_s.append(cs)
            chunk_s.append(vs)
            xp = deepnorm(xp, mp, ln1_g[layer], ln1_b[layer])
            xs = deepnorm(xs, ms, ln1_g[layer], ln1_b[layer])
            xp = deepnorm(xp, swiglu(xp, ffn_w1[i], ffn_w3[i], ffn_w2[i]), ln2_g[layer], ln2_b[layer])
            xs = deepnorm(xs, swiglu(xs, ffn_w1[i], ffn_w3[i], ffn_w2[i]), ln2_g[layer], ln2_b[layer])
        else:
            qp, kp, vp, qip, kip, wip = odd_project(xp, w_in_odd[i], pos_p)
            ap = dsa_prompt(qp, kp, vp, qip, kip, wip) @ w_out_odd[i]
            qs, kn, vn, qis, kis, wis = odd_project(xs, w_in_odd[i], pos_s)
            a_s = dsa_sample(qs, kn, vn, qis, kis, wis, cache_k[i], cache_v[i], cache_kidx[i], page_table) @ w_out_odd[i]
            k_p.append(kp)
            v_p.append(vp)
            ki_p.append(kip)
            k_s.append(kn)
            v_s.append(vn)
            ki_s.append(kis)
            xp = deepnorm(xp, ap, ln1_g[layer], ln1_b[layer])
            xs = deepnorm(xs, a_s, ln1_g[layer], ln1_b[layer])
            mw = (router_w[i], router_b[i], moe_w1[i], moe_w3[i], moe_w2[i])
            xp = deepnorm(xp, moe_swiglu(xp, *mw), ln2_g[layer], ln2_b[layer])
            xs = deepnorm(xs, moe_swiglu(xs, *mw), ln2_g[layer], ln2_b[layer])
    y_prompt, y_sample = xp, xs
    k_prompt, v_prompt, kidx_prompt = jnp.stack(k_p), jnp.stack(v_p), jnp.stack(ki_p)
    conv_prompt = jnp.stack(conv_p)
    k_sample, v_sample, kidx_sample = jnp.stack(k_s), jnp.stack(v_s), jnp.stack(ki_s)
    conv_sample = jnp.stack(conv_s)
    chunk_v_sample = jnp.stack(chunk_s)
    return (y_prompt, y_sample, k_prompt, v_prompt, kidx_prompt, conv_prompt,
            k_sample, v_sample, kidx_sample, conv_sample, chunk_v_sample)


_drawn_inputs = setup_inputs


def setup_inputs(seed=0):
    import zlib

    import numpy as np

    out = dict(_drawn_inputs(seed))
    spreads = {}
    factors = {'sgu_ln_b': 3.013, 'router_b': 5.914}
    for name, (base, spread) in spreads.items():
        noise = np.random.default_rng([zlib.crc32(name.encode()), seed]).standard_normal(out[name].shape)
        drawn = base * np.exp(spread * noise) if base else spread * noise
        out[name] = __import__('jax').numpy.asarray(drawn.astype(out[name].dtype))
    for name, factor in factors.items():
        out[name] = (out[name] * factor).astype(out[name].dtype)
    return out
```

```python
from contextlib import ExitStack

import numpy as np

import concourse.bass as bass
from concourse import mybir

F32 = mybir.dt.float32
I32 = mybir.dt.int32
U32 = mybir.dt.uint32
ALU = mybir.AluOpType
ACT = mybir.ActivationFunctionType
AX = mybir.AxisListType.X

P = 128
D = 1024
KD = D // P
TP, TS = 256, 8
T = TP + TS
CH = 512
FF = 2816
KF = FF // P
NE = 8
PAST, PAGE = 1024, 128
NPOOL = 80
NPG = PAST // PAGE
RUN = 8
TOPK_P, TOPK_S = 64, 256
ALPHA = 4.0 ** 0.25
EPS = 1e-5
NEG = -1e30
TAKEN = -3e38
NSLOT = 6
NB = 4

V_LN1G, V_LN1B, V_LN2G, V_LN2B, V_SG, V_SB, V_CW, NVEC = 0, 16, 32, 48, 64, 68, 72, 84
QI, KI, KK, VV, QQ = 0, 4, 5, 7, 9
ROPED = [QI, QI + 1, QI + 2, QI + 3, KI, KK, KK + 1] + [QQ + c for c in range(KD)]


class Count:

    def __init__(self, sem):
        self.sem, self.base, self.k, self.phase = sem, 0, 0, 0

    def inc(self, ins, by=1):
        ins.then_inc(self.sem, by)
        self.k += by
        return self.base + self.k

    def enter(self, i, per):
        self.start, self.per = self.base + self.k, per
        self.base, self.k, self.phase = self.start + i * per, 0, self.start

    def leave(self, n):
        assert self.k == self.per, (self.k, self.per)
        self.base, self.k = 0, self.start + n * self.per
        self.phase = 0


def build(nc, x_prompt, x_sample, cache_k, cache_v, cache_kidx, state_conv, page_table,
          ln1_g, ln1_b, ln2_g, ln2_b, w_in_even, conv_w, sgu_ln_g, sgu_ln_b, sgu_w, sgu_b,
          w_out_even, ffn_w1, ffn_w3, ffn_w2, w_in_odd, w_out_odd, router_w, router_b,
          moe_w1, moe_w3, moe_w2, c_square, c_rope, c_pick,
          y_p, y_s, k_p, v_p, ki_p, conv_p, k_s, v_s, ki_s, conv_s, chunk_s):
    ctx = ExitStack()
    with ctx:
        ctx.enter_context(nc.allow_non_contiguous_dma(reason="small tables and packed vectors"))

        def sb(name, shape, dt=F32):
            return ctx.enter_context(nc.sbuf_tensor(name, shape, dt))

        def sem(name):
            return ctx.enter_context(nc.semaphore(name))

        slot = [sb(f"slot{i}", [P, 4096]) for i in range(NSLOT)]
        xT = sb("xT", [P, KD, T])
        rT = sb("rT", [P, KD, T])
        sqT = sb("sqT", [P, KD, T])
        hT = sb("hT", [P, KF, T])
        yT = sb("yT", [P, KD, T])
        scr = sb("scr", [P, 6144])
        kbuf = [sb("kbuf", [P, 4 * 256]), hT[:, 17:21, :].rearrange("p c t -> p (c t)")[:, 0:1024]]
        kibuf = [sb(f"kibuf{i}", [P, RUN * 64]) for i in range(2)]
        square = sb("square", [P, 3, P])
        rope = sb("rope", [P, 2, T])
        pick = sb("pick", [8, P])
        ones = sb("ones", [P, P])
        one8 = sb("one8", [8, P])
        vecraw = sb("vecraw", [NVEC, P])
        vec = sb("vec", [P, NVEC])
        mean = sb("mean", [P, T])
        var = sb("var", [P, T])
        rstd = sb("rstd", [P, T])
        silu = sb("silu", [P, 2, T])
        eps = sb("eps", [P, 1])
        w00 = sb("w00", [P, 2, 4])
        idx = sb("idx", [P, 3, NPG], I32)
        idxf = sb("idxf", [P, NPG])
        sg = sb("sg", [P, 1])
        wrt = sb("wrt", [P, KD, NE])
        wrb = sb("wrb", [1, NE])
        ktv = sb("ktv", [P, 2, 512])
        kvs = sb("kvs", [8, 512])
        kit = sb("kit", [P, 3, 64])
        wit = sb("wit", [P, 2, 8])
        wiT = sb("wiT", [8, T])
        stat = sb("stat", [P, 24])
        qiB = sb("qiB", [P, 8, 8])
        rt = sb("rt", [P, 3, 48])
        iota8 = sb("iota8", [P, 8])
        mxi = sb("mxi", [P, 8], U32)
        mx8p = sb("mx8p", [P, 8])
        one_cell = sb("one_cell", [1, 2])

        ident = square[:, 0, :]
        rot = square[:, 1, :]
        swap = square[:, 2, :]

        ps = [ctx.enter_context(nc.psum_tensor(f"ps{i}", [P, 512], F32)) for i in range(8)]

        xtok = scr[:, 0:2048].rearrange("p (t d) -> p t d", t=2)
        xstok = scr[0:8, 2048:3072]
        zext = scr[:, 0:4 * 258].rearrange("p (c t) -> p c t", c=4)
        vtok = scr[:, 1040:2064].rearrange("p (t c) -> p t c", t=2)
        wsT = scr[:, 3072:3584].rearrange("p (g i) -> p g i", g=4)
        wsr = scr[:, 3584:4096].rearrange("p (g j) -> p g j", g=4)
        stT = scr[:, 4096:4160].rearrange("p (c n) -> p c n", c=4)
        str_ = scr[0:16, 4160:4672]
        zlast = scr[:, 4672:4712].rearrange("p (c n) -> p c n", c=4)
        zrow = scr[0:10, 4736:5248]
        vrow = scr[0:8, 5248:5760]
        sgb = scr[0:1, 5248:5760]
        cst = scr[:, 5760:5760 + 256]
        css = scr[:, 6016:6024]
        rel = [scr[:, 512 * i:512 * i + 512].rearrange("p (h s) -> p h s", h=2) for i in range(2)]
        sc = scr[:, 1024:1536].rearrange("p (t s) -> p t s", t=2)
        work = scr[:, 1536:2048].rearrange("p (t s) -> p t s", t=2)
        S = [scr[:, 2048 + 1024 * i:3072 + 1024 * i].rearrange("p (u h s) -> p u h s", u=2, h=2) for i in range(2)]
        PT = [scr[:, 4096 + 1024 * i:5120 + 1024 * i] for i in range(2)]
        kiT = [scr[:, 512 * i:512 * i + 512] for i in range(2)]
        srel = scr[:, 1024:1600]
        wib = scr[:, 1600:1664]
        dwi = scr[0:8, 1664:1728]
        score = scr[:, 1728:1792].rearrange("p (a r b) -> p a r b", a=2, r=4)
        sc9 = scr[0:8, 1792:1800]
        row = scr[0:8, 1808:2840]
        qbd = scr[:, 2848:2976].rearrange("p (j b x) -> p j b x", j=2, b=8)
        KT = [scr[:, 3072 + 1024 * i:4096 + 1024 * i].rearrange("p (r j s) -> p r j s", r=4, j=2) for i in range(2)]
        lgS = scr[:, 0:1152]
        SS = scr[:, 3072:3072 + 1032]
        bSS = scr[:, 4112:4112 + 1032]
        PTs = scr[:, 0:1152].rearrange("p (r q) -> p r q", r=9)
        st8 = scr[:, 5152:5168]
        mx8 = scr[0:8, 5168:5176]
        combT = wiT
        yacc = hT[:, KD:2 * KD, :]
        ytile = hT[:, 0:12, 0:256]

        def slab(s, k, n):
            return slot[s][:, 0:k * n].rearrange("p (k n) -> p k n", k=k)

        consts_in, x_in, even_in, idx_in = sem("consts_in"), sem("x_in"), sem("even_in"), sem("idx_in")
        slab_in = [sem(f"slab_in{s}") for s in range(NSLOT)]
        pool_consts, causal_w = sem("pool_consts"), sem("causal_w")
        group_done = sem("group_done")
        group_free = sem("group_free")
        silu_done = sem("silu_done")
        even_t, even_tc = sem("even_t"), sem("even_tc")
        resid_done, sq_done = sem("resid_done"), sem("sq_done")
        stats_done, var_done, std_done = sem("stats_done"), sem("var_done"), sem("std_done")
        centred, x_ready = sem("centred"), sem("x_ready")
        vt_done, vt_copied = sem("vt_done"), sem("vt_copied")
        z_done, z_t, z_copied = sem("z_done"), sem("z_t"), sem("z_copied")
        rot_done, roped = sem("rot_done"), sem("roped")
        tok_t, tok_copied = sem("tok_t"), sem("tok_copied")
        dots_done, rel_done, rel_used = sem("dots_done"), sem("rel_done"), sem("rel_used")
        sc_causal, bias_done, bias_causal = sem("sc_causal"), sem("bias_done"), sem("bias_causal")
        lg_done, lg_read, exp_done, prob_done = sem("lg_done"), sem("lg_read"), sem("exp_done"), sem("prob_done")
        pt_done, pt_copied, o_done, o_copied = sem("pt_done"), sem("pt_copied"), sem("o_done"), sem("o_copied")
        idx_done = sem("idx_done")
        ki_in = [sem(f"ki_in{i}") for i in range(2)]
        ki_mm, k_mm = sem("ki_mm"), sem("k_mm")
        ki_t, ki_copied, qi_ready, swapped = sem("ki_t"), sem("ki_copied"), sem("qi_ready"), sem("swapped")
        wib_in, wib_done, sdots, srel_done = sem("wib_in"), sem("wib_done"), sem("sdots"), sem("srel_done")
        score_done, new_masked, row_t, row_done = sem("score_done"), sem("new_masked"), sem("row_t"), sem("row_done")
        row_masked, mask_wide, mask_copied = sem("row_masked"), sem("mask_wide"), sem("mask_copied")
        k_in = [sem(f"k_in{i}") for i in range(2)]
        v_in = [sem(f"v_in{i}") for i in range(2)]
        qbd_done, k_t, k_copied = sem("qbd_done"), sem("k_t"), sem("k_copied")
        slg_done, slg_copied, slg_t = sem("slg_done"), sem("slg_copied"), sem("slg_t")
        smax_done, sexp_done, sprob_done = sem("smax_done"), sem("sexp_done"), sem("sprob_done")
        spt_done, spt_copied, v_used, so_done = sem("spt_done"), sem("spt_copied"), sem("v_used"), sem("so_done")
        route_in, route_done, gate_e, comb_done, comb_t, combT_done, comb_wide, comb_ready = (
            sem("route_in"), sem("route_done"), sem("gate_e"), sem("comb_done"), sem("comb_t"),
            sem("combT_done"), sem("comb_wide"), sem("comb_ready"))
        yt_done, yt_copied = sem("yt_done"), sem("yt_copied")
        even_stored, state_stored, kv_stored, y_stored = (
            sem("even_stored"), sem("state_stored"), sem("kv_stored"), sem("y_stored"))
        dchain = sem("dchain")

        block = ctx.enter_context(nc.Block())

        S_EIN, S_EOUT, S_UP, S_UPLAST = (0, 1, 2, 3, 4), (5, 0), (1, 2, 3, 4, 5), 0
        S_DOWN, S_OIN, S_OOUT = (1, 2, 3, 4), (5, 0, 1, 2, 3), (4, 5)
        EIN_ORDER = (4, 1, 2, 3, 0)
        G_EIN = KD
        G_MIX = G_EIN + 20
        G_EOUT = G_MIX + 4
        G_UP = G_EOUT + KD
        G_DOWN = G_UP + 2 * KF
        G_OIN = G_DOWN + KD
        G_OOUT = G_OIN + 18
        G_COMB = G_OOUT + KD
        G_MOE = G_COMB + NE
        G_EXP = 3 * KD

        kdim = "(k p) n -> p k n"

        def up_views(s):
            v = slot[s][:, :].rearrange("p (w k n) -> p w k n", w=2, k=KD)
            return v[:, 0], v[:, 1]

        @block.sync
        def _(sp):
            last = [None] * NSLOT

            def slot_free(s, value):
                if last[s] is not None:
                    sp.wait_ge(group_done, last[s])
                last[s] = value

            def load(s, dst, src):
                sp.dma_start(dst, src).then_inc(slab_in[s], 16)

            sp.dma_start(xtok, x_prompt[0].rearrange("(t p) d -> p t d", p=P)).then_inc(x_in, 16)
            sp.dma_start(xstok, x_sample[:, 0, :]).then_inc(x_in, 16)
            sp.dma_start(square[:], c_square.rearrange("a p q -> p a q")).then_inc(consts_in, 16)
            w = w_in_even[0].rearrange(kdim, p=P)
            for n, (s, c) in enumerate(zip(S_EIN, EIN_ORDER)):
                slot_free(s, G_EIN + 4 * (n + 1))
                load(s, slab(s, KD, 512), w[:, :, 512 * c:512 * c + 512])
            w = w_out_even[0].rearrange(kdim, p=P)
            for c, s in enumerate(S_EOUT):
                slot_free(s, G_EOUT + 4 * (c + 1))
                load(s, slab(s, KD, 512), w[:, :, 512 * c:512 * c + 512])
            w1, w3 = (w[0].rearrange(kdim, p=P) for w in (ffn_w1, ffn_w3))
            before = [last[s] for s in S_UP]
            with sp.Fori(0, 2) as i:
                for n, s in enumerate(S_UP):
                    sp.wait_ge(group_done, before[n] + i * (G_UP + 4 * (n + 1) - before[n]))
                    a, b = up_views(s)
                    load(s, a, w1[:, :, bass.ds(i * 1280 + n * 256, 256)])
                    load(s, b, w3[:, :, bass.ds(i * 1280 + n * 256, 256)])
            for n, s in enumerate(S_UP):
                last[s] = G_UP + 20 + 4 * (n + 1)
            slot_free(S_UPLAST, G_DOWN)
            a, b = up_views(S_UPLAST)
            load(S_UPLAST, a, w1[:, :, 2560:2816])
            load(S_UPLAST, b, w3[:, :, 2560:2816])
            w2 = ffn_w2[0].rearrange("(u k p) n -> p u k n", p=P, u=2)
            before = [last[s] for s in S_DOWN]
            with sp.Fori(0, 2) as i:
                for n, s in enumerate(S_DOWN):
                    sp.wait_ge(group_done, before[n] + i * (G_DOWN + 2 * (n // 2 + 1) - before[n]))
                    load(s, slab(s, 11, 256), w2[:, n % 2, :, bass.ds(i * 512 + (n // 2) * 256, 256)])
            for n, s in enumerate(S_DOWN):
                last[s] = G_DOWN + 4 + 2 * (n // 2 + 1)
            w = w_in_odd[0].rearrange(kdim, p=P)
            slot_free(S_OIN[0], G_OIN + 4)
            load(S_OIN[0], slab(S_OIN[0], KD, 512), w[:, :, 1536:2048])
            slot_free(S_OIN[1], G_OIN + 6)
            v = slab(S_OIN[1], KD, 136)
            load(S_OIN[1], v[:, :, 0:64], w[:, :, 2048:2112])
            load(S_OIN[1], v[:, :, 64:136], w[:, :, 2048:2120])
            slot_free(S_OIN[2], G_OIN + 10)
            load(S_OIN[2], slab(S_OIN[2], KD, 512), w[:, :, 1024:1536])
            for c in range(2):
                slot_free(S_OIN[3 + c], G_OIN + 14 + 4 * c)
                v = slab(S_OIN[3 + c], KD, 512)
                for i in range(4):
                    for a in range(2):
                        src = 512 * c + 256 * a + 64 * i
                        load(S_OIN[3 + c], v[:, :, P * i + 64 * a:P * i + 64 * a + 64], w[:, :, src:src + 64])
            for c, s in enumerate(S_OOUT):
                slot_free(s, G_OOUT + 4 * (c + 1))
                for half in range(2):
                    v = slab(s, KD, 512)[64 * half:64 * half + 64]
                    for j in range(2):
                        src = w_out_odd[0, 512 * j + 256 * half:512 * j + 256 * half + 256, 512 * c:512 * c + 512]
                        load(s, v[:, 4 * j:4 * j + 4, :], src.rearrange("(i d) n -> d i n", d=64))

            def load_expert(s, e):
                if s < 4:
                    for v, w in zip(up_views(s), (moe_w1[0], moe_w3[0])):
                        src = w[bass.ds(e, 1), :, 256 * s:256 * s + 256]
                        load(s, v, src.rearrange("e (k p) n -> p (e k) n", p=P))
                else:
                    src = moe_w2[0][bass.ds(e, 1), :, 512 * (s - 4):512 * (s - 4) + 512]
                    load(s, slab(s, KD, 512), src.rearrange("e (k p) n -> p (e k) n", p=P))

            sp.wait_ge(z_copied, 2)
            sp.dma_start(conv_p[0, 0], zrow[0:2, :]).then_inc(even_stored, 16)
            sp.dma_start(conv_s[0, :, 1, :], zrow[2:10, :]).then_inc(even_stored, 16)
            sp.dma_start(chunk_s[0, :, 0, :], vrow).then_inc(even_stored, 16)
            for s in range(4):
                slot_free(s, None)
                load_expert(s, 0)
            sp.wait_ge(tok_copied, 5)
            kv = lambda a: a[0, 0].rearrange("(t p) h d -> p t (h d)", p=P)
            sp.dma_start(kv(k_p), ktv[:, :, 0:256]).then_inc(kv_stored, 16)
            sp.dma_start(kv(v_p), ktv[:, :, 256:512]).then_inc(kv_stored, 16)
            sp.dma_start(ki_p[0, 0].rearrange("(t p) d -> p t d", p=P), kit[:, 0:2, :]).then_inc(kv_stored, 16)
            sp.dma_start(k_s[0, :, 0].rearrange("b h d -> b (h d)"), kvs[:, 0:256]).then_inc(kv_stored, 16)
            sp.dma_start(v_s[0, :, 0].rearrange("b h d -> b (h d)"), kvs[:, 256:512]).then_inc(kv_stored, 16)
            sp.dma_start(ki_s[0, :, 0], kit[0:8, 2, :]).then_inc(kv_stored, 16)
            for s in (4, 5):
                slot_free(s, None)
                load_expert(s, 0)
            with sp.Fori(1, NE) as e:
                for s in range(NSLOT):
                    sp.wait_ge(group_done, G_MOE + (e - 1) * G_EXP + 4 * (s + 1))
                    load_expert(s, e)
            for t in range(3):
                sp.wait_ge(yt_copied, 2 * (t + 1))
                m = P if t < 2 else 8
                dst = y_p[0, P * t:P * t + P, :] if t < 2 else y_s[:, 0, :]
                sp.dma_start(dst.rearrange("p (c q) -> p c q", q=256), ytile[0:m, 4 * t:4 * t + 4, :]).then_inc(y_stored, 16)
            for stored, n in ((even_stored, 3), (state_stored, 1), (kv_stored, 6), (y_stored, 3)):
                sp.wait_ge(stored, 16 * n)

        @block.gpsimd
        def _(pool):
            pool.memset(ones[:], 1.0 / D).then_inc(pool_consts, 1)
            pool.memset(one8[:], 1.0).then_inc(pool_consts, 1)
            pool.iota(iota8[:], pattern=[[1, 8]], base=0, channel_multiplier=0,
                      allow_small_or_imprecise_dtypes=True).then_inc(pool_consts, 1)
            pool.memset(one_cell[:], 0.0).then_inc(pool_consts, 1)
            pool.memset(eps[:], EPS).then_inc(pool_consts, 1)
            n = 0
            for dst, src in ((vecraw[0:16], ln1_g.rearrange("l (c p) -> (l c) p", p=P)),
                             (vecraw[16:32], ln1_b.rearrange("l (c p) -> (l c) p", p=P)),
                             (vecraw[32:48], ln2_g.rearrange("l (c p) -> (l c) p", p=P)),
                             (vecraw[48:64], ln2_b.rearrange("l (c p) -> (l c) p", p=P)),
                             (vecraw[64:68], sgu_ln_g.rearrange("l (c p) -> (l c) p", p=P)),
                             (vecraw[68:72], sgu_ln_b.rearrange("l (c p) -> (l c) p", p=P)),
                             (vecraw[72:84], conv_w[0].rearrange("w (c p) -> (w c) p", p=P)),
                             (wsr, sgu_w[0].rearrange("g i j -> i g j")),
                             (sgb, sgu_b.rearrange("l g i -> l (g i)")),
                             (str_, state_conv[0].rearrange("b w c -> (b w) c")),
                             (w00[:, 0, :], sgu_w[0, :, 0, 0:1].rearrange("g a -> a g").to_broadcast([P, 4])),
                             (w00[:, 1, :], sgu_b[0, :, 0:1].rearrange("g a -> a g").to_broadcast([P, 4]))):
                pool.dma_start(dst, src).then_inc(even_in, 16)
                n += 1
            assert n == 12
            pool.dma_start(rope[:], c_rope.rearrange("a p t -> p a t")).then_inc(idx_in, 16)
            pool.dma_start(pick[:], c_pick[0:8, :]).then_inc(idx_in, 16)
            pool.dma_start(sg[:], c_pick[8:9, :].rearrange("a p -> p a")).then_inc(idx_in, 16)
            pool.dma_start(wrt[:], router_w[0].rearrange("(k p) e -> p k e", p=P)).then_inc(idx_in, 16)
            pool.dma_start(wrb[:], router_b).then_inc(idx_in, 16)
            for pg in range(NPG):
                src = page_table[:, pg:pg + 1].rearrange("b a -> a b").to_broadcast([16, TS])
                pool.dma_start(idx[16 * pg:16 * pg + 16, 0, :], src).then_inc(idx_in, 16)
            pool.wait_ge(even_in, 16 * 12)
            pool.affine_select(out=wsr, in_=wsr, pattern=[[0, 4], [-1, P]], compare_op=ALU.is_ge, fill=0.0,
                               base=0, channel_multiplier=1).then_inc(causal_w, 1)
            pool.dma_start(conv_s[0, :, 0, :], str_[1:16:2, :]).then_inc(state_stored, 16)

            pool.wait_ge(idx_done, 1)
            kirows = cache_kidx[0].rearrange("n (r s) d -> (n r) (s d)", s=RUN)
            krows = cache_k[0].rearrange("n (r s) h d -> (n r) (s h d)", s=4)
            vrows = cache_v[0].rearrange("n (r s) h d -> (n r) (s h d)", s=RUN)
            off = lambda a, b: bass.IndirectOffsetOnAxis(ap=idx[:, a, b:b + 1].bitcast(U32), axis=0)

            def gather_ki(b):
                pool.indirect_dma_start(out=kibuf[b % 2][:], out_offset=None, in_=kirows,
                                        in_offset=off(0, b)).then_inc(ki_in[b % 2], 16)

            def gather_k(u):
                pool.indirect_dma_start(out=kbuf[u % 2][:], out_offset=None, in_=krows,
                                        in_offset=off(1 + u % 2, u // 2)).then_inc(k_in[u % 2], 16)

            def gather_v(b):
                dst = (rT, sqT)[b % 2][:].rearrange("p c t -> p (c t)")[:, 0:RUN * 256]
                pool.indirect_dma_start(out=dst, out_offset=None, in_=vrows,
                                        in_offset=off(0, b)).then_inc(v_in[b % 2], 16)

            for b in range(2):
                gather_ki(b)
            pool.wait_ge(x_ready, 4 + 2 * KD)
            for u in range(2):
                gather_k(u)
            for b in range(2):
                gather_v(b)
            for t in range(2):
                pool.wait_ge(rel_used, 4 * (t + 1))
                pool.affine_select(out=sc[:, t, 0:P * (t + 1)], in_=sc[:, t, 0:P * (t + 1)], pattern=[[-1, P * (t + 1)]], compare_op=ALU.is_ge,
                                   fill=NEG, base=P * t, channel_multiplier=1).then_inc(sc_causal, 1)
            for t in range(2):
                pool.wait_ge(bias_done, t + 1)
                pool.affine_select(out=work[:, t, 0:P * (t + 1)], in_=work[:, t, 0:P * (t + 1)], pattern=[[-1, P * (t + 1)]], compare_op=ALU.is_ge,
                                   fill=NEG, base=P * t, channel_multiplier=1).then_inc(bias_causal, 1)
            for b in range(2, TS):
                pool.wait_ge(ki_t, b - 1)
                gather_ki(b)
            pool.wait_ge(score_done, 2)
            pool.affine_select(out=sc9, in_=sc9, pattern=[[-1, 8]], compare_op=ALU.is_equal, fill=NEG,
                               base=0, channel_multiplier=1).then_inc(new_masked, 1)
            for u in range(2, 2 * TS):
                pool.wait_ge(k_t, 2 * (u - 1))
                gather_k(u)
            for b in range(2, TS):
                pool.wait_ge(v_used, b - 1)
                gather_v(b)

        @block.tensor
        def _(pe):
            done = Count(group_done)
            loads = [Count(s) for s in slab_in]
            got = [0]

            def arrived(s, by=16):
                loads[s].k += by
                pe.wait_ge(slab_in[s], loads[s].base + loads[s].k)

            def bank():
                g = done.base + done.k
                if done.phase + done.k >= NB:
                    pe.wait_ge(group_free, g - (NB - 1))
                return ps[(done.phase + done.k) % NB]

            def group(lhs, rhs, n, m=P):
                out = bank()[0:m, 0:T]
                for k in range(n):
                    mm = pe.matmul(out, lhs(k), rhs(k), start=(k == 0), stop=(k == n - 1))
                done.inc(mm)

            def stats(c, n, src, sq, ready):
                if c == 0 and got[0]:
                    pe.wait_ge(var_done, got[0])
                pe.wait_ge(*ready)
                squares[0] += 1
                pe.wait_ge(sq_done, squares[0])
                pe.matmul(ps[4][:, 0:T], ones[:], src[:, c, :], start=(c == 0), stop=(c == n - 1))
                mm = pe.matmul(ps[5][:, 0:T], ones[:], sq[:, c, :], start=(c == 0), stop=(c == n - 1))
                if c == n - 1:
                    mm.then_inc(stats_done, 1)
                    got[0] += 1

            squares = [0]

            def proj_with_stats(slots, rhs, g0, by=16):
                for n, s in enumerate(slots):
                    arrived(s, by)
                    for j in range(4):
                        c = 4 * n + j
                        group(lambda k: slab(s, KD, 512)[:, k, P * j:P * j + P], rhs, KD)
                        if c:
                            stats(c - 1, KD, rT, sqT, (group_free, g0 + c))
                stats(KD - 1, KD, rT, sqT, (group_free, g0 + KD))

            x = lambda k: xT[:, k, :]
            y = lambda k: yT[:, k, :]

            pe.wait_ge(consts_in, 16)
            pe.wait_ge(x_in, 32)
            for c in range(KD):
                b = bank()
                for t in range(2):
                    pe.transpose(b[:, P * t:P * t + P], xtok[:, t, P * c:P * c + P], ident)
                done.inc(pe.transpose(b[:, TP:T], xstok[:, P * c:P * c + P], square[0:8, 0, 0:8]))
            pe.wait_ge(even_in, 16 * 12)
            pe.wait_ge(causal_w, 1)
            pe.wait_ge(pool_consts, 5)
            pe.transpose(ps[6][:, 0:NVEC], vecraw[:], square[0:NVEC, 0, 0:NVEC])
            for c in range(4):
                mm = pe.transpose(ps[6][:, 128 + 16 * c:144 + 16 * c], str_[:, P * c:P * c + P], square[0:16, 0, 0:16])
            mm.then_inc(even_t, 1)
            for g in range(4):
                mm = pe.transpose(ps[7][:, P * g:P * g + P], wsr[:, g, :], ident)
            mm.then_inc(even_t, 1)

            pe.wait_ge(group_free, KD)
            for n, s in enumerate(S_EIN):
                arrived(s)
                for j in range(4):
                    group(lambda k: slab(s, KD, 512)[:, k, P * j:P * j + P], x, KD)
                if n == 1:
                    for c in range(4):
                        stats(c, 4, hT[:, 16:20, :], sqT, (group_free, G_EIN + c + 1))
                if n == 3:
                    pe.wait_ge(x_ready, 4)
                    pe.wait_ge(even_tc, 2)
                    for t in range(2):
                        for c in range(4):
                            mm = pe.transpose(ps[6 + t][:, P * c:P * c + P], hT[:, 16 + c, P * t:P * t + P], ident)
                    mm.then_inc(vt_done, 1)
            pe.wait_ge(vt_copied, 1)
            for g in range(4):
                b = bank()
                for t in range(2):
                    pe.matmul(b[:, P * t:P * t + P], vtok[:, t, P * g:P * g + P], wsT[:, g, :], start=True, stop=False)
                    mm = pe.matmul(b[:, P * t:P * t + P], one8[0:1, :], sgb[:, P * g:P * g + P], start=False, stop=True)
                done.inc(mm)
            pe.wait_ge(z_done, 1)
            for c in range(4):
                mm = pe.transpose(ps[6][0:10, P * c:P * c + P], zlast[:, c, :], ident)
            mm.then_inc(z_t, 1)
            for c in range(4):
                mm = pe.transpose(ps[7][0:8, P * c:P * c + P], hT[:, 16 + c, TP:T], ident)
            mm.then_inc(z_t, 1)
            pe.wait_ge(group_free, G_EOUT)
            proj_with_stats(S_EOUT, y, G_EOUT)

            def up(s, xin):
                arrived(s, 32)
                for j in range(2):
                    for v in up_views(s):
                        group(lambda k: v[:, k, P * j:P * j + P], xin, KD)

            pe.wait_ge(x_ready, 4 + KD)
            with pe.Fori(0, 2) as i:
                done.enter(i, 20)
                for s in S_UP:
                    loads[s].enter(i, 32)
                    up(s, x)
                    loads[s].leave(2)
                done.leave(2)
            up(S_UPLAST, x)
            pe.wait_ge(group_free, G_DOWN)
            for i in range(2):
                for pair in range(2):
                    pr = S_DOWN[2 * pair:2 * pair + 2]
                    for s in pr:
                        arrived(s)
                    for j in range(2):
                        c = 4 * i + 2 * pair + j
                        group(lambda k: slab(pr[k // 11], 11, 256)[:, k % 11, P * j:P * j + P],
                              lambda k: hT[:, k, :], KF)
                        if c:
                            stats(c - 1, KD, rT, sqT, (group_free, G_DOWN + c))
            stats(KD - 1, KD, rT, sqT, (group_free, G_DOWN + KD))

            pe.wait_ge(x_ready, 4 + 2 * KD)
            pe.wait_ge(idx_in, 16 * 13)
            pe.wait_ge(var_done, got[0])
            turned = []

            def rotate(n, g):
                q = len(turned)
                pe.wait_ge(group_free, g + 1)
                if q >= 2:
                    pe.wait_ge(roped, q - 1)
                pe.matmul(ps[4 + q % 2][:, 0:T], rot, hT[:, n, :], start=True, stop=True).then_inc(rot_done, 1)
                turned.append(n)

            todo = []
            for s, n0, kind in zip(S_OIN, (QI, KI, KK, QQ, QQ + 4), ("std", "ki", "kv", "q", "q")):
                arrived(s, {"ki": 32, "q": 128}.get(kind, 16))
                if kind == "ki":
                    v = slab(s, KD, 136)
                    todo.append((KI, done.k))
                    group(lambda k: v[:, k, 0:P], x, KD)
                    group(lambda k: v[:, k, P:P + 8], x, KD, m=8)
                    continue
                for j in range(4):
                    now = (n0 + j, done.base + done.k)
                    group(lambda k: slab(s, KD, 512)[:, k, P * j:P * j + P], x, KD)
                    if todo:
                        rotate(*todo.pop(0))
                    if kind != "kv" or j < 2:
                        todo.append(now)
            for now in todo:
                rotate(*now)
            assert turned == ROPED, turned
            pe.wait_ge(roped, len(ROPED))
            for t in range(2):
                for c in range(4):
                    pe.transpose(ps[4 + t][:, P * c:P * c + P], hT[:, KK + c, P * t:P * t + P], ident)
            for c in range(4):
                pe.transpose(ps[6][0:8, P * c:P * c + P], hT[:, KK + c, TP:T], ident)
            for t in range(2):
                pe.transpose(ps[7][:, 64 * t:64 * t + 64], hT[0:64, KI, P * t:P * t + P], square[0:64, 0, 0:64])
                pe.transpose(ps[7][:, 192 + 8 * t:200 + 8 * t], wiT[:, P * t:P * t + P], square[0:8, 0, 0:8])
            pe.transpose(ps[7][0:8, 128:192], hT[0:64, KI, TP:T], square[0:64, 0, 0:64]).then_inc(tok_t, 1)

            for u in range(4):
                t, c0 = u // 2, 2 * (u % 2)
                L = P * (t + 1)
                for half in range(2):
                    if u >= 2:
                        pe.wait_ge(rel_done, 2 * (u - 2) + half + 1)
                    for c in range(2):
                        mm = pe.matmul(ps[2 * (u % 2) + half][:, 256 * c:256 * c + L],
                                       hT[64 * half:64 * half + 64, QI + c0 + c, P * t:P * t + P],
                                       hT[64 * half:64 * half + 64, KI, 0:L], start=True, stop=True)
                    mm.then_inc(dots_done, 1)

            def logits(u):
                t, c0 = u // 4, 2 * (u % 4)
                L = P * (t + 1)
                for half in range(2):
                    if u >= 2:
                        pe.wait_ge(lg_read, 2 * (u - 2) + half + 1)
                    else:
                        pe.wait_ge(rel_done, 8)
                    for c in range(2):
                        mm = pe.matmul(ps[2 * (u % 2) + half][:, 256 * c:256 * c + L],
                                       hT[64 * half:64 * half + 64, QQ + c0 + c, P * t:P * t + P],
                                       hT[64 * half:64 * half + 64, KK + c0 // 4, 0:L], start=True, stop=True)
                    mm.then_inc(lg_done, 1)

            def values(u):
                t, c0 = u // 4, 2 * (u % 4)
                nb = t + 1
                for half in range(2):
                    v = 2 * u + half
                    pe.wait_ge(prob_done, v + 1)
                    if v >= 2:
                        pe.wait_ge(pt_copied, v - 1)
                    for c in range(2):
                        for k in range(nb):
                            mm = pe.transpose(ps[4 + v % 2][:, P * (c * nb + k):P * (c * nb + k) + P],
                                              S[u % 2][:, half, c, P * k:P * k + P], ident)
                    mm.then_inc(pt_done, 1)
                for half in range(2):
                    v = 2 * u + half
                    pe.wait_ge(pt_copied, v + 1)
                    if u >= 2 and half == 0:
                        pe.wait_ge(o_copied, u - 1)
                    head = 2 * (c0 // 4) + half
                    for c in range(2):
                        for k in range(nb):
                            mm = pe.matmul(ps[6 + u % 2][64 * half:64 * half + 64, P * c:P * c + P],
                                           ktv[:, k, 256 + 64 * head:320 + 64 * head],
                                           PT[v % 2][:, P * (c * nb + k):P * (c * nb + k) + P],
                                           start=(k == 0), stop=(k == nb - 1))
                    mm.then_inc(o_done, 1)

            pe.wait_ge(tok_copied, 5)
            logits(0)
            for u in range(8):
                if u < 7:
                    logits(u + 1)
                values(u)

            pe.wait_ge(o_copied, 8)
            pe.matmul(ps[6][:, 0:32].rearrange("p (c b) -> p c b", c=4), swap, hT[:, QI:QI + 4, TP:T],
                      start=True, stop=True).then_inc(swapped, 1)
            pe.wait_ge(wib_in, 1)
            pe.matmul(ps[6][:, 64:128], one8[:], dwi, start=True, stop=True).then_inc(swapped, 1)
            pe.wait_ge(qi_ready, 2)
            for b in range(TS):
                pe.wait_ge(ki_in[b % 2], 16 * (b // 2 + 1))
                if b >= 2:
                    pe.wait_ge(ki_copied, b - 1)
                else:
                    pe.wait_ge(lg_read, 16)
                for c in range(4):
                    mm = pe.transpose(ps[b % 2][:, P * c:P * c + P], kibuf[b % 2][:, P * c:P * c + P], ident)
                mm.then_inc(ki_t, 1)
                pe.wait_ge(ki_copied, b + 1)
                for r in range(RUN):
                    h = r % 2
                    mm = pe.matmul(ps[2 + h][:, 32 * b + 8 * (r // 2):32 * b + 8 * (r // 2) + 8],
                                   kiT[b % 2][64 * h:64 * h + 64, P * (r // 2):P * (r // 2) + P],
                                   qiB[64 * h:64 * h + 64, b, :], start=True, stop=True)
                mm.then_inc(ki_mm, 1)
            pe.matmul(ps[2][0:8, 256:320], hT[0:64, KI, TP:T], qiB[0:64, :, :], start=True, stop=True)
            pe.matmul(ps[3][0:8, 256:257], one8[:, 0:8], one8[:, 0:1], start=True, stop=True).then_inc(sdots, 1)
            pe.wait_ge(score_done, 1)
            for a in range(2):
                for r in range(4):
                    pe.transpose(ps[4 + a][0:8, P * r:P * r + P], score[:, a, r, :], ident)
            pe.wait_ge(new_masked, 1)
            pe.transpose(ps[7][0:8, 0:8], sc9, square[0:8, 0, 0:8]).then_inc(row_t, 1)

            pe.wait_ge(qbd_done, 1)
            for u in range(2 * TS):
                b, hf = u // 2, u % 2
                pe.wait_ge(k_in[hf], 16 * (b + 1))
                for j in range(2):
                    if u >= 1:
                        pe.wait_ge(k_copied, 2 * (u - 1) + j + 1)
                    for r in range(4):
                        mm = pe.transpose(ps[j][:, P * r:P * r + P],
                                          kbuf[hf][:, 256 * r + P * j:256 * r + P * j + P], ident)
                    mm.then_inc(k_t, 1)
                if u == 0:
                    pe.wait_ge(srel_done, 3)
                for j in range(2):
                    pe.wait_ge(k_copied, 2 * u + j + 1)
                    for r in range(4):
                        o = P * r + 16 * b + 8 * j
                        mm = pe.matmul(ps[2 + hf][:, o:o + 8], KT[u % 2][:, r, j, :], qbd[:, j, b, :],
                                       start=True, stop=True)
                mm.then_inc(k_mm, 1)
            for j in range(2):
                mm = pe.matmul(ps[6][0:8, 0:P].rearrange("p (b j x) -> p b j x", b=8, j=2)[:, :, j, :],
                               hT[:, KK + j, TP:T], qbd[:, j, :, :], start=True, stop=True)
            mm.then_inc(slg_done, 1)
            pe.wait_ge(row_masked, 1)
            rv = row[:, 0:1024].rearrange("b (s r) -> b r s", r=8)
            for a in range(2):
                pe.matmul(ps[4 + a][:, :], pick[:], rv[:, 4 * a:4 * a + 4, :], start=True, stop=True)
            pe.matmul(ps[7][:, 0:8], pick[:], row[:, 1024:1032], start=True, stop=True).then_inc(mask_wide, 1)
            pe.wait_ge(slg_copied, 3)
            for a in range(2):
                for r in range(4):
                    pe.transpose(ps[2 + a][:, P * r:P * r + P], lgS[:, 512 * a + P * r:512 * a + P * r + P], ident)
            pe.transpose(ps[6][:, 256:264], lgS[0:8, 1024:1152], square[0:8, 0, 0:8]).then_inc(slg_t, 1)
            pe.wait_ge(sprob_done, 1)
            for a in range(2):
                for r in range(4):
                    pe.transpose(ps[a][:, P * r:P * r + P], SS[:, 512 * a + P * r:512 * a + P * r + P], ident)
            pe.transpose(ps[6][0:8, 0:P], SS[:, 1024:1032], ident).then_inc(spt_done, 1)
            pe.wait_ge(spt_copied, 3)
            for b in range(TS):
                pe.wait_ge(v_in[b % 2], 16 * (b // 2 + 1))
                vb = (rT, sqT)[b % 2][:].rearrange("p c t -> p (c t)")
                for j in range(2):
                    out = ps[4][:, 64 * j + 8 * b:64 * j + 8 * b + 8]
                    for r in range(RUN):
                        pe.matmul(out, vb[:, 256 * r + P * j:256 * r + P * j + P],
                                  PTs[:, r, 16 * b + 8 * j:16 * b + 8 * j + 8], start=(r == 0), stop=False)
                    mm = pe.matmul(out, kvs[0:8, 256 + P * j:256 + P * j + P],
                                   PTs[0:8, 8, 16 * b + 8 * j:16 * b + 8 * j + 8], start=False, stop=True)
                mm.then_inc(v_used, 1)

            pe.wait_ge(so_done, 1)
            proj_with_stats(S_OOUT, y, G_OOUT, by=64)
            pe.wait_ge(x_ready, 4 + 3 * KD)
            for t in range(3):
                m = P if t < 2 else 8
                out = ps[6][0:m, 8 * t:8 * t + 8]
                for k in range(KD):
                    pe.matmul(out, xT[:, k, P * t:P * t + m], wrt[:, k, :], start=(k == 0), stop=False)
                mm = pe.matmul(out, one8[0:1, 0:m], wrb[:], start=False, stop=True)
                mm.then_inc(route_done, 1)
            pe.wait_ge(comb_done, 3)
            for t in range(3):
                m = P if t < 2 else 8
                mm = pe.transpose(ps[7][0:8, P * t:P * t + m], rt[0:m, t, 40:48], square[0:m, 0, 0:m])
            mm.then_inc(comb_t, 1)
            pe.wait_ge(combT_done, 1)
            for e in range(NE):
                b = bank()
                done.inc(pe.matmul(b[:, 0:T], square[0:8, 0, e:e + 1].to_broadcast([8, P]), combT[:],
                                   start=True, stop=True))
            with pe.Fori(0, NE) as e:
                done.enter(e, G_EXP)
                for s in range(NSLOT):
                    loads[s].enter(e, 32 if s < 4 else 16)
                    if s < 4:
                        up(s, x)
                    else:
                        if s == 4:
                            pe.wait_ge(group_free, G_MOE + e * G_EXP + 2 * KD)
                        arrived(s)
                        for j in range(4):
                            group(lambda k: slab(s, KD, 512)[:, k, P * j:P * j + P], lambda k: hT[:, k, :], KD)
                    loads[s].leave(NE)
                done.leave(NE)
            for c in range(KD):
                stats(c, KD, rT, sqT, (resid_done, c + 1))
            pe.wait_ge(x_ready, 4 + 4 * KD)
            for t in range(3):
                m = P if t < 2 else 8
                for a in range(2):
                    n = 2 * t + a
                    if n >= 2:
                        pe.wait_ge(yt_copied, n - 1)
                    for c in range(4):
                        mm = pe.transpose(ps[6 + n % 2][0:m, P * c:P * c + P], xT[:, 4 * a + c, P * t:P * t + m], ident)
                    mm.then_inc(yt_done, 1)

        @block.scalar
        def _(act):
            norms, cen = [0], [0]

            def squares(n, src, ready):
                for c in range(n):
                    act.wait_ge(ready[0], ready[1] + c + 1)
                    act.activation(sqT[:, c, :], src[:, c, :], ACT.Square).then_inc(sq_done, 1)

            def norm(n, dst, src, g, b):
                norms[0] += 1
                act.wait_ge(var_done, norms[0])
                act.activation(rstd[:], var[:], ACT.Sqrt, bias=eps[:, 0:1]).then_inc(std_done, 1)
                for c in range(n):
                    cen[0] += 1
                    act.wait_ge(centred, cen[0])
                    act.activation(dst[:, c, :], src[:, c, :], ACT.Identity, scale=vec[:, g + c:g + c + 1],
                                   bias=vec[:, b + c:b + c + 1]).then_inc(x_ready, 1)

            def silus(n, g0, first):
                for m in range(n):
                    act.wait_ge(group_done, g0 + 2 * m + 1)
                    act.wait_ge(group_free, g0 + 2 * m - 2)
                    act.activation(silu[:, m % 2, :], ps[(first + 2 * m) % NB][:, 0:T], ACT.Silu).then_inc(silu_done, 1)

            vT = hT[:, 16:20, :]
            squares(4, vT, (group_free, G_EIN))
            act.wait_ge(even_tc, 2)
            act.wait_ge(pool_consts, 5)
            norm(4, vT, vT, V_SG, V_SB)
            squares(KD, rT, (group_free, G_EOUT))
            norm(KD, xT, rT, V_LN1G, V_LN1B)
            with act.Fori(0, 2) as i:
                silus(10, G_UP + 20 * i, G_UP % NB)
            silus(2, G_UP + 40, G_UP % NB)
            squares(KD, rT, (group_free, G_DOWN))
            norm(KD, xT, rT, V_LN2G, V_LN2B)

            act.wait_ge(tok_t, 1)
            act.copy(ktv[:, 0, :], ps[4][:, :]).then_inc(tok_copied, 1)
            act.copy(kvs[:], ps[6][0:8, :]).then_inc(tok_copied, 1)
            for u in range(4):
                L = P * (u // 2 + 1)
                for half in range(2):
                    v = 2 * u + half
                    act.wait_ge(dots_done, v + 1)
                    if v >= 2:
                        act.wait_ge(rel_used, v - 1)
                    src = ps[2 * (u % 2) + half][:, :].rearrange("p (c s) -> p c s", c=2)[:, :, 0:L]
                    act.activation(rel[half][:, :, 0:L], src, ACT.Relu, scale=0.125).then_inc(rel_done, 1)

            def exps(u):
                L = P * (u // 4 + 1)
                for half in range(2):
                    act.wait_ge(lg_read, 2 * u + half + 1)
                    for c in range(2):
                        col = 4 * (u % 2) + 2 * half + c
                        row_ = S[u % 2][:, half, c, 0:L]
                        ins = act.activation(row_, row_, ACT.Exp, bias=stat[:, col:col + 1],
                                             accum_out=stat[:, 8 + col:9 + col])
                    ins.then_inc(exp_done, 1)

            def probs_by_key(u):
                n = 256 * (u // 4 + 1)
                for half in range(2):
                    v = 2 * u + half
                    act.wait_ge(pt_done, v + 1)
                    if v >= 2:
                        act.wait_ge(o_done, v - 1)
                    act.copy(PT[v % 2][:, 0:n], ps[4 + v % 2][:, 0:n]).then_inc(pt_copied, 1)

            act.wait_ge(even_stored, 16 * 3)
            act.wait_ge(state_stored, 16)
            exps(0)
            for u in range(8):
                if u < 7:
                    exps(u + 1)
                probs_by_key(u)

            for b in range(TS):
                act.wait_ge(ki_t, b + 1)
                if b >= 2:
                    act.wait_ge(ki_mm, b - 1)
                act.copy(kiT[b % 2], ps[b % 2][:, :]).then_inc(ki_copied, 1)
            act.wait_ge(sdots, 1)
            for a in range(2):
                act.activation(srel[:, 256 * a:256 * a + 256], ps[2 + a][:, 0:256], ACT.Relu,
                               scale=0.125).then_inc(srel_done, 1)
            act.activation(srel[0:8, 512:576], ps[2][0:8, 256:320], ACT.Relu, scale=0.125).then_inc(srel_done, 1)
            for u in range(2 * TS):
                for j in range(2):
                    act.wait_ge(k_t, 2 * u + j + 1)
                    if u >= 2:
                        act.wait_ge(k_mm, u - 1)
                    act.copy(KT[u % 2][:, :, j, :],
                             ps[j][:, :].rearrange("p (r s) -> p r s", r=4)).then_inc(k_copied, 1)
            act.wait_ge(slg_done, 1)
            for a in range(2):
                act.copy(lgS[:, 512 * a:512 * a + 512], ps[2 + a][:, :]).then_inc(slg_copied, 1)
            act.copy(lgS[0:8, 1024:1152], ps[6][0:8, 0:P]).then_inc(slg_copied, 1)
            act.wait_ge(mask_wide, 1)
            for a in range(2):
                act.mul(bSS[:, 512 * a:512 * a + 512], ps[4 + a][:, :], NEG).then_inc(mask_copied, 1)
            act.mul(bSS[:, 1024:1032], ps[7][:, 0:8], NEG).then_inc(mask_copied, 1)
            act.wait_ge(smax_done, 1)
            act.activation(SS, SS, ACT.Exp, bias=st8[:, 0:1], accum_out=st8[:, 1:2]).then_inc(sexp_done, 1)
            act.wait_ge(spt_done, 1)
            for a in range(2):
                act.copy(PTs[:, 4 * a:4 * a + 4, :].rearrange("p r q -> p (r q)"), ps[a][:, :]).then_inc(spt_copied, 1)
            act.copy(PTs[0:8, 8, :], ps[6][0:8, 0:P]).then_inc(spt_copied, 1)
            squares(KD, rT, (group_free, G_OOUT))
            norm(KD, xT, rT, V_LN1G + 8, V_LN1B + 8)
            for t in range(3):
                m = P if t < 2 else 8
                act.wait_ge(route_in, t + 1)
                act.activation(rt[0:m, t, 25:26], rt[0:m, t, 24:25], ACT.Exp).then_inc(gate_e, 1)
            with act.Fori(0, NE) as e:
                silus(KD, G_MOE + e * G_EXP, G_MOE % NB)
            squares(KD, rT, (resid_done, 0))
            norm(KD, xT, rT, V_LN2G + 8, V_LN2B + 8)

        @block.vector
        def _(dve):
            V = nc.vector
            chain = Count(dchain)
            free = Count(group_free)
            norms = [0]

            def mark(ins):
                return chain.inc(ins)

            def link(ins):
                dve.wait_ge(dchain, chain.inc(ins))

            def filled(ahead=0):
                dve.wait_ge(group_done, free.base + free.k + 1 + ahead)
                return ps[(free.phase + free.k + ahead) % NB]

            def residual(n):
                for c in range(n):
                    free.inc(V.scalar_tensor_tensor(out=rT[:, c, :], in0=xT[:, c, :], scalar=ALPHA,
                                                    in1=filled()[:, 0:T], op0=ALU.mult, op1=ALU.add))

            def norm(n, src):
                norms[0] += 1
                scale = float(KD // n)
                dve.wait_ge(stats_done, norms[0])
                link(V.tensor_scalar(mean[:], ps[4][:, 0:T], scale, None, ALU.mult))
                link(V.tensor_tensor(var[:], mean[:], mean[:], ALU.mult))
                V.scalar_tensor_tensor(out=var[:], in0=ps[5][:, 0:T], scalar=scale, in1=var[:],
                                       op0=ALU.mult, op1=ALU.subtract).then_inc(var_done, 1)
                dve.wait_ge(std_done, norms[0])
                link(V.reciprocal(rstd[:], rstd[:]))
                at = [mark(V.tensor_tensor(src[:, 0, :], src[:, 0, :], mean[:], ALU.subtract))]
                for c in range(n):
                    if c + 1 < n:
                        at.append(mark(V.tensor_tensor(src[:, c + 1, :], src[:, c + 1, :], mean[:], ALU.subtract)))
                    dve.wait_ge(dchain, at[c])
                    V.tensor_tensor(src[:, c, :], src[:, c, :], rstd[:], ALU.mult).then_inc(centred, 1)

            for c in range(KD):
                free.inc(V.tensor_copy(xT[:, c, :], filled()[:, 0:T]))
            dve.wait_ge(even_t, 1)
            V.tensor_copy(vec[:], ps[6][:, 0:NVEC])
            V.tensor_copy(stT, ps[6][:, 128:192].rearrange("p (c n) -> p c n", c=4)).then_inc(even_tc, 1)
            dve.wait_ge(even_t, 2)
            V.tensor_copy(wsT, ps[7][:, :].rearrange("p (g i) -> p g i", g=4)).then_inc(even_tc, 1)
            dve.wait_ge(idx_in, 16 * 13)
            link(V.tensor_copy(idxf[:], idx[:, 0, :]))
            link(V.tensor_scalar(idxf[:], idxf[:], float(PAGE // RUN), sg[:, 0:1], ALU.mult, ALU.add))
            V.tensor_copy(idx[:, 0, :], idxf[:])
            V.tensor_scalar(idx[:, 1, :], idxf[:], 2.0, None, ALU.mult)
            V.tensor_scalar(idx[:, 2, :], idxf[:], 2.0, 1.0, ALU.mult, ALU.add).then_inc(idx_done, 1)

            dve.wait_ge(even_tc, 2)
            V.memset(zext[:, :, 0:2], 0.0)
            for c in range(4):
                free.inc(V.tensor_copy(hT[:, 16 + c, :], filled()[:, 0:T]))
            for c in range(4):
                free.inc(V.tensor_copy(hT[:, 4 + c, :], filled()[:, 0:T]))
            norm(4, hT[:, 16:20, :])
            dve.wait_ge(group_free, free.k)
            w_ = lambda j, c: vec[:, V_CW + 4 * j + c:V_CW + 4 * j + c + 1]
            for c in range(4):
                b = filled()
                mark(V.tensor_tensor(zext[:, c, 2:258], b[:, 0:TP], hT[:, 4 + c, 0:TP], ALU.mult))
                free.inc(V.tensor_tensor(zlast[:, c, 2:10], b[:, TP:T], hT[:, 4 + c, TP:T], ALU.mult))
                dve.wait_ge(group_free, free.k)
                mark(V.tensor_scalar(cst, zext[:, c, 2:258], w_(2, c), None, ALU.mult))
                link(V.tensor_scalar(css, zlast[:, c, 2:10], w_(2, c), None, ALU.mult))
                mark(V.scalar_tensor_tensor(out=cst, in0=zext[:, c, 1:257], scalar=w_(1, c), in1=cst,
                                            op0=ALU.mult, op1=ALU.add))
                link(V.scalar_tensor_tensor(out=css, in0=stT[:, c, 1:16:2], scalar=w_(1, c), in1=css,
                                            op0=ALU.mult, op1=ALU.add))
                mark(V.scalar_tensor_tensor(out=hT[:, 8 + c, 0:TP], in0=zext[:, c, 0:256], scalar=w_(0, c), in1=cst,
                                            op0=ALU.mult, op1=ALU.add))
                link(V.scalar_tensor_tensor(out=hT[:, 8 + c, TP:T], in0=stT[:, c, 0:16:2], scalar=w_(0, c), in1=css,
                                            op0=ALU.mult, op1=ALU.add))
            V.tensor_copy(zlast[:, :, 0:2], zext[:, :, 256:258]).then_inc(z_done, 1)
            for c in range(4):
                free.inc(V.tensor_copy(hT[:, 12 + c, :], filled()[:, 0:T]))
            dve.wait_ge(vt_done, 1)
            for t in range(2):
                ins = V.tensor_copy(vtok[:, t, :], ps[6 + t][:, :])
            ins.then_inc(vt_copied, 1)
            for c in range(4):
                free.inc(V.tensor_tensor(yT[:, c, :], filled()[:, 0:T], hT[:, 8 + c, :], ALU.mult))
            dve.wait_ge(x_ready, 4)
            for g in range(4):
                b = filled()
                V.tensor_tensor(yT[:, 4 + g, 0:TP], b[:, 0:TP], hT[:, 12 + g, 0:TP], ALU.mult)
                link(V.tensor_scalar(css, hT[:, 16 + g, TP:T], w00[:, 0, g:g + 1], w00[:, 1, g:g + 1],
                                     ALU.mult, ALU.add))
                free.inc(V.tensor_tensor(yT[:, 4 + g, TP:T], css, hT[:, 12 + g, TP:T], ALU.mult))
                dve.wait_ge(group_free, free.k)
            dve.wait_ge(z_t, 1)
            V.tensor_copy(zrow, ps[6][0:10, :]).then_inc(z_copied, 1)
            dve.wait_ge(z_t, 2)
            V.tensor_copy(vrow, ps[7][0:8, :]).then_inc(z_copied, 1)
            residual(KD)
            norm(KD, rT)

            def hidden(m, dst):
                filled(1)
                b = ps[(free.phase + free.k + 1) % NB]
                free.inc(V.tensor_tensor(dst, silu[:, m % 2, :], b[:, 0:T], ALU.mult), 2)

            silus = Count(silu_done)
            with dve.Fori(0, 2) as i:
                free.enter(i, 20)
                silus.enter(i, 10)
                for m in range(10):
                    silus.k += 1
                    dve.wait_ge(silu_done, silus.base + silus.k)
                    hidden(m, hT[:, bass.ds(i * 10 + m, 1), :].rearrange("p a t -> p (a t)"))
                silus.leave(2)
                free.leave(2)
            for m in range(2):
                silus.k += 1
                dve.wait_ge(silu_done, silus.base + silus.k)
                hidden(m, hT[:, 20 + m, :])
            residual(KD)
            norm(KD, rT)

            ropes = [0]

            def turn():
                q = ropes[0]
                n = ROPED[q]
                dve.wait_ge(rot_done, q + 1)
                mark(V.tensor_tensor(mean[:], hT[:, n, :], rope[:, 0, :], ALU.mult))
                link(V.tensor_tensor(var[:], ps[4 + q % 2][:, 0:T], rope[:, 1, :], ALU.mult))
                V.tensor_tensor(hT[:, n, :], mean[:], var[:], ALU.add).then_inc(roped, 1)
                dve.wait_ge(roped, q + 1)
                ropes[0] += 1

            waiting = 0
            for n0, kind in ((QI, "std"), (KI, "ki"), (KK, "kv"), (QQ, "q"), (QQ + 4, "q")):
                if kind == "ki":
                    free.inc(V.tensor_copy(hT[:, KI, :], filled()[:, 0:T]))
                    free.inc(V.tensor_scalar(wiT[:], filled()[0:8, 0:T], 8.0 ** -0.5, None, ALU.mult))
                    waiting += 1
                    continue
                for j in range(4):
                    free.inc(V.tensor_copy(hT[:, n0 + j, :], filled()[:, 0:T]))
                    if waiting:
                        turn()
                        waiting -= 1
                    if kind != "kv" or j < 2:
                        waiting += 1
            while waiting:
                turn()
                waiting -= 1
            dve.wait_ge(tok_t, 1)
            V.tensor_copy(ktv[:, 1, :], ps[5][:, :]).then_inc(tok_copied, 1)
            V.tensor_copy(kit[0:8, 2, :], ps[7][0:8, 128:192])
            V.tensor_copy(kit[:, 0:2, :], ps[7][:, 0:128].rearrange("p (t d) -> p t d", t=2)).then_inc(tok_copied, 1)
            V.tensor_copy(wit[:], ps[7][:, 192:208].rearrange("p (t h) -> p t h", t=2)).then_inc(tok_copied, 1)
            dve.wait_ge(tok_copied, 5)
            for u in range(4):
                t, c0 = u // 2, 2 * (u % 2)
                L = P * (t + 1)
                for half in range(2):
                    v = 2 * u + half
                    dve.wait_ge(rel_done, v + 1)
                    for c in range(2):
                        wgt = wit[:, t, 2 * (c0 + c) + half:2 * (c0 + c) + half + 1]
                        src = rel[half][:, c, 0:L]
                        if u % 2 == 0 and half == 0 and c == 0:
                            ins = V.tensor_scalar(sc[:, t, 0:L], src, wgt, None, ALU.mult)
                        else:
                            ins = V.scalar_tensor_tensor(out=sc[:, t, 0:L], in0=src, scalar=wgt, in1=sc[:, t, 0:L],
                                                         op0=ALU.mult, op1=ALU.add)
                        if c == 0:
                            link(ins)
                    ins.then_inc(rel_used, 1)
                    dve.wait_ge(rel_used, v + 1)

            def select(src, dst, mx, k):
                for _ in range(k // 8):
                    link(V.max(out=mx, in_=src))
                    link(V.match_replace(out=dst, in_to_replace=mx, in_values=src, imm_value=TAKEN))
                    src = dst

            for t in range(2):
                L = P * (t + 1)
                dve.wait_ge(sc_causal, t + 1)
                select(sc[:, t, 0:L], work[:, t, 0:L], mx8p[:], TOPK_P)
                V.tensor_scalar(work[:, t, 0:L], work[:, t, 0:L], TAKEN / 2, NEG, ALU.is_gt,
                                ALU.mult).then_inc(bias_done, 1)

            def masked_logits(u):
                t = u // 4
                L = P * (t + 1)
                dve.wait_ge(bias_causal, t + 1)
                if u >= 2:
                    dve.wait_ge(pt_done, 2 * (u - 1))
                for half in range(2):
                    dve.wait_ge(lg_done, 2 * u + half + 1)
                    dst = S[u % 2][:, half, :, 0:L]
                    col = 4 * (u % 2) + 2 * half
                    link(V.scalar_tensor_tensor(
                        out=dst, in0=ps[2 * (u % 2) + half][:, :].rearrange("p (c s) -> p c s", c=2)[:, :, 0:L],
                        scalar=0.125, in1=work[:, t:t + 1, 0:L].to_broadcast([P, 2, L]), op0=ALU.mult, op1=ALU.add))
                    link(V.tensor_reduce(out=stat[:, col:col + 2], in_=dst, axis=AX, op=ALU.max))
                    V.tensor_scalar(stat[:, col:col + 2], stat[:, col:col + 2], -1.0, None,
                                    ALU.mult).then_inc(lg_read, 1)

            def probs(u):
                L = P * (u // 4 + 1)
                for half in range(2):
                    dve.wait_ge(exp_done, 2 * u + half + 1)
                    col = 4 * (u % 2) + 2 * half
                    link(V.reciprocal(stat[:, 16 + col:18 + col], stat[:, 8 + col:10 + col]))
                    for c in range(2):
                        row_ = S[u % 2][:, half, c, 0:L]
                        ins = V.tensor_scalar(row_, row_, stat[:, 16 + col + c:17 + col + c], None, ALU.mult)
                    ins.then_inc(prob_done, 1)

            def heads_out(u):
                t, c0 = u // 4, 2 * (u % 4)
                dve.wait_ge(o_done, 2 * (u + 1))
                V.tensor_copy(yT[:, c0:c0 + 2, P * t:P * t + P],
                              ps[6 + u % 2][:, 0:256].rearrange("p (c q) -> p c q", c=2)).then_inc(o_copied, 1)

            masked_logits(0)
            for u in range(8):
                if u < 7:
                    masked_logits(u + 1)
                probs(u)
                if u:
                    heads_out(u - 1)
            heads_out(7)

            link(V.memset(qbd, 0.0))
            lo, hi = slice(0, 64), slice(64, P)
            for j in range(2):
                q = hT[:, QQ + 4 * j:QQ + 4 * j + 4, TP:T].rearrange("p x b -> p b x")
                V.tensor_copy(qbd[lo, j, :, 0:4], q[lo])
                ins = V.tensor_copy(qbd[hi, j, :, 4:8], q[hi])
            ins.then_inc(qbd_done, 1)
            V.tensor_tensor(dwi.rearrange("h (b g) -> h b g", b=8),
                            wiT[:, TP:T].unsqueeze(2).to_broadcast([8, 8, 8]),
                            square[0:8, 0:1, 0:8].to_broadcast([8, 8, 8]), ALU.mult).then_inc(wib_in, 1)
            dve.wait_ge(swapped, 2)
            qv = qiB[:].rearrange("p b (c a) -> p a c b", a=2)
            raw = hT[:, QI:QI + 4, TP:T]
            swp = ps[6][:, 0:32].rearrange("p (c b) -> p c b", c=4)
            V.tensor_copy(qv[lo, 0], raw[lo])
            V.tensor_copy(qv[hi, 1], raw[hi])
            V.tensor_copy(qv[lo, 1], swp[lo])
            V.tensor_copy(qv[hi, 0], swp[hi]).then_inc(qi_ready, 1)
            V.tensor_copy(wib, ps[6][:, 64:128]).then_inc(qi_ready, 1)
            dve.wait_ge(qi_ready, 2)
            dve.wait_ge(srel_done, 3)
            for a in range(2):
                v = srel[:, 256 * a:256 * a + 256]
                link(V.tensor_tensor(v.rearrange("p (b r h) -> p b r h", b=8, r=4),
                                     v.rearrange("p (b r h) -> p b r h", b=8, r=4),
                                     wib.rearrange("p (b h) -> p b h", b=8).unsqueeze(2).to_broadcast([P, 8, 4, 8]),
                                     ALU.mult))
                ins = V.tensor_reduce(out=score[:, a].rearrange("p r b -> p b r"),
                                      in_=v.rearrange("p (b r h) -> p b r h", b=8, r=4), axis=AX, op=ALU.add)
            ins.then_inc(score_done, 1)
            v = srel[0:8, 512:576]
            link(V.tensor_tensor(v, v, wib[0:8, :], ALU.mult))
            V.tensor_reduce(out=sc9, in_=v.rearrange("p (b h) -> p b h", b=8), axis=AX,
                            op=ALU.add).then_inc(score_done, 1)
            dve.wait_ge(row_t, 1)
            rv = row[:, 0:1024].rearrange("b (p r a) -> b a r p", r=4, a=2)
            for a in range(2):
                mark(V.tensor_copy(rv[:, a], ps[4 + a][0:8, :].rearrange("b (r p) -> b r p", r=4)))
            link(V.tensor_copy(row[:, 1024:1032], ps[7][0:8, 0:8]))
            select(row, row, mx8, TOPK_S)
            V.tensor_scalar(row, row, TAKEN / 2, None, ALU.is_gt).then_inc(row_masked, 1)
            dve.wait_ge(slg_t, 1)
            dve.wait_ge(mask_copied, 3)
            for a in range(2):
                mark(V.scalar_tensor_tensor(out=SS[:, 512 * a:512 * a + 512], in0=ps[2 + a][:, :], scalar=0.125,
                                            in1=bSS[:, 512 * a:512 * a + 512], op0=ALU.mult, op1=ALU.add))
            link(V.scalar_tensor_tensor(out=SS[:, 1024:1032], in0=ps[6][:, 256:264], scalar=0.125,
                                        in1=bSS[:, 1024:1032], op0=ALU.mult, op1=ALU.add))
            link(V.reduce_max(st8[:, 2:3], SS, AX))
            V.tensor_scalar(st8[:, 0:1], st8[:, 2:3], -1.0, None, ALU.mult).then_inc(smax_done, 1)
            dve.wait_ge(sexp_done, 1)
            link(V.reciprocal(st8[:, 3:4], st8[:, 1:2]))
            V.tensor_scalar(SS, SS, st8[:, 3:4], None, ALU.mult).then_inc(sprob_done, 1)
            dve.wait_ge(v_used, TS)
            for j in range(2):
                o = ps[4][:, 64 * j:64 * j + 64].rearrange("p (b x) -> p x b", b=8)
                V.tensor_copy(yT[lo, 4 * j:4 * j + 4, TP:T], o[lo, 0:4])
                ins = V.tensor_copy(yT[hi, 4 * j:4 * j + 4, TP:T], o[hi, 4:8])
            ins.then_inc(so_done, 1)
            residual(KD)
            norm(KD, rT)

            for t in range(3):
                m = P if t < 2 else 8
                r = rt[0:m, t, :]
                dve.wait_ge(route_done, 3)
                link(V.tensor_copy(r[:, 0:8], ps[6][0:m, 8 * t:8 * t + 8]))
                link(V.max(out=r[:, 8:16], in_=r[:, 0:8]))
                V.tensor_tensor(r[:, 24:25], r[:, 9:10], r[:, 8:9], ALU.subtract).then_inc(route_in, 1)
                link(V.max_index(mxi[0:m, :], r[:, 8:16], r[:, 0:8]))
                link(V.tensor_copy(r[:, 16:24], mxi[0:m, :]))
                dve.wait_ge(gate_e, t + 1)
                link(V.tensor_scalar(r[:, 26:27], r[:, 25:26], 1.0, None, ALU.add))
                link(V.reciprocal(r[:, 27:28], r[:, 26:27]))
                link(V.tensor_tensor(r[:, 28:29], r[:, 27:28], r[:, 25:26], ALU.mult))
                mark(V.tensor_scalar(r[:, 32:40], iota8[0:m, :], r[:, 16:17], r[:, 27:28], ALU.is_equal, ALU.mult))
                link(V.tensor_scalar(r[:, 40:48], iota8[0:m, :], r[:, 17:18], r[:, 28:29], ALU.is_equal, ALU.mult))
                V.tensor_tensor(r[:, 40:48], r[:, 40:48], r[:, 32:40], ALU.add).then_inc(comb_done, 1)
            dve.wait_ge(comb_t, 1)
            V.tensor_copy(combT[:], ps[7][0:8, 0:T]).then_inc(combT_done, 1)
            for e in range(NE):
                free.inc(V.tensor_copy(yT[:, e, :], filled()[:, 0:T]))
            link(V.memset(yacc, 0.0))
            dve.wait_ge(group_free, free.k)

            with dve.Fori(0, NE) as e:
                free.enter(e, G_EXP)
                silus.enter(e, KD)
                chain.enter(e, KD + 1)
                for m in range(KD):
                    silus.k += 1
                    dve.wait_ge(silu_done, silus.base + silus.k)
                    s_ = silu[:, m % 2, :]
                    link(V.tensor_tensor(s_, s_, yT[:, bass.ds(e, 1), :].rearrange("p a t -> p (a t)"), ALU.mult))
                    hidden(m, hT[:, m, :])
                for c in range(KD):
                    free.inc(V.tensor_tensor(yacc[:, c, :], yacc[:, c, :], filled()[:, 0:T], ALU.add))
                dve.wait_ge(group_free, free.base + free.k)
                link(V.memset(one_cell[:], 0.0))
                chain.leave(NE)
                silus.leave(NE)
                free.leave(NE)
            for c in range(KD):
                V.scalar_tensor_tensor(out=rT[:, c, :], in0=xT[:, c, :], scalar=ALPHA, in1=yacc[:, c, :],
                                       op0=ALU.mult, op1=ALU.add).then_inc(resid_done, 1)
            norm(KD, rT)
            for t in range(3):
                m = P if t < 2 else 8
                for a in range(2):
                    n = 2 * t + a
                    dve.wait_ge(yt_done, n + 1)
                    V.tensor_copy(ytile[0:m, 4 * t + 2 * a:4 * t + 2 * a + 2, :],
                                  ps[6 + n % 2][0:m, :].rearrange("p (c q) -> p c q", c=2)).then_inc(yt_copied, 1)


def constants():
    square = np.zeros((3, P, P), np.float32)
    square[0] = np.eye(P)
    for h in (0, 64):
        for i in range(8):
            square[1, h + i + 8, h + i] = -1.0
            square[1, h + i, h + i + 8] = 1.0
    square[2] = np.roll(np.eye(P), 64, axis=0)
    inv = np.float32(500000.0) ** (-np.arange(8, dtype=np.float32) / np.float32(8))
    pos = np.concatenate([np.arange(TP), np.full(TS, PAST)]).astype(np.float32)
    ang = (pos[:, None] * inv[None, :].astype(np.float32)).astype(np.float32)
    rope = np.zeros((2, P, T), np.float32)
    rope[0] = 1.0
    for h in (0, 64):
        for i in range(16):
            rope[0, h + i] = np.cos(ang[:, i % 8].astype(np.float64))
            rope[1, h + i] = np.sin(ang[:, i % 8].astype(np.float64))
    pick = np.zeros((9, P), np.float32)
    pick[np.arange(P) // 16, np.arange(P)] = 1.0
    pick[8] = np.arange(P) % (PAGE // RUN)
    return {"c_square": square, "c_rope": rope, "c_pick": pick}


INPUTS = ["x_prompt", "x_sample", "cache_k", "cache_v", "cache_kidx", "state_conv", "page_table",
          "ln1_g", "ln1_b", "ln2_g", "ln2_b", "w_in_even", "conv_w", "sgu_ln_g", "sgu_ln_b", "sgu_w", "sgu_b",
          "w_out_even", "ffn_w1", "ffn_w3", "ffn_w2", "w_in_odd", "w_out_odd", "router_w", "router_b",
          "moe_w1", "moe_w3", "moe_w2"]
OUTPUTS = [(1, TP, D), (TS, 1, D), (1, 1, TP, 4, 64), (1, 1, TP, 4, 64), (1, 1, TP, 64), (1, 1, 2, CH),
           (1, TS, 1, 4, 64), (1, TS, 1, 4, 64), (1, TS, 1, 64), (1, TS, 2, CH), (1, TS, 1, CH)]


def kernel(**inputs):
    import concourse.bacc as bacc
    from concourse.bass_utils import run_bass_kernel_spmd

    nc = bacc.Bacc("TRN2", target_bir_lowering=False, num_devices=1)
    arrays = {name: np.ascontiguousarray(inputs[name]) for name in INPUTS}
    arrays.update(constants())
    args = [nc.dram_tensor(name, a.shape, mybir.dt.from_np(a.dtype), kind="ExternalInput").ap()
            for name, a in arrays.items()]
    args += [nc.dram_tensor(f"out_{i}", shape, F32, kind="ExternalOutput").ap() for i, shape in enumerate(OUTPUTS)]
    build(nc, *args)
    got = run_bass_kernel_spmd(nc, [arrays], core_ids=[0])
    return tuple(got.results[0][f"out_{i}"] for i in range(len(OUTPUTS)))
```

```python
from contextlib import ExitStack

import numpy as np

import concourse.bass as bass
from concourse import mybir

F32 = mybir.dt.float32
I32 = mybir.dt.int32
U32 = mybir.dt.uint32
ALU = mybir.AluOpType
ACT = mybir.ActivationFunctionType
AX = mybir.AxisListType.X

P = 128
D = 1024
KD = D // P
TP, TS = 256, 8
T = TP + TS
CH = 512
FF = 2816
KF = FF // P
NE = 8
CAP = 112
ROUNDS = -(-(TP + TS) // CAP)
PAST, PAGE = 1024, 128
NPOOL = 80
NPG = PAST // PAGE
RUN = 8
TOPK_P, TOPK_S = 64, 256
ALPHA = 4.0 ** 0.25
EPS = 1e-5
NEG = -1e30
TAKEN = -3e38
NSLOT = 6
NB = 4

V_LN1G, V_LN1B, V_LN2G, V_LN2B, V_SG, V_SB, V_CW, NVEC = 0, 16, 32, 48, 64, 68, 72, 84
QI, KI, KK, VV, QQ = 0, 4, 5, 7, 9
ROPED = [QI, QI + 1, QI + 2, QI + 3, KI, KK, KK + 1] + [QQ + c for c in range(KD)]


class Count:

    def __init__(self, sem):
        self.sem, self.base, self.k, self.phase = sem, 0, 0, 0

    def inc(self, ins, by=1):
        ins.then_inc(self.sem, by)
        self.k += by
        return self.base + self.k

    def enter(self, i, per):
        self.start, self.per = self.base + self.k, per
        self.base, self.k, self.phase = self.start + i * per, 0, self.start

    def leave(self, n):
        assert self.k == self.per, (self.k, self.per)
        self.base, self.k = 0, self.start + n * self.per
        self.phase = 0


def build(nc, x_prompt, x_sample, cache_k, cache_v, cache_kidx, state_conv, page_table,
          ln1_g, ln1_b, ln2_g, ln2_b, w_in_even, conv_w, sgu_ln_g, sgu_ln_b, sgu_w, sgu_b,
          w_out_even, ffn_w1, ffn_w3, ffn_w2, w_in_odd, w_out_odd, router_w, router_b,
          moe_w1, moe_w3, moe_w2, c_square, c_rope, c_pick, x_rows, r_rows,
          y_p, y_s, k_p, v_p, ki_p, conv_p, k_s, v_s, ki_s, conv_s, chunk_s):
    ctx = ExitStack()
    with ctx:
        ctx.enter_context(nc.allow_non_contiguous_dma(reason="small tables and packed vectors"))

        def sb(name, shape, dt=F32):
            return ctx.enter_context(nc.sbuf_tensor(name, shape, dt))

        def sem(name):
            return ctx.enter_context(nc.semaphore(name))

        slot = [sb(f"slot{i}", [P, 4096]) for i in range(NSLOT)]
        xT = sb("xT", [P, KD, T])
        rT = sb("rT", [P, KD, T])
        sqT = sb("sqT", [P, KD, T])
        hT = sb("hT", [P, KF, T])
        yT = sb("yT", [P, KD, T])
        scr = sb("scr", [P, 6144])
        cache = sb("cache", [P, 2048])
        kbuf = [cache[:, 0:1024], hT[:, 17:21, :].rearrange("p c t -> p (c t)")[:, 0:1024]]
        kibuf = [cache[:, 1024 + 512 * i:1536 + 512 * i] for i in range(2)]
        square = sb("square", [P, 5, P])
        rope = sb("rope", [P, 2, T])
        pick = sb("pick", [8, P])
        ones = sb("ones", [P, P])
        one8 = sb("one8", [8, P])
        vecraw = sb("vecraw", [NVEC, P])
        vec = sb("vec", [P, NVEC])
        mean = sb("mean", [P, T])
        var = sb("var", [P, T])
        rstd = sb("rstd", [P, T])
        silu = sb("silu", [P, 2, T])
        eps = sb("eps", [P, 1])
        w00 = sb("w00", [P, 2, 4])
        idx = sb("idx", [P, 3, NPG], I32)
        idxf = sb("idxf", [P, NPG])
        sg = sb("sg", [P, 1])
        wrt = sb("wrt", [P, KD, NE])
        wrb = sb("wrb", [1, NE])
        ktv = sb("ktv", [P, 2, 512])
        kvs = sb("kvs", [8, 512])
        kit = sb("kit", [P, 3, 64])
        wit = sb("wit", [P, 2, 8])
        wiT = sb("wiT", [8, T])
        stat = sb("stat", [P, 24])
        qiB = sb("qiB", [P, 8, 8])
        lgr = sb("lgr", [P, 3, 8])
        top = sb("top", [P, 3, 8])
        mxi = sb("mxi", [P, 3, 8], U32)
        topi = sb("topi", [P, 3, 8])
        gate = sb("gate", [P, 4, 3])
        choice = sb("choice", [P, 3, 3, 8])
        place = sb("place", [P, 3, 8])
        tg = sb("tg", [P, 3, 8, 2])
        rowk = sb("rowk", [P, 3, 2], I32)
        tmp8 = sb("tmp8", [P, 3, 8])
        tmp8b = sb("tmp8b", [P, 3, 8])
        rowf = sb("rowf", [P, 2, 3])
        cnt = sb("cnt", [P, 4])
        npass = sb("npass", [1, 1], I32)
        iota8 = sb("iota8", [P, 8])
        iotac = sb("iotac", [P, ROUNDS * CAP])
        tokg = sb("tokg", [P, ROUNDS * NE + 1, 2])
        curi = sb("curi", [P, 1], I32)
        curg = sb("curg", [P, 2])
        fin = sb("fin", [P, 3, 16])
        mx8p = sb("mx8p", [P, 8])

        ident = square[:, 0, :]
        rot = square[:, 1, :]
        swap = square[:, 2, :]
        before = square[:, 3, :]
        all1 = square[:, 4, :]

        ps = [ctx.enter_context(nc.psum_tensor(f"ps{i}", [P, 512], F32)) for i in range(8)]

        xtok = scr[:, 0:2048].rearrange("p (t d) -> p t d", t=2)
        xstok = scr[0:8, 2048:3072]
        zext = scr[:, 0:4 * 258].rearrange("p (c t) -> p c t", c=4)
        vtok = scr[:, 1040:2064].rearrange("p (t c) -> p t c", t=2)
        wsT = scr[:, 3072:3584].rearrange("p (g i) -> p g i", g=4)
        wsr = scr[:, 3584:4096].rearrange("p (g j) -> p g j", g=4)
        stT = scr[:, 4096:4160].rearrange("p (c n) -> p c n", c=4)
        str_ = scr[0:16, 4160:4672]
        zlast = scr[:, 4672:4712].rearrange("p (c n) -> p c n", c=4)
        zrow = scr[0:10, 4736:5248]
        vrow = scr[0:8, 5248:5760]
        sgb = scr[0:1, 5248:5760]
        cst = scr[:, 5760:5760 + 256]
        css = scr[:, 6016:6024]
        rel = [scr[:, 512 * i:512 * i + 512].rearrange("p (h s) -> p h s", h=2) for i in range(2)]
        sc = scr[:, 1024:1536].rearrange("p (t s) -> p t s", t=2)
        work = scr[:, 1536:2048].rearrange("p (t s) -> p t s", t=2)
        S = [scr[:, 2048 + 1024 * i:3072 + 1024 * i].rearrange("p (u h s) -> p u h s", u=2, h=2) for i in range(2)]
        PT = [scr[:, 4096 + 1024 * i:5120 + 1024 * i] for i in range(2)]
        kiT = [scr[:, 512 * i:512 * i + 512] for i in range(2)]
        srel = scr[:, 1024:1600]
        wib = scr[:, 1600:1664]
        dwi = scr[0:8, 1664:1728]
        score = scr[:, 1728:1792].rearrange("p (a r b) -> p a r b", a=2, r=4)
        sc9 = scr[0:8, 1792:1800]
        row = scr[0:8, 1808:2840]
        qbd = scr[:, 2848:2976].rearrange("p (j b x) -> p j b x", j=2, b=8)
        KT = [scr[:, 3072 + 1024 * i:4096 + 1024 * i].rearrange("p (r j s) -> p r j s", r=4, j=2) for i in range(2)]
        lgS = scr[:, 0:1152]
        SS = scr[:, 3072:3072 + 1032]
        bSS = scr[:, 4112:4112 + 1032]
        PTs = scr[:, 0:1152].rearrange("p (r q) -> p r q", r=9)
        st8 = scr[:, 5152:5168]
        mx8 = scr[0:8, 5168:5176]
        flat = lambda a: a[:].rearrange("p c t -> p (c t)")
        xrow = flat(hT)[:, 0:3072].rearrange("p (t d) -> p t d", t=3)
        hg = flat(hT)[:, 3072:3072 + KD * CAP].rearrange("p (c s) -> p c s", c=KD)
        xgT = flat(hT)[:, 4000:4000 + KD * CAP].rearrange("p (c s) -> p c s", c=KD)
        xg = flat(rT)[0:CAP, 0:D]
        orow = flat(yT)[0:CAP, 0:D]
        sel = scr[:, 0:3 * NE * CAP].rearrange("p (t e s) -> p t e s", t=3, e=NE)
        res = scr[:, :].rearrange("p (t k d) -> p t k d", t=3, k=2)
        silug = silu[:].rearrange("p a t -> p (a t)")[:, 0:2 * CAP].rearrange("p (a s) -> p a s", a=2)

        def slab(s, k, n):
            return slot[s][:, 0:k * n].rearrange("p (k n) -> p k n", k=k)

        consts_in, x_in, even_in, idx_in = sem("consts_in"), sem("x_in"), sem("even_in"), sem("idx_in")
        slab_in = [sem(f"slab_in{s}") for s in range(NSLOT)]
        pool_consts, causal_w = sem("pool_consts"), sem("causal_w")
        group_done = sem("group_done")
        group_free = sem("group_free")
        silu_done = sem("silu_done")
        even_t, even_tc = sem("even_t"), sem("even_tc")
        sq_done = sem("sq_done")
        stats_done, var_done, std_done = sem("stats_done"), sem("var_done"), sem("std_done")
        centred, x_ready = sem("centred"), sem("x_ready")
        vt_done, vt_copied = sem("vt_done"), sem("vt_copied")
        z_done, z_t, z_copied = sem("z_done"), sem("z_t"), sem("z_copied")
        rot_done, roped = sem("rot_done"), sem("roped")
        tok_t, tok_copied = sem("tok_t"), sem("tok_copied")
        dots_done, rel_done, rel_used = sem("dots_done"), sem("rel_done"), sem("rel_used")
        sc_causal, bias_done, bias_causal = sem("sc_causal"), sem("bias_done"), sem("bias_causal")
        lg_done, lg_read, exp_done, prob_done = sem("lg_done"), sem("lg_read"), sem("exp_done"), sem("prob_done")
        pt_done, pt_copied, o_done, o_copied = sem("pt_done"), sem("pt_copied"), sem("o_done"), sem("o_copied")
        idx_done = sem("idx_done")
        ki_in = [sem(f"ki_in{i}") for i in range(2)]
        ki_mm, k_mm = sem("ki_mm"), sem("k_mm")
        ki_t, ki_copied, qi_ready, swapped = sem("ki_t"), sem("ki_copied"), sem("qi_ready"), sem("swapped")
        wib_in, wib_done, sdots, srel_done = sem("wib_in"), sem("wib_done"), sem("sdots"), sem("srel_done")
        score_done, new_masked, row_t, row_done = sem("score_done"), sem("new_masked"), sem("row_t"), sem("row_done")
        row_masked, mask_wide, mask_copied = sem("row_masked"), sem("mask_wide"), sem("mask_copied")
        k_in = [sem(f"k_in{i}") for i in range(2)]
        v_in = [sem(f"v_in{i}") for i in range(2)]
        qbd_done, k_t, k_copied = sem("qbd_done"), sem("k_t"), sem("k_copied")
        slg_done, slg_copied, slg_t = sem("slg_done"), sem("slg_copied"), sem("slg_t")
        smax_done, sexp_done, sprob_done = sem("smax_done"), sem("sexp_done"), sem("sprob_done")
        spt_done, spt_copied, v_used, so_done = sem("spt_done"), sem("spt_copied"), sem("v_used"), sem("so_done")
        route_in, route_done, gate_e = sem("route_in"), sem("route_done"), sem("gate_e")
        xt_t, xt_copied, rows_stored = sem("xt_t"), sem("xt_copied"), sem("rows_stored")
        gathers_due = sem("gathers_due")
        chosen, counted, passes_ready = sem("chosen"), sem("counted"), sem("passes_ready")
        sel_ready, sel_done, cur_ready = sem("sel_ready"), sem("sel_done"), sem("cur_ready")
        xg_in, rowk_ready, gb_in = sem("xg_in"), sem("rowk_ready"), sem("gb_in")
        res_in = [sem(f"res_in{t}") for t in range(3)]
        zeros_ready, rows_cleared = sem("zeros_ready"), sem("rows_cleared")
        fvar, fstd, final_ready = sem("fvar"), sem("fstd"), sem("final_ready")
        even_stored, state_stored, kv_stored, y_stored = (
            sem("even_stored"), sem("state_stored"), sem("kv_stored"), sem("y_stored"))
        dchain, tchain = sem("dchain"), sem("tchain")

        block = ctx.enter_context(nc.Block())

        S_EIN, S_EOUT, S_UP, S_UPLAST = (0, 1, 2, 3, 4), (5, 0), (1, 2, 3, 4, 5), 0
        S_DOWN, S_OIN, S_OOUT = (1, 2, 3, 4), (5, 0, 1, 2, 3), (4, 5)
        EIN_ORDER = (4, 1, 2, 3, 0)
        G_EIN = KD
        G_MIX = G_EIN + 20
        G_EOUT = G_MIX + 4
        G_UP = G_EOUT + KD
        G_DOWN = G_UP + 2 * KF
        G_OIN = G_DOWN + KD
        G_OOUT = G_OIN + 18
        G_XG = G_OOUT + KD
        G_MOE = G_XG + 2
        G_EXP = KD + 2 + 2

        kdim = "(k p) n -> p k n"

        def up_views(s):
            v = slot[s][:, :].rearrange("p (w k n) -> p w k n", w=2, k=KD)
            return v[:, 0], v[:, 1]

        @block.sync
        def _(sp):
            last = [None] * NSLOT

            def slot_free(s, value):
                if last[s] is not None:
                    sp.wait_ge(group_done, last[s])
                last[s] = value

            def load(s, dst, src):
                sp.dma_start(dst, src).then_inc(slab_in[s], 16)

            sp.dma_start(xtok, x_prompt[0].rearrange("(t p) d -> p t d", p=P)).then_inc(x_in, 16)
            sp.dma_start(xstok, x_sample[:, 0, :]).then_inc(x_in, 16)
            sp.dma_start(square[:], c_square.rearrange("a p q -> p a q")).then_inc(consts_in, 16)
            w = w_in_even[0].rearrange(kdim, p=P)
            for n, (s, c) in enumerate(zip(S_EIN, EIN_ORDER)):
                slot_free(s, G_EIN + 4 * (n + 1))
                load(s, slab(s, KD, 512), w[:, :, 512 * c:512 * c + 512])
            w = w_out_even[0].rearrange(kdim, p=P)
            for c, s in enumerate(S_EOUT):
                slot_free(s, G_EOUT + 4 * (c + 1))
                load(s, slab(s, KD, 512), w[:, :, 512 * c:512 * c + 512])
            w1, w3 = (w[0].rearrange(kdim, p=P) for w in (ffn_w1, ffn_w3))
            before = [last[s] for s in S_UP]
            with sp.Fori(0, 2) as i:
                for n, s in enumerate(S_UP):
                    sp.wait_ge(group_done, before[n] + i * (G_UP + 4 * (n + 1) - before[n]))
                    a, b = up_views(s)
                    load(s, a, w1[:, :, bass.ds(i * 1280 + n * 256, 256)])
                    load(s, b, w3[:, :, bass.ds(i * 1280 + n * 256, 256)])
            for n, s in enumerate(S_UP):
                last[s] = G_UP + 20 + 4 * (n + 1)
            slot_free(S_UPLAST, G_DOWN)
            a, b = up_views(S_UPLAST)
            load(S_UPLAST, a, w1[:, :, 2560:2816])
            load(S_UPLAST, b, w3[:, :, 2560:2816])
            w2 = ffn_w2[0].rearrange("(u k p) n -> p u k n", p=P, u=2)
            before = [last[s] for s in S_DOWN]
            with sp.Fori(0, 2) as i:
                for n, s in enumerate(S_DOWN):
                    sp.wait_ge(group_done, before[n] + i * (G_DOWN + 2 * (n // 2 + 1) - before[n]))
                    load(s, slab(s, 11, 256), w2[:, n % 2, :, bass.ds(i * 512 + (n // 2) * 256, 256)])
            for n, s in enumerate(S_DOWN):
                last[s] = G_DOWN + 4 + 2 * (n // 2 + 1)
            w = w_in_odd[0].rearrange(kdim, p=P)
            slot_free(S_OIN[0], G_OIN + 4)
            load(S_OIN[0], slab(S_OIN[0], KD, 512), w[:, :, 1536:2048])
            slot_free(S_OIN[1], G_OIN + 6)
            v = slab(S_OIN[1], KD, 136)
            load(S_OIN[1], v[:, :, 0:64], w[:, :, 2048:2112])
            load(S_OIN[1], v[:, :, 64:136], w[:, :, 2048:2120])
            slot_free(S_OIN[2], G_OIN + 10)
            load(S_OIN[2], slab(S_OIN[2], KD, 512), w[:, :, 1024:1536])
            for c in range(2):
                slot_free(S_OIN[3 + c], G_OIN + 14 + 4 * c)
                v = slab(S_OIN[3 + c], KD, 512)
                for i in range(4):
                    for a in range(2):
                        src = 512 * c + 256 * a + 64 * i
                        load(S_OIN[3 + c], v[:, :, P * i + 64 * a:P * i + 64 * a + 64], w[:, :, src:src + 64])
            for c, s in enumerate(S_OOUT):
                slot_free(s, G_OOUT + 4 * (c + 1))
                for half in range(2):
                    v = slab(s, KD, 512)[64 * half:64 * half + 64]
                    for j in range(2):
                        src = w_out_odd[0, 512 * j + 256 * half:512 * j + 256 * half + 256, 512 * c:512 * c + 512]
                        load(s, v[:, 4 * j:4 * j + 4, :], src.rearrange("(i d) n -> d i n", d=64))

            def load_expert(s, e):
                if s < 4:
                    for v, w in zip(up_views(s), (moe_w1[0], moe_w3[0])):
                        src = w[bass.ds(e, 1), :, 256 * s:256 * s + 256]
                        load(s, v, src.rearrange("e (k p) n -> p (e k) n", p=P))
                else:
                    src = moe_w2[0][bass.ds(e, 1), :, 512 * (s - 4):512 * (s - 4) + 512]
                    load(s, slab(s, KD, 512), src.rearrange("e (k p) n -> p (e k) n", p=P))

            sp.wait_ge(z_copied, 2)
            sp.dma_start(conv_p[0, 0], zrow[0:2, :]).then_inc(even_stored, 16)
            sp.dma_start(conv_s[0, :, 1, :], zrow[2:10, :]).then_inc(even_stored, 16)
            sp.dma_start(chunk_s[0, :, 0, :], vrow).then_inc(even_stored, 16)
            for s in range(4):
                slot_free(s, None)
                load_expert(s, 0)
            sp.wait_ge(tok_copied, 5)
            kv = lambda a: a[0, 0].rearrange("(t p) h d -> p t (h d)", p=P)
            sp.dma_start(kv(k_p), ktv[:, :, 0:256]).then_inc(kv_stored, 16)
            sp.dma_start(kv(v_p), ktv[:, :, 256:512]).then_inc(kv_stored, 16)
            sp.dma_start(ki_p[0, 0].rearrange("(t p) d -> p t d", p=P), kit[:, 0:2, :]).then_inc(kv_stored, 16)
            sp.dma_start(k_s[0, :, 0].rearrange("b h d -> b (h d)"), kvs[:, 0:256]).then_inc(kv_stored, 16)
            sp.dma_start(v_s[0, :, 0].rearrange("b h d -> b (h d)"), kvs[:, 256:512]).then_inc(kv_stored, 16)
            sp.dma_start(ki_s[0, :, 0], kit[0:8, 2, :]).then_inc(kv_stored, 16)
            for s in (4, 5):
                slot_free(s, None)
                load_expert(s, 0)
            sp.wait_ge(passes_ready, 1)
            n = sp.value_load(npass[0:1, 0:1], min_val=NE, max_val=ROUNDS * NE)
            with sp.Fori(1, n) as i:
                for s in range(NSLOT):
                    sp.wait_ge(group_done, G_MOE + (i - 1) * G_EXP + (2 * (s + 1) if s < 4 else KD + 2 + s - 3))
                    load_expert(s, i % NE)
            for t in range(3):
                sp.wait_ge(final_ready, t + 1)
                if t < 2:
                    sp.dma_start(y_p[0, P * t:P * t + P, :], res[:, t, 0, :]).then_inc(y_stored, 16)
                else:
                    sp.dma_start(y_s[:, 0, :], res[0:8, t, 0, :]).then_inc(y_stored, 16)
            for stored, n in ((even_stored, 3), (state_stored, 1), (kv_stored, 6), (y_stored, 3)):
                sp.wait_ge(stored, 16 * n)

        @block.gpsimd
        def _(pool):
            pool.memset(ones[:], 1.0 / D).then_inc(pool_consts, 1)
            pool.memset(one8[:], 1.0).then_inc(pool_consts, 1)
            pool.iota(iota8[:], pattern=[[1, 8]], base=0, channel_multiplier=0,
                      allow_small_or_imprecise_dtypes=True).then_inc(pool_consts, 1)
            pool.iota(iotac[:], pattern=[[1, ROUNDS * CAP]], base=1, channel_multiplier=0,
                      allow_small_or_imprecise_dtypes=True).then_inc(pool_consts, 1)
            for t in range(3):
                pool.iota(tg[:, t, :, 0], pattern=[[0, 8]], base=P * t, channel_multiplier=1,
                          allow_small_or_imprecise_dtypes=True).then_inc(pool_consts, 1)
            pool.memset(eps[:], EPS).then_inc(pool_consts, 1)
            n = 0
            for dst, src in ((vecraw[0:16], ln1_g.rearrange("l (c p) -> (l c) p", p=P)),
                             (vecraw[16:32], ln1_b.rearrange("l (c p) -> (l c) p", p=P)),
                             (vecraw[32:48], ln2_g.rearrange("l (c p) -> (l c) p", p=P)),
                             (vecraw[48:64], ln2_b.rearrange("l (c p) -> (l c) p", p=P)),
                             (vecraw[64:68], sgu_ln_g.rearrange("l (c p) -> (l c) p", p=P)),
                             (vecraw[68:72], sgu_ln_b.rearrange("l (c p) -> (l c) p", p=P)),
                             (vecraw[72:84], conv_w[0].rearrange("w (c p) -> (w c) p", p=P)),
                             (wsr, sgu_w[0].rearrange("g i j -> i g j")),
                             (sgb, sgu_b.rearrange("l g i -> l (g i)")),
                             (str_, state_conv[0].rearrange("b w c -> (b w) c")),
                             (w00[:, 0, :], sgu_w[0, :, 0, 0:1].rearrange("g a -> a g").to_broadcast([P, 4])),
                             (w00[:, 1, :], sgu_b[0, :, 0:1].rearrange("g a -> a g").to_broadcast([P, 4]))):
                pool.dma_start(dst, src).then_inc(even_in, 16)
                n += 1
            assert n == 12
            pool.dma_start(rope[:], c_rope.rearrange("a p t -> p a t")).then_inc(idx_in, 16)
            pool.dma_start(pick[:], c_pick[0:8, :]).then_inc(idx_in, 16)
            pool.dma_start(sg[:], c_pick[8:9, :].rearrange("a p -> p a")).then_inc(idx_in, 16)
            pool.dma_start(wrt[:], router_w[0].rearrange("(k p) e -> p k e", p=P)).then_inc(idx_in, 16)
            pool.dma_start(wrb[:], router_b).then_inc(idx_in, 16)
            for pg in range(NPG):
                src = page_table[:, pg:pg + 1].rearrange("b a -> a b").to_broadcast([16, TS])
                pool.dma_start(idx[16 * pg:16 * pg + 16, 0, :], src).then_inc(idx_in, 16)
            pool.wait_ge(even_in, 16 * 12)
            pool.affine_select(out=wsr, in_=wsr, pattern=[[0, 4], [-1, P]], compare_op=ALU.is_ge, fill=0.0,
                               base=0, channel_multiplier=1).then_inc(causal_w, 1)
            pool.dma_start(conv_s[0, :, 0, :], str_[1:16:2, :]).then_inc(state_stored, 16)

            pool.wait_ge(idx_done, 1)
            kirows = cache_kidx[0].rearrange("n (r s) d -> (n r) (s d)", s=RUN)
            krows = cache_k[0].rearrange("n (r s) h d -> (n r) (s h d)", s=4)
            vrows = cache_v[0].rearrange("n (r s) h d -> (n r) (s h d)", s=RUN)
            off = lambda a, b: bass.IndirectOffsetOnAxis(ap=idx[:, a, b:b + 1].bitcast(U32), axis=0)

            def gather_ki(b):
                pool.indirect_dma_start(out=kibuf[b % 2], out_offset=None, in_=kirows,
                                        in_offset=off(0, b)).then_inc(ki_in[b % 2], 16)

            def gather_k(u):
                pool.indirect_dma_start(out=kbuf[u % 2], out_offset=None, in_=krows,
                                        in_offset=off(1 + u % 2, u // 2)).then_inc(k_in[u % 2], 16)

            def gather_v(b):
                dst = (rT, sqT)[b % 2][:].rearrange("p c t -> p (c t)")[:, 0:RUN * 256]
                pool.indirect_dma_start(out=dst, out_offset=None, in_=vrows,
                                        in_offset=off(0, b)).then_inc(v_in[b % 2], 16)

            for b in range(2):
                gather_ki(b)
            pool.wait_ge(x_ready, 4 + 2 * KD)
            for u in range(2):
                gather_k(u)
            for b in range(2):
                gather_v(b)
            for t in range(2):
                pool.wait_ge(rel_used, 4 * (t + 1))
                pool.affine_select(out=sc[:, t, 0:P * (t + 1)], in_=sc[:, t, 0:P * (t + 1)], pattern=[[-1, P * (t + 1)]], compare_op=ALU.is_ge,
                                   fill=NEG, base=P * t, channel_multiplier=1).then_inc(sc_causal, 1)
            for t in range(2):
                pool.wait_ge(bias_done, t + 1)
                pool.affine_select(out=work[:, t, 0:P * (t + 1)], in_=work[:, t, 0:P * (t + 1)], pattern=[[-1, P * (t + 1)]], compare_op=ALU.is_ge,
                                   fill=NEG, base=P * t, channel_multiplier=1).then_inc(bias_causal, 1)
            for b in range(2, TS):
                pool.wait_ge(ki_t, b - 1)
                gather_ki(b)
            pool.wait_ge(score_done, 2)
            pool.affine_select(out=sc9, in_=sc9, pattern=[[-1, 8]], compare_op=ALU.is_equal, fill=NEG,
                               base=0, channel_multiplier=1).then_inc(new_masked, 1)
            for u in range(2, 2 * TS):
                pool.wait_ge(k_t, 2 * (u - 1))
                gather_k(u)
            for b in range(2, TS):
                pool.wait_ge(v_used, b - 1)
                gather_v(b)
            for a, v in enumerate((ln2_g, ln2_b)):
                pool.dma_start(cache[:, D * a:D * a + D], v[1:2, :].to_broadcast([P, D])).then_inc(gb_in, 16)

            pool.wait_ge(xt_copied, 6)
            pool.dma_start(x_rows[0:TP, :].rearrange("(t p) d -> p t d", p=P), xrow[:, 0:2, :]).then_inc(rows_stored, 16)
            pool.dma_start(x_rows[TP:T, :], xrow[0:8, 2, :]).then_inc(rows_stored, 16)

            def gather_x(now, places):
                pool.wait_ge(cur_ready, now)
                pool.sem_inc(gathers_due, 1)
                if places:
                    pool.wait_ge(sel_done, places)
                pool.indirect_dma_start(out=xg, out_offset=None, in_=x_rows,
                                        in_offset=bass.IndirectOffsetOnAxis(ap=curi[0:CAP, 0:1].bitcast(U32), axis=0)
                                        ).then_inc(xg_in, 16)

            pool.wait_ge(rows_cleared, 16)
            pool.wait_ge(rows_stored, 32)
            gather_x(1, 0)
            pool.wait_ge(passes_ready, 1)
            n = pool.value_load(npass[0:1, 0:1], min_val=NE, max_val=ROUNDS * NE)
            with pool.Fori(0, n) as i:
                pool.wait_ge(group_done, G_MOE + (i - 1) * G_EXP + KD + 2)
                gather_x(i + 2, ROUNDS)
                pool.wait_ge(group_free, G_MOE + (i + 1) * G_EXP)
                pool.dma_start(r_rows[bass.ds(i * CAP, CAP), :], orow).then_inc(rows_stored, 16)
            pool.wait_ge(rows_stored, 32 + 16 * n)
            pool.sem_inc(gathers_due, 1)
            pool.wait_ge(rowk_ready, 1)
            for t in range(3):
                m = P if t < 2 else 8
                for k in range(2):
                    pool.indirect_dma_start(out=res[0:m, t, k, :], out_offset=None, in_=r_rows,
                                            in_offset=bass.IndirectOffsetOnAxis(
                                                ap=rowk[0:m, t, k:k + 1].bitcast(U32), axis=0)).then_inc(res_in[t], 16)

        @block.tensor
        def _(pe):
            done = Count(group_done)
            loads = [Count(s) for s in slab_in]
            got = [0]

            def arrived(s, by=16):
                loads[s].k += by
                pe.wait_ge(slab_in[s], loads[s].base + loads[s].k)

            def bank():
                g = done.base + done.k
                if done.phase + done.k >= NB:
                    pe.wait_ge(group_free, g - (NB - 1))
                return ps[(done.phase + done.k) % NB]

            def group(lhs, rhs, n, m=P):
                out = bank()[0:m, 0:T]
                for k in range(n):
                    mm = pe.matmul(out, lhs(k), rhs(k), start=(k == 0), stop=(k == n - 1))
                done.inc(mm)

            def stats(c, n, src, sq, ready):
                if c == 0 and got[0]:
                    pe.wait_ge(var_done, got[0])
                pe.wait_ge(*ready)
                squares[0] += 1
                pe.wait_ge(sq_done, squares[0])
                pe.matmul(ps[4][:, 0:T], ones[:], src[:, c, :], start=(c == 0), stop=(c == n - 1))
                mm = pe.matmul(ps[5][:, 0:T], ones[:], sq[:, c, :], start=(c == 0), stop=(c == n - 1))
                if c == n - 1:
                    mm.then_inc(stats_done, 1)
                    got[0] += 1

            squares = [0]

            def proj_with_stats(slots, rhs, g0, by=16):
                for n, s in enumerate(slots):
                    arrived(s, by)
                    for j in range(4):
                        c = 4 * n + j
                        group(lambda k: slab(s, KD, 512)[:, k, P * j:P * j + P], rhs, KD)
                        if c:
                            stats(c - 1, KD, rT, sqT, (group_free, g0 + c))
                stats(KD - 1, KD, rT, sqT, (group_free, g0 + KD))

            x = lambda k: xT[:, k, :]
            y = lambda k: yT[:, k, :]

            pe.wait_ge(consts_in, 16)
            pe.wait_ge(x_in, 32)
            for c in range(KD):
                b = bank()
                for t in range(2):
                    pe.transpose(b[:, P * t:P * t + P], xtok[:, t, P * c:P * c + P], ident)
                done.inc(pe.transpose(b[:, TP:T], xstok[:, P * c:P * c + P], square[0:8, 0, 0:8]))
            pe.wait_ge(even_in, 16 * 12)
            pe.wait_ge(causal_w, 1)
            pe.wait_ge(pool_consts, 8)
            pe.transpose(ps[6][:, 0:NVEC], vecraw[:], square[0:NVEC, 0, 0:NVEC])
            for c in range(4):
                mm = pe.transpose(ps[6][:, 128 + 16 * c:144 + 16 * c], str_[:, P * c:P * c + P], square[0:16, 0, 0:16])
            mm.then_inc(even_t, 1)
            for g in range(4):
                mm = pe.transpose(ps[7][:, P * g:P * g + P], wsr[:, g, :], ident)
            mm.then_inc(even_t, 1)

            pe.wait_ge(group_free, KD)
            for n, s in enumerate(S_EIN):
                arrived(s)
                for j in range(4):
                    group(lambda k: slab(s, KD, 512)[:, k, P * j:P * j + P], x, KD)
                if n == 1:
                    for c in range(4):
                        stats(c, 4, hT[:, 16:20, :], sqT, (group_free, G_EIN + c + 1))
                if n == 3:
                    pe.wait_ge(x_ready, 4)
                    pe.wait_ge(even_tc, 2)
                    for t in range(2):
                        for c in range(4):
                            mm = pe.transpose(ps[6 + t][:, P * c:P * c + P], hT[:, 16 + c, P * t:P * t + P], ident)
                    mm.then_inc(vt_done, 1)
            pe.wait_ge(vt_copied, 1)
            for g in range(4):
                b = bank()
                for t in range(2):
                    pe.matmul(b[:, P * t:P * t + P], vtok[:, t, P * g:P * g + P], wsT[:, g, :], start=True, stop=False)
                    mm = pe.matmul(b[:, P * t:P * t + P], one8[0:1, :], sgb[:, P * g:P * g + P], start=False, stop=True)
                done.inc(mm)
            pe.wait_ge(z_done, 1)
            for c in range(4):
                mm = pe.transpose(ps[6][0:10, P * c:P * c + P], zlast[:, c, :], ident)
            mm.then_inc(z_t, 1)
            for c in range(4):
                mm = pe.transpose(ps[7][0:8, P * c:P * c + P], hT[:, 16 + c, TP:T], ident)
            mm.then_inc(z_t, 1)
            pe.wait_ge(group_free, G_EOUT)
            proj_with_stats(S_EOUT, y, G_EOUT)

            def up(s, xin):
                arrived(s, 32)
                for j in range(2):
                    for v in up_views(s):
                        group(lambda k: v[:, k, P * j:P * j + P], xin, KD)

            pe.wait_ge(x_ready, 4 + KD)
            with pe.Fori(0, 2) as i:
                done.enter(i, 20)
                for s in S_UP:
                    loads[s].enter(i, 32)
                    up(s, x)
                    loads[s].leave(2)
                done.leave(2)
            up(S_UPLAST, x)
            pe.wait_ge(group_free, G_DOWN)
            for i in range(2):
                for pair in range(2):
                    pr = S_DOWN[2 * pair:2 * pair + 2]
                    for s in pr:
                        arrived(s)
                    for j in range(2):
                        c = 4 * i + 2 * pair + j
                        group(lambda k: slab(pr[k // 11], 11, 256)[:, k % 11, P * j:P * j + P],
                              lambda k: hT[:, k, :], KF)
                        if c:
                            stats(c - 1, KD, rT, sqT, (group_free, G_DOWN + c))
            stats(KD - 1, KD, rT, sqT, (group_free, G_DOWN + KD))

            pe.wait_ge(x_ready, 4 + 2 * KD)
            pe.wait_ge(idx_in, 16 * 13)
            pe.wait_ge(var_done, got[0])
            turned = []

            def rotate(n, g):
                q = len(turned)
                pe.wait_ge(group_free, g + 1)
                if q >= 2:
                    pe.wait_ge(roped, q - 1)
                pe.matmul(ps[4 + q % 2][:, 0:T], rot, hT[:, n, :], start=True, stop=True).then_inc(rot_done, 1)
                turned.append(n)

            todo = []
            for s, n0, kind in zip(S_OIN, (QI, KI, KK, QQ, QQ + 4), ("std", "ki", "kv", "q", "q")):
                arrived(s, {"ki": 32, "q": 128}.get(kind, 16))
                if kind == "ki":
                    v = slab(s, KD, 136)
                    todo.append((KI, done.k))
                    group(lambda k: v[:, k, 0:P], x, KD)
                    group(lambda k: v[:, k, P:P + 8], x, KD, m=8)
                    continue
                for j in range(4):
                    now = (n0 + j, done.base + done.k)
                    group(lambda k: slab(s, KD, 512)[:, k, P * j:P * j + P], x, KD)
                    if todo:
                        rotate(*todo.pop(0))
                    if kind != "kv" or j < 2:
                        todo.append(now)
            for now in todo:
                rotate(*now)
            assert turned == ROPED, turned
            pe.wait_ge(roped, len(ROPED))
            for t in range(2):
                for c in range(4):
                    pe.transpose(ps[4 + t][:, P * c:P * c + P], hT[:, KK + c, P * t:P * t + P], ident)
            for c in range(4):
                pe.transpose(ps[6][0:8, P * c:P * c + P], hT[:, KK + c, TP:T], ident)
            for t in range(2):
                pe.transpose(ps[7][:, 64 * t:64 * t + 64], hT[0:64, KI, P * t:P * t + P], square[0:64, 0, 0:64])
                pe.transpose(ps[7][:, 192 + 8 * t:200 + 8 * t], wiT[:, P * t:P * t + P], square[0:8, 0, 0:8])
            pe.transpose(ps[7][0:8, 128:192], hT[0:64, KI, TP:T], square[0:64, 0, 0:64]).then_inc(tok_t, 1)

            for u in range(4):
                t, c0 = u // 2, 2 * (u % 2)
                L = P * (t + 1)
                for half in range(2):
                    if u >= 2:
                        pe.wait_ge(rel_done, 2 * (u - 2) + half + 1)
                    for c in range(2):
                        mm = pe.matmul(ps[2 * (u % 2) + half][:, 256 * c:256 * c + L],
                                       hT[64 * half:64 * half + 64, QI + c0 + c, P * t:P * t + P],
                                       hT[64 * half:64 * half + 64, KI, 0:L], start=True, stop=True)
                    mm.then_inc(dots_done, 1)

            def logits(u):
                t, c0 = u // 4, 2 * (u % 4)
                L = P * (t + 1)
                for half in range(2):
                    if u >= 2:
                        pe.wait_ge(lg_read, 2 * (u - 2) + half + 1)
                    else:
                        pe.wait_ge(rel_done, 8)
                    for c in range(2):
                        mm = pe.matmul(ps[2 * (u % 2) + half][:, 256 * c:256 * c + L],
                                       hT[64 * half:64 * half + 64, QQ + c0 + c, P * t:P * t + P],
                                       hT[64 * half:64 * half + 64, KK + c0 // 4, 0:L], start=True, stop=True)
                    mm.then_inc(lg_done, 1)

            def values(u):
                t, c0 = u // 4, 2 * (u % 4)
                nb = t + 1
                for half in range(2):
                    v = 2 * u + half
                    pe.wait_ge(prob_done, v + 1)
                    if v >= 2:
                        pe.wait_ge(pt_copied, v - 1)
                    for c in range(2):
                        for k in range(nb):
                            mm = pe.transpose(ps[4 + v % 2][:, P * (c * nb + k):P * (c * nb + k) + P],
                                              S[u % 2][:, half, c, P * k:P * k + P], ident)
                    mm.then_inc(pt_done, 1)
                for half in range(2):
                    v = 2 * u + half
                    pe.wait_ge(pt_copied, v + 1)
                    if u >= 2 and half == 0:
                        pe.wait_ge(o_copied, u - 1)
                    head = 2 * (c0 // 4) + half
                    for c in range(2):
                        for k in range(nb):
                            mm = pe.matmul(ps[6 + u % 2][64 * half:64 * half + 64, P * c:P * c + P],
                                           ktv[:, k, 256 + 64 * head:320 + 64 * head],
                                           PT[v % 2][:, P * (c * nb + k):P * (c * nb + k) + P],
                                           start=(k == 0), stop=(k == nb - 1))
                    mm.then_inc(o_done, 1)

            pe.wait_ge(tok_copied, 5)
            logits(0)
            for u in range(8):
                if u < 7:
                    logits(u + 1)
                values(u)

            pe.wait_ge(o_copied, 8)
            pe.matmul(ps[6][:, 0:32].rearrange("p (c b) -> p c b", c=4), swap, hT[:, QI:QI + 4, TP:T],
                      start=True, stop=True).then_inc(swapped, 1)
            pe.wait_ge(wib_in, 1)
            pe.matmul(ps[6][:, 64:128], one8[:], dwi, start=True, stop=True).then_inc(swapped, 1)
            pe.wait_ge(qi_ready, 2)
            for b in range(TS):
                pe.wait_ge(ki_in[b % 2], 16 * (b // 2 + 1))
                if b >= 2:
                    pe.wait_ge(ki_copied, b - 1)
                else:
                    pe.wait_ge(lg_read, 16)
                for c in range(4):
                    mm = pe.transpose(ps[b % 2][:, P * c:P * c + P], kibuf[b % 2][:, P * c:P * c + P], ident)
                mm.then_inc(ki_t, 1)
                pe.wait_ge(ki_copied, b + 1)
                for r in range(RUN):
                    h = r % 2
                    mm = pe.matmul(ps[2 + h][:, 32 * b + 8 * (r // 2):32 * b + 8 * (r // 2) + 8],
                                   kiT[b % 2][64 * h:64 * h + 64, P * (r // 2):P * (r // 2) + P],
                                   qiB[64 * h:64 * h + 64, b, :], start=True, stop=True)
                mm.then_inc(ki_mm, 1)
            pe.matmul(ps[2][0:8, 256:320], hT[0:64, KI, TP:T], qiB[0:64, :, :], start=True, stop=True)
            pe.matmul(ps[3][0:8, 256:257], one8[:, 0:8], one8[:, 0:1], start=True, stop=True).then_inc(sdots, 1)
            pe.wait_ge(score_done, 1)
            for a in range(2):
                for r in range(4):
                    pe.transpose(ps[4 + a][0:8, P * r:P * r + P], score[:, a, r, :], ident)
            pe.wait_ge(new_masked, 1)
            pe.transpose(ps[7][0:8, 0:8], sc9, square[0:8, 0, 0:8]).then_inc(row_t, 1)

            pe.wait_ge(qbd_done, 1)
            for u in range(2 * TS):
                b, hf = u // 2, u % 2
                pe.wait_ge(k_in[hf], 16 * (b + 1))
                for j in range(2):
                    if u >= 1:
                        pe.wait_ge(k_copied, 2 * (u - 1) + j + 1)
                    for r in range(4):
                        mm = pe.transpose(ps[j][:, P * r:P * r + P],
                                          kbuf[hf][:, 256 * r + P * j:256 * r + P * j + P], ident)
                    mm.then_inc(k_t, 1)
                if u == 0:
                    pe.wait_ge(srel_done, 3)
                for j in range(2):
                    pe.wait_ge(k_copied, 2 * u + j + 1)
                    for r in range(4):
                        o = P * r + 16 * b + 8 * j
                        mm = pe.matmul(ps[2 + hf][:, o:o + 8], KT[u % 2][:, r, j, :], qbd[:, j, b, :],
                                       start=True, stop=True)
                mm.then_inc(k_mm, 1)
            for j in range(2):
                mm = pe.matmul(ps[6][0:8, 0:P].rearrange("p (b j x) -> p b j x", b=8, j=2)[:, :, j, :],
                               hT[:, KK + j, TP:T], qbd[:, j, :, :], start=True, stop=True)
            mm.then_inc(slg_done, 1)
            pe.wait_ge(row_masked, 1)
            rv = row[:, 0:1024].rearrange("b (s r) -> b r s", r=8)
            for a in range(2):
                pe.matmul(ps[4 + a][:, :], pick[:], rv[:, 4 * a:4 * a + 4, :], start=True, stop=True)
            pe.matmul(ps[7][:, 0:8], pick[:], row[:, 1024:1032], start=True, stop=True).then_inc(mask_wide, 1)
            pe.wait_ge(slg_copied, 3)
            for a in range(2):
                for r in range(4):
                    pe.transpose(ps[2 + a][:, P * r:P * r + P], lgS[:, 512 * a + P * r:512 * a + P * r + P], ident)
            pe.transpose(ps[6][:, 256:264], lgS[0:8, 1024:1152], square[0:8, 0, 0:8]).then_inc(slg_t, 1)
            pe.wait_ge(sprob_done, 1)
            for a in range(2):
                for r in range(4):
                    pe.transpose(ps[a][:, P * r:P * r + P], SS[:, 512 * a + P * r:512 * a + P * r + P], ident)
            pe.transpose(ps[6][0:8, 0:P], SS[:, 1024:1032], ident).then_inc(spt_done, 1)
            pe.wait_ge(spt_copied, 3)
            for b in range(TS):
                pe.wait_ge(v_in[b % 2], 16 * (b // 2 + 1))
                vb = (rT, sqT)[b % 2][:].rearrange("p c t -> p (c t)")
                for j in range(2):
                    out = ps[4][:, 64 * j + 8 * b:64 * j + 8 * b + 8]
                    for r in range(RUN):
                        pe.matmul(out, vb[:, 256 * r + P * j:256 * r + P * j + P],
                                  PTs[:, r, 16 * b + 8 * j:16 * b + 8 * j + 8], start=(r == 0), stop=False)
                    mm = pe.matmul(out, kvs[0:8, 256 + P * j:256 + P * j + P],
                                   PTs[0:8, 8, 16 * b + 8 * j:16 * b + 8 * j + 8], start=False, stop=True)
                mm.then_inc(v_used, 1)

            pe.wait_ge(so_done, 1)
            proj_with_stats(S_OOUT, y, G_OOUT, by=64)
            pe.wait_ge(x_ready, 4 + 3 * KD)
            for t in range(3):
                m = P if t < 2 else 8
                out = ps[6][0:m, 8 * t:8 * t + 8]
                for k in range(KD):
                    pe.matmul(out, xT[:, k, P * t:P * t + m], wrt[:, k, :], start=(k == 0), stop=False)
                mm = pe.matmul(out, one8[0:1, 0:m], wrb[:], start=False, stop=True)
                mm.then_inc(route_done, 1)
            for t in range(3):
                m = P if t < 2 else 8
                for a in range(2):
                    q = 2 * t + a
                    if q >= 2:
                        pe.wait_ge(xt_copied, q - 1)
                    else:
                        pe.wait_ge(var_done, got[0])
                    for c in range(4):
                        mm = pe.transpose(ps[4 + q % 2][0:m, P * c:P * c + P], xT[:, 4 * a + c, P * t:P * t + m], ident)
                    mm.then_inc(xt_t, 1)
            pe.wait_ge(chosen, 1)
            for t in range(4):
                m = 8 if t == 2 else P
                out = ps[7][0:m, 8 * t:8 * t + 8]
                last = min(t, 2)
                for k in range(last + 1):
                    mk = P if k < 2 else 8
                    w = before if k == t else all1
                    mm = pe.matmul(out, w[0:mk, 0:m], choice[0:mk, 2, k, :], start=(k == 0), stop=(k == last))
            mm.then_inc(counted, 1)
            for r in range(ROUNDS):
                for e in range(NE):
                    out = ps[(6, 7, 6)[r]][0:CAP, 2 * e:2 * e + 2]
                    for t in range(3):
                        m = P if t < 2 else 8
                        if e == 0:
                            pe.wait_ge(sel_ready, 3 * r + t + 1)
                        mm = pe.matmul(out, sel[0:m, t, e, :], tg[0:m, t, e, :], start=(t == 0), stop=(t == 2))
                mm.then_inc(sel_done, 1)

            def gathered():
                for a in range(2):
                    b = bank()
                    for c in range(4):
                        mm = pe.transpose(b[:, CAP * c:CAP * c + CAP], xg[:, P * (4 * a + c):P * (4 * a + c) + P],
                                          square[0:CAP, 0, 0:CAP])
                    done.inc(mm)

            pe.wait_ge(xg_in, 16)
            gathered()
            pe.wait_ge(passes_ready, 1)
            n = pe.value_load(npass[0:1, 0:1], min_val=NE, max_val=ROUNDS * NE)
            with pe.Fori(0, n) as i:
                done.enter(i, G_EXP)
                for s in range(NSLOT):
                    loads[s].enter(i, 32 if s < 4 else 16)
                pe.wait_ge(group_free, done.base)
                for s in range(4):
                    arrived(s, 32)
                    for j in range(2):
                        b = bank()
                        for a, v in enumerate(up_views(s)):
                            for k in range(KD):
                                mm = pe.matmul(b[:, CAP * a:CAP * a + CAP], v[:, k, P * j:P * j + P], xgT[:, k, :],
                                               start=(k == 0), stop=(k == KD - 1))
                        done.inc(mm)
                pe.wait_ge(xg_in, 16 * (i + 2))
                gathered()
                pe.wait_ge(group_free, done.base + KD)
                for s in (4, 5):
                    arrived(s)
                    b = bank()
                    for k in range(KD):
                        mm = pe.matmul(b[0:CAP, :], hg[:, k, :], slab(s, KD, 512)[:, k, :],
                                       start=(k == 0), stop=(k == KD - 1))
                    done.inc(mm)
                for s in range(NSLOT):
                    loads[s].leave(n)
                done.leave(n)

        @block.scalar
        def _(act):
            norms, cen = [0], [0]

            def squares(n, src, ready):
                for c in range(n):
                    act.wait_ge(ready[0], ready[1] + c + 1)
                    act.activation(sqT[:, c, :], src[:, c, :], ACT.Square).then_inc(sq_done, 1)

            def norm(n, dst, src, g, b):
                norms[0] += 1
                act.wait_ge(var_done, norms[0])
                act.activation(rstd[:], var[:], ACT.Sqrt, bias=eps[:, 0:1]).then_inc(std_done, 1)
                for c in range(n):
                    cen[0] += 1
                    act.wait_ge(centred, cen[0])
                    act.activation(dst[:, c, :], src[:, c, :], ACT.Identity, scale=vec[:, g + c:g + c + 1],
                                   bias=vec[:, b + c:b + c + 1]).then_inc(x_ready, 1)

            def silus(n, g0, first):
                for m in range(n):
                    act.wait_ge(group_done, g0 + 2 * m + 1)
                    act.wait_ge(group_free, g0 + 2 * m - 2)
                    act.activation(silu[:, m % 2, :], ps[(first + 2 * m) % NB][:, 0:T], ACT.Silu).then_inc(silu_done, 1)

            vT = hT[:, 16:20, :]
            squares(4, vT, (group_free, G_EIN))
            act.wait_ge(even_tc, 2)
            act.wait_ge(pool_consts, 8)
            norm(4, vT, vT, V_SG, V_SB)
            squares(KD, rT, (group_free, G_EOUT))
            norm(KD, xT, rT, V_LN1G, V_LN1B)
            with act.Fori(0, 2) as i:
                silus(10, G_UP + 20 * i, G_UP % NB)
            silus(2, G_UP + 40, G_UP % NB)
            squares(KD, rT, (group_free, G_DOWN))
            norm(KD, xT, rT, V_LN2G, V_LN2B)
            act.wait_ge(zeros_ready, 1)
            act.dma_start(r_rows[NE * CAP:ROUNDS * NE * CAP, :].rearrange("(p a) (c q) -> p (a c) q", p=P, q=512),
                          silu[:].rearrange("p a t -> p (a t)")[:, 0:512].unsqueeze(1)
                          .to_broadcast([P, (ROUNDS - 1) * NE * CAP * 2 // P, 512])
                          ).then_inc(rows_cleared, 16)

            act.wait_ge(tok_t, 1)
            act.copy(ktv[:, 0, :], ps[4][:, :]).then_inc(tok_copied, 1)
            act.copy(kvs[:], ps[6][0:8, :]).then_inc(tok_copied, 1)
            for u in range(4):
                L = P * (u // 2 + 1)
                for half in range(2):
                    v = 2 * u + half
                    act.wait_ge(dots_done, v + 1)
                    if v >= 2:
                        act.wait_ge(rel_used, v - 1)
                    src = ps[2 * (u % 2) + half][:, :].rearrange("p (c s) -> p c s", c=2)[:, :, 0:L]
                    act.activation(rel[half][:, :, 0:L], src, ACT.Relu, scale=0.125).then_inc(rel_done, 1)

            def exps(u):
                L = P * (u // 4 + 1)
                for half in range(2):
                    act.wait_ge(lg_read, 2 * u + half + 1)
                    for c in range(2):
                        col = 4 * (u % 2) + 2 * half + c
                        row_ = S[u % 2][:, half, c, 0:L]
                        ins = act.activation(row_, row_, ACT.Exp, bias=stat[:, col:col + 1],
                                             accum_out=stat[:, 8 + col:9 + col])
                    ins.then_inc(exp_done, 1)

            def probs_by_key(u):
                n = 256 * (u // 4 + 1)
                for half in range(2):
                    v = 2 * u + half
                    act.wait_ge(pt_done, v + 1)
                    if v >= 2:
                        act.wait_ge(o_done, v - 1)
                    act.copy(PT[v % 2][:, 0:n], ps[4 + v % 2][:, 0:n]).then_inc(pt_copied, 1)

            act.wait_ge(even_stored, 16 * 3)
            act.wait_ge(state_stored, 16)
            exps(0)
            for u in range(8):
                if u < 7:
                    exps(u + 1)
                probs_by_key(u)

            for b in range(TS):
                act.wait_ge(ki_t, b + 1)
                if b >= 2:
                    act.wait_ge(ki_mm, b - 1)
                act.copy(kiT[b % 2], ps[b % 2][:, :]).then_inc(ki_copied, 1)
            act.wait_ge(sdots, 1)
            for a in range(2):
                act.activation(srel[:, 256 * a:256 * a + 256], ps[2 + a][:, 0:256], ACT.Relu,
                               scale=0.125).then_inc(srel_done, 1)
            act.activation(srel[0:8, 512:576], ps[2][0:8, 256:320], ACT.Relu, scale=0.125).then_inc(srel_done, 1)
            for u in range(2 * TS):
                for j in range(2):
                    act.wait_ge(k_t, 2 * u + j + 1)
                    if u >= 2:
                        act.wait_ge(k_mm, u - 1)
                    act.copy(KT[u % 2][:, :, j, :],
                             ps[j][:, :].rearrange("p (r s) -> p r s", r=4)).then_inc(k_copied, 1)
            act.wait_ge(slg_done, 1)
            for a in range(2):
                act.copy(lgS[:, 512 * a:512 * a + 512], ps[2 + a][:, :]).then_inc(slg_copied, 1)
            act.copy(lgS[0:8, 1024:1152], ps[6][0:8, 0:P]).then_inc(slg_copied, 1)
            act.wait_ge(mask_wide, 1)
            for a in range(2):
                act.mul(bSS[:, 512 * a:512 * a + 512], ps[4 + a][:, :], NEG).then_inc(mask_copied, 1)
            act.mul(bSS[:, 1024:1032], ps[7][:, 0:8], NEG).then_inc(mask_copied, 1)
            act.wait_ge(smax_done, 1)
            act.activation(SS, SS, ACT.Exp, bias=st8[:, 0:1], accum_out=st8[:, 1:2]).then_inc(sexp_done, 1)
            act.wait_ge(spt_done, 1)
            for a in range(2):
                act.copy(PTs[:, 4 * a:4 * a + 4, :].rearrange("p r q -> p (r q)"), ps[a][:, :]).then_inc(spt_copied, 1)
            act.copy(PTs[0:8, 8, :], ps[6][0:8, 0:P]).then_inc(spt_copied, 1)
            squares(KD, rT, (group_free, G_OOUT))
            norm(KD, xT, rT, V_LN1G + 8, V_LN1B + 8)
            for t in range(3):
                m = P if t < 2 else 8
                for a in range(2):
                    q = 2 * t + a
                    act.wait_ge(xt_t, q + 1)
                    act.copy(xrow[0:m, t, 512 * a:512 * a + 512], ps[4 + q % 2][0:m, :]).then_inc(xt_copied, 1)
                    if q == 1:
                        act.wait_ge(route_in, 1)
                        act.activation(gate[:, 1, :], gate[:, 0, :], ACT.Exp).then_inc(gate_e, 1)
            act.wait_ge(passes_ready, 1)
            act.wait_ge(rows_cleared, 16)
            n = act.value_load(npass[0:1, 0:1], min_val=NE, max_val=ROUNDS * NE)
            with act.Fori(0, n) as i:
                for m in range(KD):
                    act.wait_ge(group_done, G_MOE + i * G_EXP + m + 1)
                    act.wait_ge(group_free, G_MOE + i * G_EXP + m - 1)
                    act.activation(silug[:, m % 2, :], ps[(G_MOE + m) % NB][:, 0:CAP], ACT.Silu).then_inc(silu_done, 1)
            act.wait_ge(fvar, 1)
            act.activation(fin[:, :, 14], fin[:, :, 13], ACT.Sqrt, bias=eps[:, 0:1]).then_inc(fstd, 1)

        @block.vector
        def _(dve):
            V = nc.vector
            chain = Count(dchain)
            free = Count(group_free)
            norms = [0]

            def mark(ins):
                return chain.inc(ins)

            def link(ins):
                dve.wait_ge(dchain, chain.inc(ins))

            def filled(ahead=0):
                dve.wait_ge(group_done, free.base + free.k + 1 + ahead)
                return ps[(free.phase + free.k + ahead) % NB]

            def residual(n):
                for c in range(n):
                    free.inc(V.scalar_tensor_tensor(out=rT[:, c, :], in0=xT[:, c, :], scalar=ALPHA,
                                                    in1=filled()[:, 0:T], op0=ALU.mult, op1=ALU.add))

            def norm(n, src):
                norms[0] += 1
                scale = float(KD // n)
                dve.wait_ge(stats_done, norms[0])
                link(V.tensor_scalar(mean[:], ps[4][:, 0:T], scale, None, ALU.mult))
                link(V.tensor_tensor(var[:], mean[:], mean[:], ALU.mult))
                V.scalar_tensor_tensor(out=var[:], in0=ps[5][:, 0:T], scalar=scale, in1=var[:],
                                       op0=ALU.mult, op1=ALU.subtract).then_inc(var_done, 1)
                dve.wait_ge(std_done, norms[0])
                link(V.reciprocal(rstd[:], rstd[:]))
                at = [mark(V.tensor_tensor(src[:, 0, :], src[:, 0, :], mean[:], ALU.subtract))]
                for c in range(n):
                    if c + 1 < n:
                        at.append(mark(V.tensor_tensor(src[:, c + 1, :], src[:, c + 1, :], mean[:], ALU.subtract)))
                    dve.wait_ge(dchain, at[c])
                    V.tensor_tensor(src[:, c, :], src[:, c, :], rstd[:], ALU.mult).then_inc(centred, 1)

            V.memset(lgr[:], 0.0)
            V.memset(place[:], 0.0)
            V.memset(fin[:], 1.0)
            V.memset(tokg[:, ROUNDS * NE, :], 0.0)
            for c in range(KD):
                free.inc(V.tensor_copy(xT[:, c, :], filled()[:, 0:T]))
            dve.wait_ge(even_t, 1)
            V.tensor_copy(vec[:], ps[6][:, 0:NVEC])
            V.tensor_copy(stT, ps[6][:, 128:192].rearrange("p (c n) -> p c n", c=4)).then_inc(even_tc, 1)
            dve.wait_ge(even_t, 2)
            V.tensor_copy(wsT, ps[7][:, :].rearrange("p (g i) -> p g i", g=4)).then_inc(even_tc, 1)
            dve.wait_ge(idx_in, 16 * 13)
            link(V.tensor_copy(idxf[:], idx[:, 0, :]))
            link(V.tensor_scalar(idxf[:], idxf[:], float(PAGE // RUN), sg[:, 0:1], ALU.mult, ALU.add))
            V.tensor_copy(idx[:, 0, :], idxf[:])
            V.tensor_scalar(idx[:, 1, :], idxf[:], 2.0, None, ALU.mult)
            V.tensor_scalar(idx[:, 2, :], idxf[:], 2.0, 1.0, ALU.mult, ALU.add).then_inc(idx_done, 1)

            dve.wait_ge(even_tc, 2)
            V.memset(zext[:, :, 0:2], 0.0)
            for c in range(4):
                free.inc(V.tensor_copy(hT[:, 16 + c, :], filled()[:, 0:T]))
            for c in range(4):
                free.inc(V.tensor_copy(hT[:, 4 + c, :], filled()[:, 0:T]))
            norm(4, hT[:, 16:20, :])
            dve.wait_ge(group_free, free.k)
            w_ = lambda j, c: vec[:, V_CW + 4 * j + c:V_CW + 4 * j + c + 1]
            for c in range(4):
                b = filled()
                mark(V.tensor_tensor(zext[:, c, 2:258], b[:, 0:TP], hT[:, 4 + c, 0:TP], ALU.mult))
                free.inc(V.tensor_tensor(zlast[:, c, 2:10], b[:, TP:T], hT[:, 4 + c, TP:T], ALU.mult))
                dve.wait_ge(group_free, free.k)
                mark(V.tensor_scalar(cst, zext[:, c, 2:258], w_(2, c), None, ALU.mult))
                link(V.tensor_scalar(css, zlast[:, c, 2:10], w_(2, c), None, ALU.mult))
                mark(V.scalar_tensor_tensor(out=cst, in0=zext[:, c, 1:257], scalar=w_(1, c), in1=cst,
                                            op0=ALU.mult, op1=ALU.add))
                link(V.scalar_tensor_tensor(out=css, in0=stT[:, c, 1:16:2], scalar=w_(1, c), in1=css,
                                            op0=ALU.mult, op1=ALU.add))
                mark(V.scalar_tensor_tensor(out=hT[:, 8 + c, 0:TP], in0=zext[:, c, 0:256], scalar=w_(0, c), in1=cst,
                                            op0=ALU.mult, op1=ALU.add))
                link(V.scalar_tensor_tensor(out=hT[:, 8 + c, TP:T], in0=stT[:, c, 0:16:2], scalar=w_(0, c), in1=css,
                                            op0=ALU.mult, op1=ALU.add))
            V.tensor_copy(zlast[:, :, 0:2], zext[:, :, 256:258]).then_inc(z_done, 1)
            for c in range(4):
                free.inc(V.tensor_copy(hT[:, 12 + c, :], filled()[:, 0:T]))
            dve.wait_ge(vt_done, 1)
            for t in range(2):
                ins = V.tensor_copy(vtok[:, t, :], ps[6 + t][:, :])
            ins.then_inc(vt_copied, 1)
            for c in range(4):
                free.inc(V.tensor_tensor(yT[:, c, :], filled()[:, 0:T], hT[:, 8 + c, :], ALU.mult))
            dve.wait_ge(x_ready, 4)
            for g in range(4):
                b = filled()
                V.tensor_tensor(yT[:, 4 + g, 0:TP], b[:, 0:TP], hT[:, 12 + g, 0:TP], ALU.mult)
                link(V.tensor_scalar(css, hT[:, 16 + g, TP:T], w00[:, 0, g:g + 1], w00[:, 1, g:g + 1],
                                     ALU.mult, ALU.add))
                free.inc(V.tensor_tensor(yT[:, 4 + g, TP:T], css, hT[:, 12 + g, TP:T], ALU.mult))
                dve.wait_ge(group_free, free.k)
            dve.wait_ge(z_t, 1)
            V.tensor_copy(zrow, ps[6][0:10, :]).then_inc(z_copied, 1)
            dve.wait_ge(z_t, 2)
            V.tensor_copy(vrow, ps[7][0:8, :]).then_inc(z_copied, 1)
            residual(KD)
            norm(KD, rT)

            def hidden(m, dst):
                filled(1)
                b = ps[(free.phase + free.k + 1) % NB]
                free.inc(V.tensor_tensor(dst, silu[:, m % 2, :], b[:, 0:T], ALU.mult), 2)

            silus = Count(silu_done)
            with dve.Fori(0, 2) as i:
                free.enter(i, 20)
                silus.enter(i, 10)
                for m in range(10):
                    silus.k += 1
                    dve.wait_ge(silu_done, silus.base + silus.k)
                    hidden(m, hT[:, bass.ds(i * 10 + m, 1), :].rearrange("p a t -> p (a t)"))
                silus.leave(2)
                free.leave(2)
            for m in range(2):
                silus.k += 1
                dve.wait_ge(silu_done, silus.base + silus.k)
                hidden(m, hT[:, 20 + m, :])
            residual(KD)
            norm(KD, rT)

            V.memset(silu[:], 0.0).then_inc(zeros_ready, 1)

            ropes = [0]

            def turn():
                q = ropes[0]
                n = ROPED[q]
                dve.wait_ge(rot_done, q + 1)
                mark(V.tensor_tensor(mean[:], hT[:, n, :], rope[:, 0, :], ALU.mult))
                link(V.tensor_tensor(var[:], ps[4 + q % 2][:, 0:T], rope[:, 1, :], ALU.mult))
                V.tensor_tensor(hT[:, n, :], mean[:], var[:], ALU.add).then_inc(roped, 1)
                dve.wait_ge(roped, q + 1)
                ropes[0] += 1

            waiting = 0
            for n0, kind in ((QI, "std"), (KI, "ki"), (KK, "kv"), (QQ, "q"), (QQ + 4, "q")):
                if kind == "ki":
                    free.inc(V.tensor_copy(hT[:, KI, :], filled()[:, 0:T]))
                    free.inc(V.tensor_scalar(wiT[:], filled()[0:8, 0:T], 8.0 ** -0.5, None, ALU.mult))
                    waiting += 1
                    continue
                for j in range(4):
                    free.inc(V.tensor_copy(hT[:, n0 + j, :], filled()[:, 0:T]))
                    if waiting:
                        turn()
                        waiting -= 1
                    if kind != "kv" or j < 2:
                        waiting += 1
            while waiting:
                turn()
                waiting -= 1
            dve.wait_ge(tok_t, 1)
            V.tensor_copy(ktv[:, 1, :], ps[5][:, :]).then_inc(tok_copied, 1)
            V.tensor_copy(kit[0:8, 2, :], ps[7][0:8, 128:192])
            V.tensor_copy(kit[:, 0:2, :], ps[7][:, 0:128].rearrange("p (t d) -> p t d", t=2)).then_inc(tok_copied, 1)
            V.tensor_copy(wit[:], ps[7][:, 192:208].rearrange("p (t h) -> p t h", t=2)).then_inc(tok_copied, 1)
            dve.wait_ge(tok_copied, 5)
            for u in range(4):
                t, c0 = u // 2, 2 * (u % 2)
                L = P * (t + 1)
                for half in range(2):
                    v = 2 * u + half
                    dve.wait_ge(rel_done, v + 1)
                    for c in range(2):
                        wgt = wit[:, t, 2 * (c0 + c) + half:2 * (c0 + c) + half + 1]
                        src = rel[half][:, c, 0:L]
                        if u % 2 == 0 and half == 0 and c == 0:
                            ins = V.tensor_scalar(sc[:, t, 0:L], src, wgt, None, ALU.mult)
                        else:
                            ins = V.scalar_tensor_tensor(out=sc[:, t, 0:L], in0=src, scalar=wgt, in1=sc[:, t, 0:L],
                                                         op0=ALU.mult, op1=ALU.add)
                        if c == 0:
                            link(ins)
                    ins.then_inc(rel_used, 1)
                    dve.wait_ge(rel_used, v + 1)

            def select(src, dst, mx, k):
                for _ in range(k // 8):
                    link(V.max(out=mx, in_=src))
                    link(V.match_replace(out=dst, in_to_replace=mx, in_values=src, imm_value=TAKEN))
                    src = dst

            for t in range(2):
                L = P * (t + 1)
                dve.wait_ge(sc_causal, t + 1)
                select(sc[:, t, 0:L], work[:, t, 0:L], mx8p[:], TOPK_P)
                V.tensor_scalar(work[:, t, 0:L], work[:, t, 0:L], TAKEN / 2, NEG, ALU.is_gt,
                                ALU.mult).then_inc(bias_done, 1)

            def masked_logits(u):
                t = u // 4
                L = P * (t + 1)
                dve.wait_ge(bias_causal, t + 1)
                if u >= 2:
                    dve.wait_ge(pt_done, 2 * (u - 1))
                for half in range(2):
                    dve.wait_ge(lg_done, 2 * u + half + 1)
                    dst = S[u % 2][:, half, :, 0:L]
                    col = 4 * (u % 2) + 2 * half
                    link(V.scalar_tensor_tensor(
                        out=dst, in0=ps[2 * (u % 2) + half][:, :].rearrange("p (c s) -> p c s", c=2)[:, :, 0:L],
                        scalar=0.125, in1=work[:, t:t + 1, 0:L].to_broadcast([P, 2, L]), op0=ALU.mult, op1=ALU.add))
                    link(V.tensor_reduce(out=stat[:, col:col + 2], in_=dst, axis=AX, op=ALU.max))
                    V.tensor_scalar(stat[:, col:col + 2], stat[:, col:col + 2], -1.0, None,
                                    ALU.mult).then_inc(lg_read, 1)

            def probs(u):
                L = P * (u // 4 + 1)
                for half in range(2):
                    dve.wait_ge(exp_done, 2 * u + half + 1)
                    col = 4 * (u % 2) + 2 * half
                    link(V.reciprocal(stat[:, 16 + col:18 + col], stat[:, 8 + col:10 + col]))
                    for c in range(2):
                        row_ = S[u % 2][:, half, c, 0:L]
                        ins = V.tensor_scalar(row_, row_, stat[:, 16 + col + c:17 + col + c], None, ALU.mult)
                    ins.then_inc(prob_done, 1)

            def heads_out(u):
                t, c0 = u // 4, 2 * (u % 4)
                dve.wait_ge(o_done, 2 * (u + 1))
                V.tensor_copy(yT[:, c0:c0 + 2, P * t:P * t + P],
                              ps[6 + u % 2][:, 0:256].rearrange("p (c q) -> p c q", c=2)).then_inc(o_copied, 1)

            masked_logits(0)
            for u in range(8):
                if u < 7:
                    masked_logits(u + 1)
                probs(u)
                if u:
                    heads_out(u - 1)
            heads_out(7)

            link(V.memset(qbd, 0.0))
            lo, hi = slice(0, 64), slice(64, P)
            for j in range(2):
                q = hT[:, QQ + 4 * j:QQ + 4 * j + 4, TP:T].rearrange("p x b -> p b x")
                V.tensor_copy(qbd[lo, j, :, 0:4], q[lo])
                ins = V.tensor_copy(qbd[hi, j, :, 4:8], q[hi])
            ins.then_inc(qbd_done, 1)
            V.tensor_tensor(dwi.rearrange("h (b g) -> h b g", b=8),
                            wiT[:, TP:T].unsqueeze(2).to_broadcast([8, 8, 8]),
                            square[0:8, 0:1, 0:8].to_broadcast([8, 8, 8]), ALU.mult).then_inc(wib_in, 1)
            dve.wait_ge(swapped, 2)
            qv = qiB[:].rearrange("p b (c a) -> p a c b", a=2)
            raw = hT[:, QI:QI + 4, TP:T]
            swp = ps[6][:, 0:32].rearrange("p (c b) -> p c b", c=4)
            V.tensor_copy(qv[lo, 0], raw[lo])
            V.tensor_copy(qv[hi, 1], raw[hi])
            V.tensor_copy(qv[lo, 1], swp[lo])
            V.tensor_copy(qv[hi, 0], swp[hi]).then_inc(qi_ready, 1)
            V.tensor_copy(wib, ps[6][:, 64:128]).then_inc(qi_ready, 1)
            dve.wait_ge(qi_ready, 2)
            dve.wait_ge(srel_done, 3)
            for a in range(2):
                v = srel[:, 256 * a:256 * a + 256]
                link(V.tensor_tensor(v.rearrange("p (b r h) -> p b r h", b=8, r=4),
                                     v.rearrange("p (b r h) -> p b r h", b=8, r=4),
                                     wib.rearrange("p (b h) -> p b h", b=8).unsqueeze(2).to_broadcast([P, 8, 4, 8]),
                                     ALU.mult))
                ins = V.tensor_reduce(out=score[:, a].rearrange("p r b -> p b r"),
                                      in_=v.rearrange("p (b r h) -> p b r h", b=8, r=4), axis=AX, op=ALU.add)
            ins.then_inc(score_done, 1)
            v = srel[0:8, 512:576]
            link(V.tensor_tensor(v, v, wib[0:8, :], ALU.mult))
            V.tensor_reduce(out=sc9, in_=v.rearrange("p (b h) -> p b h", b=8), axis=AX,
                            op=ALU.add).then_inc(score_done, 1)
            dve.wait_ge(row_t, 1)
            rv = row[:, 0:1024].rearrange("b (p r a) -> b a r p", r=4, a=2)
            for a in range(2):
                mark(V.tensor_copy(rv[:, a], ps[4 + a][0:8, :].rearrange("b (r p) -> b r p", r=4)))
            link(V.tensor_copy(row[:, 1024:1032], ps[7][0:8, 0:8]))
            select(row, row, mx8, TOPK_S)
            V.tensor_scalar(row, row, TAKEN / 2, None, ALU.is_gt).then_inc(row_masked, 1)
            dve.wait_ge(slg_t, 1)
            dve.wait_ge(mask_copied, 3)
            for a in range(2):
                mark(V.scalar_tensor_tensor(out=SS[:, 512 * a:512 * a + 512], in0=ps[2 + a][:, :], scalar=0.125,
                                            in1=bSS[:, 512 * a:512 * a + 512], op0=ALU.mult, op1=ALU.add))
            link(V.scalar_tensor_tensor(out=SS[:, 1024:1032], in0=ps[6][:, 256:264], scalar=0.125,
                                        in1=bSS[:, 1024:1032], op0=ALU.mult, op1=ALU.add))
            link(V.reduce_max(st8[:, 2:3], SS, AX))
            V.tensor_scalar(st8[:, 0:1], st8[:, 2:3], -1.0, None, ALU.mult).then_inc(smax_done, 1)
            dve.wait_ge(sexp_done, 1)
            link(V.reciprocal(st8[:, 3:4], st8[:, 1:2]))
            V.tensor_scalar(SS, SS, st8[:, 3:4], None, ALU.mult).then_inc(sprob_done, 1)
            dve.wait_ge(v_used, TS)
            for j in range(2):
                o = ps[4][:, 64 * j:64 * j + 64].rearrange("p (b x) -> p x b", b=8)
                V.tensor_copy(yT[lo, 4 * j:4 * j + 4, TP:T], o[lo, 0:4])
                ins = V.tensor_copy(yT[hi, 4 * j:4 * j + 4, TP:T], o[hi, 4:8])
            ins.then_inc(so_done, 1)
            residual(KD)
            norm(KD, rT)

            dve.wait_ge(route_done, 3)
            V.tensor_copy(lgr[:, 0:2, :], ps[6][:, 0:16].rearrange("p (t e) -> p t e", t=2))
            link(V.tensor_copy(lgr[0:8, 2, :], ps[6][0:8, 16:24]))
            for t in range(3):
                mark(V.max(out=top[:, t, :], in_=lgr[:, t, :]))
            dve.wait_ge(dchain, chain.k)
            V.tensor_tensor(gate[:, 0, :], top[:, :, 1], top[:, :, 0], ALU.subtract).then_inc(route_in, 1)
            for t in range(3):
                mark(V.max_index(mxi[:, t, :], top[:, t, :], lgr[:, t, :]))
            dve.wait_ge(dchain, chain.k)
            link(V.tensor_copy(topi[:], mxi[:]))
            wide = lambda a: a.unsqueeze(2).to_broadcast([P, 3, 8])
            io = iota8[:].unsqueeze(1).to_broadcast([P, 3, 8])
            for k in range(2):
                mark(V.tensor_tensor(choice[:, k], io, wide(topi[:, :, k]), ALU.is_equal))
            dve.wait_ge(dchain, chain.k)
            V.tensor_tensor(choice[:, 2], choice[:, 0], choice[:, 1], ALU.add).then_inc(chosen, 1)
            dve.wait_ge(gate_e, 1)
            link(V.tensor_scalar(gate[:, 2, :], gate[:, 1, :], 1.0, None, ALU.add))
            link(V.reciprocal(gate[:, 2, :], gate[:, 2, :]))
            link(V.tensor_tensor(gate[:, 3, :], gate[:, 2, :], gate[:, 1, :], ALU.mult))
            mark(V.tensor_tensor(tmp8[:], choice[:, 0], wide(gate[:, 2, :]), ALU.mult))
            link(V.tensor_tensor(tmp8b[:], choice[:, 1], wide(gate[:, 3, :]), ALU.mult))
            mark(V.tensor_tensor(tg[:, :, :, 1], tmp8[:], tmp8b[:], ALU.add))
            dve.wait_ge(counted, 1)
            mark(V.scalar_tensor_tensor(out=place[:, 0:2, :], in0=ps[7][:, 0:16].rearrange("p (t e) -> p t e", t=2),
                                        scalar=1.0, in1=choice[:, 2, 0:2, :], op0=ALU.add, op1=ALU.mult))
            mark(V.scalar_tensor_tensor(out=place[0:8, 2, :], in0=ps[7][0:8, 16:24],
                                        scalar=1.0, in1=choice[0:8, 2, 2, :], op0=ALU.add, op1=ALU.mult))
            link(V.reduce_max(cnt[:, 0:1], ps[7][:, 24:32], AX))

            def sel_round(r):
                if r:
                    dve.wait_ge(sel_done, r)
                for t in range(3):
                    m = P if t < 2 else 8
                    V.tensor_tensor(sel[0:m, t], iotac[0:m, CAP * r:CAP * r + CAP].unsqueeze(1).to_broadcast([m, NE, CAP]),
                                    place[0:m, t, :].unsqueeze(2).to_broadcast([m, NE, CAP]),
                                    ALU.is_equal).then_inc(sel_ready, 1)

            def places(r):
                dve.wait_ge(sel_done, r + 1)
                link(V.tensor_copy(tokg[0:CAP, NE * r:NE * r + NE, :],
                                   ps[(6, 7, 6)[r]][0:CAP, 0:2 * NE].rearrange("p (e a) -> p e a", a=2)))

            def current(i):
                V.tensor_copy(curi[0:CAP, :], tokg[0:CAP, bass.ds(i, 1), 0]).then_inc(cur_ready, 1)

            sel_round(0)
            mark(V.tensor_scalar(cnt[:, 1:2], cnt[:, 0:1], float(CAP), float(NE), ALU.is_gt, ALU.mult))
            link(V.tensor_scalar(cnt[:, 2:3], cnt[:, 0:1], 2.0 * CAP, float(NE), ALU.is_gt, ALU.mult))
            link(V.scalar_tensor_tensor(out=cnt[:, 3:4], in0=cnt[:, 1:2], scalar=float(NE), in1=cnt[:, 2:3],
                                        op0=ALU.add, op1=ALU.add))
            V.tensor_copy(npass[:], cnt[0:1, 3:4]).then_inc(passes_ready, 1)
            places(0)
            current(0)
            sel_round(1)
            places(1)
            sel_round(2)
            places(2)
            over = float(NE * CAP - CAP)
            mark(V.tensor_scalar(tmp8[:], place[:], CAP + 1.0, over, ALU.is_ge, ALU.mult))
            link(V.tensor_scalar(tmp8b[:], place[:], 2.0 * CAP + 1.0, over, ALU.is_ge, ALU.mult))
            link(V.tensor_tensor(tmp8[:], tmp8[:], tmp8b[:], ALU.add))
            link(V.scalar_tensor_tensor(out=tmp8[:], in0=place[:], scalar=-1.0, in1=tmp8[:], op0=ALU.add, op1=ALU.add))
            link(V.scalar_tensor_tensor(out=tmp8[:], in0=io, scalar=float(CAP), in1=tmp8[:], op0=ALU.mult, op1=ALU.add))
            for k in range(2):
                link(V.tensor_tensor(tmp8b[:], tmp8[:], choice[:, k], ALU.mult))
                link(V.tensor_reduce(out=rowf[:, k, :], in_=tmp8b[:], axis=AX, op=ALU.add))
                ins = V.tensor_copy(rowk[:, :, k], rowf[:, k, :])
            ins.then_inc(rowk_ready, 1)

            def gathered():
                for a in range(2):
                    free.inc(V.tensor_copy(xgT[:, 4 * a:4 * a + 4, :],
                                           filled()[:, 0:4 * CAP].rearrange("p (c s) -> p c s", c=4)))

            gathered()
            dve.wait_ge(group_free, free.k)
            n = dve.value_load(npass[0:1, 0:1], min_val=NE, max_val=ROUNDS * NE)
            with dve.Fori(0, n) as i:
                free.enter(i, G_EXP)
                silus.enter(i, KD)
                chain.enter(i, 1)
                link(V.tensor_copy(curg[0:CAP, :], tokg[0:CAP, bass.ds(i, 1), :].rearrange("p a b -> p (a b)")))
                current(i + 1)
                for m in range(KD):
                    silus.k += 1
                    dve.wait_ge(silu_done, silus.base + silus.k)
                    free.inc(V.tensor_tensor(hg[:, m, :], silug[:, m % 2, :],
                                             filled()[:, CAP:2 * CAP], ALU.mult))
                gathered()
                dve.wait_ge(rows_stored, 32 + 16 * i)
                for a in range(2):
                    b = filled()
                    free.inc(V.tensor_scalar(orow[:, 512 * a:512 * a + 512], b[0:CAP, :], curg[0:CAP, 1:2], None,
                                             ALU.mult))
                dve.wait_ge(group_free, free.base + free.k)
                chain.leave(n)
                silus.leave(n)
                free.leave(n)

            tail = Count(tchain)
            then = lambda ins: dve.wait_ge(tchain, tail.inc(ins))
            dve.wait_ge(gb_in, 32)
            for t in range(3):
                m = P if t < 2 else 8
                a, b = res[0:m, t, 0, :], res[0:m, t, 1, :]
                dve.wait_ge(res_in[t], 32)
                then(V.scalar_tensor_tensor(out=a, in0=xrow[0:m, t, :], scalar=ALPHA, in1=a, op0=ALU.mult, op1=ALU.add))
                then(V.tensor_tensor(a, a, b, ALU.add))
                for h in range(2):
                    ins = V.bn_stats(fin[0:m, t, 6 * h:6 * h + 6], a[:, 512 * h:512 * h + 512])
                then(ins)
                ins = V.bn_aggr(fin[0:m, t, 12:14], fin[0:m, t, 0:12])
            ins.then_inc(fvar, 1)
            dve.wait_ge(fstd, 1)
            then(V.reciprocal(fin[:, :, 15], fin[:, :, 14]))
            for t in range(3):
                m = P if t < 2 else 8
                a = res[0:m, t, 0, :]
                then(V.tensor_scalar(a, a, fin[0:m, t, 12:13], fin[0:m, t, 15:16], ALU.subtract, ALU.mult))
                then(V.tensor_tensor(a, a, cache[0:m, 0:D], ALU.mult))
                V.tensor_tensor(a, a, cache[0:m, D:2 * D], ALU.add).then_inc(final_ready, 1)


def constants():
    square = np.zeros((5, P, P), np.float32)
    square[0] = np.eye(P)
    for h in (0, 64):
        for i in range(8):
            square[1, h + i + 8, h + i] = -1.0
            square[1, h + i, h + i + 8] = 1.0
    square[2] = np.roll(np.eye(P), 64, axis=0)
    square[3] = np.triu(np.ones((P, P)), 1)
    square[4] = 1.0
    inv = np.float32(500000.0) ** (-np.arange(8, dtype=np.float32) / np.float32(8))
    pos = np.concatenate([np.arange(TP), np.full(TS, PAST)]).astype(np.float32)
    ang = (pos[:, None] * inv[None, :].astype(np.float32)).astype(np.float32)
    rope = np.zeros((2, P, T), np.float32)
    rope[0] = 1.0
    for h in (0, 64):
        for i in range(16):
            rope[0, h + i] = np.cos(ang[:, i % 8].astype(np.float64))
            rope[1, h + i] = np.sin(ang[:, i % 8].astype(np.float64))
    pick = np.zeros((9, P), np.float32)
    pick[np.arange(P) // 16, np.arange(P)] = 1.0
    pick[8] = np.arange(P) % (PAGE // RUN)
    return {"c_square": square, "c_rope": rope, "c_pick": pick}


INPUTS = ["x_prompt", "x_sample", "cache_k", "cache_v", "cache_kidx", "state_conv", "page_table",
          "ln1_g", "ln1_b", "ln2_g", "ln2_b", "w_in_even", "conv_w", "sgu_ln_g", "sgu_ln_b", "sgu_w", "sgu_b",
          "w_out_even", "ffn_w1", "ffn_w3", "ffn_w2", "w_in_odd", "w_out_odd", "router_w", "router_b",
          "moe_w1", "moe_w3", "moe_w2"]
OUTPUTS = [(1, TP, D), (TS, 1, D), (1, 1, TP, 4, 64), (1, 1, TP, 4, 64), (1, 1, TP, 64), (1, 1, 2, CH),
           (1, TS, 1, 4, 64), (1, TS, 1, 4, 64), (1, TS, 1, 64), (1, TS, 2, CH), (1, TS, 1, CH)]


def kernel(**inputs):
    import concourse.bacc as bacc
    from concourse.bass_utils import run_bass_kernel_spmd

    nc = bacc.Bacc("TRN2", target_bir_lowering=False, num_devices=1)
    arrays = {name: np.ascontiguousarray(inputs[name]) for name in INPUTS}
    arrays.update(constants())
    args = [nc.dram_tensor(name, a.shape, mybir.dt.from_np(a.dtype), kind="ExternalInput").ap()
            for name, a in arrays.items()]
    scratch = [nc.dram_tensor(name, shape, F32, kind="Internal").ap()
               for name, shape in (("x_rows", (T, D)), ("r_rows", (ROUNDS * NE * CAP, D)))]
    args += scratch
    args += [nc.dram_tensor(f"out_{i}", shape, F32, kind="ExternalOutput").ap() for i, shape in enumerate(OUTPUTS)]
    build(nc, *args)
    got = run_bass_kernel_spmd(nc, [arrays], core_ids=[0])
    return tuple(got.results[0][f"out_{i}"] for i in range(len(OUTPUTS)))
```

```python
from contextlib import ExitStack

import numpy as np

import concourse.bass as bass
from concourse import mybir

F32 = mybir.dt.float32
I32 = mybir.dt.int32
U32 = mybir.dt.uint32
ALU = mybir.AluOpType
ACT = mybir.ActivationFunctionType
AX = mybir.AxisListType.X

P = 128
D = 1024
KD = D // P
TP, TS = 256, 8
T = TP + TS
CH = 512
FF = 2816
KF = FF // P
NE = 8
CAP = 104
ROUNDS = -(-(TP + TS) // CAP)
TILES = [[t for t in range(3) if min(P * t + P, TP + TS) > CAP * r] for r in range(ROUNDS)]
SELS = [sum(len(x) for x in TILES[:r]) for r in range(ROUNDS)]
PAST, PAGE = 1024, 128
NPOOL = 80
NPG = PAST // PAGE
RUN = 8
TOPK_P, TOPK_S = 64, 256
ALPHA = 4.0 ** 0.25
EPS = 1e-5
NEG = -1e30
TAKEN = -3e38
NSLOT = 6
NB = 4

V_LN1G, V_LN1B, V_LN2G, V_LN2B, V_SG, V_SB, V_CW, NVEC = 0, 16, 32, 48, 64, 68, 72, 84
QI, KI, KK, VV, QQ = 0, 4, 5, 7, 9
ROPED = [QI, QI + 1, QI + 2, QI + 3, KI, KK, KK + 1] + [QQ + c for c in range(KD)]


class Count:

    def __init__(self, sem):
        self.sem, self.base, self.k, self.phase = sem, 0, 0, 0

    def inc(self, ins, by=1):
        ins.then_inc(self.sem, by)
        self.k += by
        return self.base + self.k

    def enter(self, i, per):
        self.start, self.per = self.base + self.k, per
        self.base, self.k, self.phase = self.start + i * per, 0, self.start

    def leave(self, n):
        assert self.k == self.per, (self.k, self.per)
        self.base, self.k = 0, self.start + n * self.per
        self.phase = 0


def build(nc, x_prompt, x_sample, cache_k, cache_v, cache_kidx, state_conv, page_table,
          ln1_g, ln1_b, ln2_g, ln2_b, w_in_even, conv_w, sgu_ln_g, sgu_ln_b, sgu_w, sgu_b,
          w_out_even, ffn_w1, ffn_w3, ffn_w2, w_in_odd, w_out_odd, router_w, router_b,
          moe_w1, moe_w3, moe_w2, c_square, c_rope, c_pick, c_heads, x_rows, r_rows,
          y_p, y_s, k_p, v_p, ki_p, conv_p, k_s, v_s, ki_s, conv_s, chunk_s):
    ctx = ExitStack()
    with ctx:
        ctx.enter_context(nc.allow_non_contiguous_dma(reason="small tables and packed vectors"))

        def sb(name, shape, dt=F32):
            return ctx.enter_context(nc.sbuf_tensor(name, shape, dt))

        def sem(name):
            return ctx.enter_context(nc.semaphore(name))

        slot = [sb(f"slot{i}", [P, 4096]) for i in range(NSLOT)]
        xT = sb("xT", [P, KD, T])
        rT = sb("rT", [P, KD, T])
        sqT = sb("sqT", [P, KD, T])
        hT = sb("hT", [P, KF, T])
        yT = sb("yT", [P, KD, T])
        scr = sb("scr", [P, 6144])
        cache = sb("cache", [P, 2048])
        kbuf = [cache[:, 0:1024], hT[:, 17:21, :].rearrange("p c t -> p (c t)")[:, 0:1024]]
        kibuf = [cache[:, 1024 + 512 * i:1536 + 512 * i] for i in range(2)]
        square = sb("square", [P, 5, P])
        rope = sb("rope", [P, 2, T])
        pick = sb("pick", [8, P])
        ones = sb("ones", [P, P])
        one8 = sb("one8", [8, P])
        vecraw = sb("vecraw", [NVEC, P])
        vec = sb("vec", [P, NVEC])
        mean = sb("mean", [P, T])
        var = sb("var", [P, T])
        rstd = sb("rstd", [P, T])
        silu = sb("silu", [P, 2, T])
        eps = sb("eps", [P, 1])
        w00 = sb("w00", [P, 2, 4])
        idx = sb("idx", [P, 3, NPG], I32)
        idxf = sb("idxf", [P, NPG])
        sg = sb("sg", [P, 1])
        wrt = sb("wrt", [P, KD, NE])
        wrb = sb("wrb", [1, NE])
        ktv = sb("ktv", [P, 2, 512])
        kvs = sb("kvs", [8, 512])
        kit = sb("kit", [P, 3, 64])
        wit = sb("wit", [P, 2, 8])
        wiT = sb("wiT", [8, T])
        stat = sb("stat", [P, 24])
        qiB = sb("qiB", [P, 8, 16])
        lgr = sb("lgr", [P, 3, 8])
        top = sb("top", [P, 3, 8])
        mxi = sb("mxi", [P, 3, 8], U32)
        topi = sb("topi", [P, 3, 8])
        gate = sb("gate", [P, 4, 3])
        choice = sb("choice", [P, 3, 3, 8])
        place = sb("place", [P, 3, 8])
        tg = sb("tg", [P, 3, 8, 2])
        rowk = sb("rowk", [P, 3, 2], I32)
        tmp8 = sb("tmp8", [P, 3, 8])
        tmp8b = sb("tmp8b", [P, 3, 8])
        rowf = sb("rowf", [P, 2, 3])
        cnt = sb("cnt", [P, 4])
        npass = sb("npass", [1, 1], I32)
        iota8 = sb("iota8", [P, 8])
        iotac = sb("iotac", [P, ROUNDS * CAP])
        tokg = sb("tokg", [P, ROUNDS * NE + 1, 2])
        curi = sb("curi", [P, 1], I32)
        curg = sb("curg", [P, 2])
        fin = sb("fin", [P, 3, 16])
        mx8p = sb("mx8p", [P, 8])

        ident = square[:, 0, :]
        rot = square[:, 1, :]
        swap = square[:, 2, :]
        before = square[:, 3, :]
        all1 = square[:, 4, :]

        ps = [ctx.enter_context(nc.psum_tensor(f"ps{i}", [P, 512], F32)) for i in range(8)]

        xtok = scr[:, 0:2048].rearrange("p (t d) -> p t d", t=2)
        xstok = scr[0:8, 2048:3072]
        zext = scr[:, 0:4 * 258].rearrange("p (c t) -> p c t", c=4)
        vtok = scr[:, 1040:2064].rearrange("p (t c) -> p t c", t=2)
        wsT = scr[:, 3072:3584].rearrange("p (g i) -> p g i", g=4)
        wsr = scr[:, 3584:4096].rearrange("p (g j) -> p g j", g=4)
        stT = scr[:, 4096:4160].rearrange("p (c n) -> p c n", c=4)
        str_ = scr[0:16, 4160:4672]
        zlast = scr[:, 4672:4712].rearrange("p (c n) -> p c n", c=4)
        zrow = scr[0:10, 4736:5248]
        vrow = scr[0:8, 5248:5760]
        sgb = scr[0:1, 5248:5760]
        cst = scr[:, 5760:5760 + 256]
        css = scr[:, 6016:6024]
        rel = [scr[:, 512 * i:512 * i + 512].rearrange("p (h s) -> p h s", h=2) for i in range(2)]
        sc = scr[:, 1024:1536].rearrange("p (t s) -> p t s", t=2)
        work = scr[:, 1536:2048].rearrange("p (t s) -> p t s", t=2)
        S = [scr[:, 2048 + 1024 * i:3072 + 1024 * i].rearrange("p (u h s) -> p u h s", u=2, h=2) for i in range(2)]
        PT = [scr[:, 4096 + 1024 * i:5120 + 1024 * i] for i in range(2)]
        kiT = [slot[2][:, 512 * i:512 * i + 512] for i in range(2)]
        srel = slot[2][:, 1024:1600]
        wib = slot[2][:, 1600:1664]
        dwi = slot[2][0:8, 1664:1728]
        score = slot[2][:, 1728:1792].rearrange("p (b r) -> p b r", b=8)
        sc9 = slot[2][0:8, 1792:1800]
        row = slot[2][0:8, 1808:2840]
        mx8 = slot[2][0:8, 2840:2848]
        st8 = slot[2][:, 2848:2864]
        heads = slot[2][0:16, 2864:3124]
        qwide = slot[3][:, 0:2048]
        qfull = mean[:, 0:256].rearrange("p (j q) -> p j q", j=2)
        KT = [slot[3][:, 2048 + 1024 * i:3072 + 1024 * i].rearrange("p (j s) -> p j s", j=2) for i in range(2)]
        SS = slot[3][:, 2048:2048 + 1032]
        PTs = slot[3][:, 0:1152].rearrange("p (r q) -> p r q", r=9)
        om = [slot[3][0:16, 1152 + 256 * i:1408 + 256 * i] for i in range(2)]
        flat = lambda a: a[:].rearrange("p c t -> p (c t)")
        xrow = flat(hT)[:, 0:3072].rearrange("p (t d) -> p t d", t=3)
        hg = flat(hT)[:, 3072:3072 + KD * CAP].rearrange("p (c s) -> p c s", c=KD)
        xgT = flat(hT)[:, 4000:4000 + KD * CAP].rearrange("p (c s) -> p c s", c=KD)
        xg = flat(rT)[0:CAP, 0:D]
        orow = flat(yT)[0:CAP, 0:D]
        sel = scr[:, 0:3 * NE * CAP].rearrange("p (t e s) -> p t e s", t=3, e=NE)
        res = scr[:, :].rearrange("p (t k d) -> p t k d", t=3, k=2)
        silug = silu[:].rearrange("p a t -> p (a t)")[:, 0:2 * CAP].rearrange("p (a s) -> p a s", a=2)

        def slab(s, k, n):
            return slot[s][:, 0:k * n].rearrange("p (k n) -> p k n", k=k)

        consts_in, x_in, even_in, idx_in = sem("consts_in"), sem("x_in"), sem("even_in"), sem("idx_in")
        slab_in = [sem(f"slab_in{s}") for s in range(NSLOT)]
        pool_consts, causal_w = sem("pool_consts"), sem("causal_w")
        group_done = sem("group_done")
        group_free = sem("group_free")
        silu_done = sem("silu_done")
        even_t, even_tc = sem("even_t"), sem("even_tc")
        sq_done = sem("sq_done")
        stats_done, var_done, std_done = sem("stats_done"), sem("var_done"), sem("std_done")
        centred, x_ready = sem("centred"), sem("x_ready")
        vt_done, vt_copied = sem("vt_done"), sem("vt_copied")
        z_done, z_t, z_copied = sem("z_done"), sem("z_t"), sem("z_copied")
        rot_done, roped = sem("rot_done"), sem("roped")
        tok_t, tok_copied = sem("tok_t"), sem("tok_copied")
        dots_done, rel_done, rel_used = sem("dots_done"), sem("rel_done"), sem("rel_used")
        sc_causal, bias_done, bias_causal = sem("sc_causal"), sem("bias_done"), sem("bias_causal")
        lg_done, lg_read, exp_done, prob_done = sem("lg_done"), sem("lg_read"), sem("exp_done"), sem("prob_done")
        pt_done, pt_copied, o_done, o_copied = sem("pt_done"), sem("pt_copied"), sem("o_done"), sem("o_copied")
        idx_done = sem("idx_done")
        ki_in = [sem(f"ki_in{i}") for i in range(2)]
        ki_mm, k_mm = sem("ki_mm"), sem("k_mm")
        ki_t, ki_copied, qi_ready, swapped = sem("ki_t"), sem("ki_copied"), sem("qi_ready"), sem("swapped")
        wib_in, wib_done, sdots, srel_done = sem("wib_in"), sem("wib_done"), sem("sdots"), sem("srel_done")
        score_done, new_masked, row_t, row_done = sem("score_done"), sem("new_masked"), sem("row_t"), sem("row_done")
        row_masked, mask_wide = sem("row_masked"), sem("mask_wide")
        k_in = [sem(f"k_in{i}") for i in range(2)]
        v_in = [sem(f"v_in{i}") for i in range(2)]
        qbd_done, k_t, k_copied = sem("qbd_done"), sem("k_t"), sem("k_copied")
        slg_done, slg_copied, heads_in = sem("slg_done"), sem("slg_copied"), sem("heads_in")
        sv_done, om_done, so_t = sem("sv_done"), sem("om_done"), sem("so_t")
        smax_done, sexp_done, sprob_done = sem("smax_done"), sem("sexp_done"), sem("sprob_done")
        spt_done, spt_copied, v_used, so_done = sem("spt_done"), sem("spt_copied"), sem("v_used"), sem("so_done")
        route_in, route_done, gate_e = sem("route_in"), sem("route_done"), sem("gate_e")
        xt_t, xt_copied, rows_stored = sem("xt_t"), sem("xt_copied"), sem("rows_stored")
        gathers_due, tokg_done = sem("gathers_due"), sem("tokg_done")
        chosen, counted, passes_ready = sem("chosen"), sem("counted"), sem("passes_ready")
        sel_ready, sel_done, cur_ready = sem("sel_ready"), sem("sel_done"), sem("cur_ready")
        xg_in, rowk_ready, gb_in = sem("xg_in"), sem("rowk_ready"), sem("gb_in")
        res_in = [sem(f"res_in{t}") for t in range(3)]
        zeros_ready, rows_cleared = sem("zeros_ready"), sem("rows_cleared")
        fvar, fstd, final_ready = sem("fvar"), sem("fstd"), sem("final_ready")
        even_stored, state_stored, kv_stored, y_stored = (
            sem("even_stored"), sem("state_stored"), sem("kv_stored"), sem("y_stored"))
        dchain, tchain = sem("dchain"), sem("tchain")

        block = ctx.enter_context(nc.Block())

        S_EIN, S_EOUT, S_UP, S_UPLAST = (0, 1, 2, 3, 4), (5, 0), (1, 2, 3, 4, 5), 0
        S_DOWN, S_OIN, S_OOUT = (1, 2, 3, 4), (5, 0, 1, 2, 3), (4, 5)
        EIN_ORDER = (4, 1, 2, 3, 0)
        G_EIN = KD
        G_MIX = G_EIN + 20
        G_EOUT = G_MIX + 4
        G_UP = G_EOUT + KD
        G_DOWN = G_UP + 2 * KF
        G_OIN = G_DOWN + KD
        G_OOUT = G_OIN + 18
        G_XG = G_OOUT + KD
        G_MOE = G_XG + 2
        G_EXP = KD + 2 + 2

        kdim = "(k p) n -> p k n"

        def up_views(s):
            v = slot[s][:, :].rearrange("p (w k n) -> p w k n", w=2, k=KD)
            return v[:, 0], v[:, 1]

        @block.sync
        def _(sp):
            last = [None] * NSLOT

            def slot_free(s, value):
                if last[s] is not None:
                    sp.wait_ge(group_done, last[s])
                last[s] = value

            def load(s, dst, src):
                sp.dma_start(dst, src).then_inc(slab_in[s], 16)

            sp.dma_start(xtok, x_prompt[0].rearrange("(t p) d -> p t d", p=P)).then_inc(x_in, 16)
            sp.dma_start(xstok, x_sample[:, 0, :]).then_inc(x_in, 16)
            sp.dma_start(square[:], c_square.rearrange("a p q -> p a q")).then_inc(consts_in, 16)
            w = w_in_even[0].rearrange(kdim, p=P)
            for n, (s, c) in enumerate(zip(S_EIN, EIN_ORDER)):
                slot_free(s, G_EIN + 4 * (n + 1))
                load(s, slab(s, KD, 512), w[:, :, 512 * c:512 * c + 512])
            w = w_out_even[0].rearrange(kdim, p=P)
            for c, s in enumerate(S_EOUT):
                slot_free(s, G_EOUT + 4 * (c + 1))
                load(s, slab(s, KD, 512), w[:, :, 512 * c:512 * c + 512])
            w1, w3 = (w[0].rearrange(kdim, p=P) for w in (ffn_w1, ffn_w3))
            before = [last[s] for s in S_UP]
            with sp.Fori(0, 2) as i:
                for n, s in enumerate(S_UP):
                    sp.wait_ge(group_done, before[n] + i * (G_UP + 4 * (n + 1) - before[n]))
                    a, b = up_views(s)
                    load(s, a, w1[:, :, bass.ds(i * 1280 + n * 256, 256)])
                    load(s, b, w3[:, :, bass.ds(i * 1280 + n * 256, 256)])
            for n, s in enumerate(S_UP):
                last[s] = G_UP + 20 + 4 * (n + 1)
            slot_free(S_UPLAST, G_DOWN)
            a, b = up_views(S_UPLAST)
            load(S_UPLAST, a, w1[:, :, 2560:2816])
            load(S_UPLAST, b, w3[:, :, 2560:2816])
            w2 = ffn_w2[0].rearrange("(u k p) n -> p u k n", p=P, u=2)
            before = [last[s] for s in S_DOWN]
            with sp.Fori(0, 2) as i:
                for n, s in enumerate(S_DOWN):
                    sp.wait_ge(group_done, before[n] + i * (G_DOWN + 2 * (n // 2 + 1) - before[n]))
                    load(s, slab(s, 11, 256), w2[:, n % 2, :, bass.ds(i * 512 + (n // 2) * 256, 256)])
            for n, s in enumerate(S_DOWN):
                last[s] = G_DOWN + 4 + 2 * (n // 2 + 1)
            w = w_in_odd[0].rearrange(kdim, p=P)
            slot_free(S_OIN[0], G_OIN + 4)
            load(S_OIN[0], slab(S_OIN[0], KD, 512), w[:, :, 1536:2048])
            slot_free(S_OIN[1], G_OIN + 6)
            v = slab(S_OIN[1], KD, 136)
            load(S_OIN[1], v[:, :, 0:64], w[:, :, 2048:2112])
            load(S_OIN[1], v[:, :, 64:136], w[:, :, 2048:2120])
            slot_free(S_OIN[2], G_OIN + 10)
            load(S_OIN[2], slab(S_OIN[2], KD, 512), w[:, :, 1024:1536])
            for c in range(2):
                slot_free(S_OIN[3 + c], G_OIN + 14 + 4 * c)
                v = slab(S_OIN[3 + c], KD, 512)
                for i in range(4):
                    for a in range(2):
                        src = 512 * c + 256 * a + 64 * i
                        load(S_OIN[3 + c], v[:, :, P * i + 64 * a:P * i + 64 * a + 64], w[:, :, src:src + 64])
            for c, s in enumerate(S_OOUT):
                slot_free(s, G_OOUT + 4 * (c + 1))
                for half in range(2):
                    v = slab(s, KD, 512)[64 * half:64 * half + 64]
                    for j in range(2):
                        src = w_out_odd[0, 512 * j + 256 * half:512 * j + 256 * half + 256, 512 * c:512 * c + 512]
                        load(s, v[:, 4 * j:4 * j + 4, :], src.rearrange("(i d) n -> d i n", d=64))

            def load_expert(s, e):
                if s < 4:
                    for v, w in zip(up_views(s), (moe_w1[0], moe_w3[0])):
                        src = w[bass.ds(e, 1), :, 256 * s:256 * s + 256]
                        load(s, v, src.rearrange("e (k p) n -> p (e k) n", p=P))
                else:
                    src = moe_w2[0][bass.ds(e, 1), :, 512 * (s - 4):512 * (s - 4) + 512]
                    load(s, slab(s, KD, 512), src.rearrange("e (k p) n -> p (e k) n", p=P))

            sp.wait_ge(z_copied, 2)
            sp.dma_start(conv_p[0, 0], zrow[0:2, :]).then_inc(even_stored, 16)
            sp.dma_start(conv_s[0, :, 1, :], zrow[2:10, :]).then_inc(even_stored, 16)
            sp.dma_start(chunk_s[0, :, 0, :], vrow).then_inc(even_stored, 16)
            for s in range(2):
                slot_free(s, None)
                load_expert(s, 0)
            sp.wait_ge(group_done, G_OIN + 18)
            sp.dma_start(heads, c_heads[:, :]).then_inc(heads_in, 16)
            sp.wait_ge(tok_copied, 5)
            kv = lambda a: a[0, 0].rearrange("(t p) h d -> p t (h d)", p=P)
            sp.dma_start(kv(k_p), ktv[:, :, 0:256]).then_inc(kv_stored, 16)
            sp.dma_start(kv(v_p), ktv[:, :, 256:512]).then_inc(kv_stored, 16)
            sp.dma_start(ki_p[0, 0].rearrange("(t p) d -> p t d", p=P), kit[:, 0:2, :]).then_inc(kv_stored, 16)
            sp.dma_start(k_s[0, :, 0].rearrange("b h d -> b (h d)"), kvs[:, 0:256]).then_inc(kv_stored, 16)
            sp.dma_start(v_s[0, :, 0].rearrange("b h d -> b (h d)"), kvs[:, 256:512]).then_inc(kv_stored, 16)
            sp.dma_start(ki_s[0, :, 0], kit[0:8, 2, :]).then_inc(kv_stored, 16)
            sp.wait_ge(so_done, 1)
            for s in (2, 3):
                load_expert(s, 0)
            for s in (4, 5):
                slot_free(s, None)
                load_expert(s, 0)
            sp.wait_ge(passes_ready, 1)
            n = sp.value_load(npass[0:1, 0:1], min_val=NE, max_val=ROUNDS * NE)
            with sp.Fori(1, n) as i:
                for s in range(NSLOT):
                    sp.wait_ge(group_done, G_MOE + (i - 1) * G_EXP + (2 * (s + 1) if s < 4 else KD + 2 + s - 3))
                    load_expert(s, i % NE)
            for t in range(3):
                sp.wait_ge(final_ready, t + 1)
                if t < 2:
                    sp.dma_start(y_p[0, P * t:P * t + P, :], res[:, t, 0, :]).then_inc(y_stored, 16)
                else:
                    sp.dma_start(y_s[:, 0, :], res[0:8, t, 0, :]).then_inc(y_stored, 16)
            for stored, n in ((even_stored, 3), (state_stored, 1), (kv_stored, 6), (y_stored, 3)):
                sp.wait_ge(stored, 16 * n)

        @block.gpsimd
        def _(pool):
            pool.memset(ones[:], 1.0 / D).then_inc(pool_consts, 1)
            pool.memset(one8[:], 1.0).then_inc(pool_consts, 1)
            pool.iota(iota8[:], pattern=[[1, 8]], base=0, channel_multiplier=0,
                      allow_small_or_imprecise_dtypes=True).then_inc(pool_consts, 1)
            pool.iota(iotac[:], pattern=[[1, ROUNDS * CAP]], base=1, channel_multiplier=0,
                      allow_small_or_imprecise_dtypes=True).then_inc(pool_consts, 1)
            for t in range(3):
                pool.iota(tg[:, t, :, 0], pattern=[[0, 8]], base=P * t, channel_multiplier=1,
                          allow_small_or_imprecise_dtypes=True).then_inc(pool_consts, 1)
            pool.memset(eps[:], EPS).then_inc(pool_consts, 1)
            n = 0
            for dst, src in ((vecraw[0:16], ln1_g.rearrange("l (c p) -> (l c) p", p=P)),
                             (vecraw[16:32], ln1_b.rearrange("l (c p) -> (l c) p", p=P)),
                             (vecraw[32:48], ln2_g.rearrange("l (c p) -> (l c) p", p=P)),
                             (vecraw[48:64], ln2_b.rearrange("l (c p) -> (l c) p", p=P)),
                             (vecraw[64:68], sgu_ln_g.rearrange("l (c p) -> (l c) p", p=P)),
                             (vecraw[68:72], sgu_ln_b.rearrange("l (c p) -> (l c) p", p=P)),
                             (vecraw[72:84], conv_w[0].rearrange("w (c p) -> (w c) p", p=P)),
                             (wsr, sgu_w[0].rearrange("g i j -> i g j")),
                             (sgb, sgu_b.rearrange("l g i -> l (g i)")),
                             (str_, state_conv[0].rearrange("b w c -> (b w) c")),
                             (w00[:, 0, :], sgu_w[0, :, 0, 0:1].rearrange("g a -> a g").to_broadcast([P, 4])),
                             (w00[:, 1, :], sgu_b[0, :, 0:1].rearrange("g a -> a g").to_broadcast([P, 4]))):
                pool.dma_start(dst, src).then_inc(even_in, 16)
                n += 1
            assert n == 12
            pool.dma_start(rope[:], c_rope.rearrange("a p t -> p a t")).then_inc(idx_in, 16)
            pool.dma_start(pick[:], c_pick[0:8, :]).then_inc(idx_in, 16)
            pool.dma_start(sg[:], c_pick[8:9, :].rearrange("a p -> p a")).then_inc(idx_in, 16)
            pool.dma_start(wrt[:], router_w[0].rearrange("(k p) e -> p k e", p=P)).then_inc(idx_in, 16)
            pool.dma_start(wrb[:], router_b).then_inc(idx_in, 16)
            for pg in range(NPG):
                src = page_table[:, pg:pg + 1].rearrange("b a -> a b").to_broadcast([16, TS])
                pool.dma_start(idx[16 * pg:16 * pg + 16, 0, :], src).then_inc(idx_in, 16)
            pool.wait_ge(even_in, 16 * 12)
            pool.affine_select(out=wsr, in_=wsr, pattern=[[0, 4], [-1, P]], compare_op=ALU.is_ge, fill=0.0,
                               base=0, channel_multiplier=1).then_inc(causal_w, 1)
            pool.dma_start(conv_s[0, :, 0, :], str_[1:16:2, :]).then_inc(state_stored, 16)

            pool.wait_ge(idx_done, 1)
            kirows = cache_kidx[0].rearrange("n (r s) d -> (n r) (s d)", s=RUN)
            krows = cache_k[0].rearrange("n (r s) h d -> (n r) (s h d)", s=4)
            vrows = cache_v[0].rearrange("n (r s) h d -> (n r) (s h d)", s=RUN)
            off = lambda a, b: bass.IndirectOffsetOnAxis(ap=idx[:, a, b:b + 1].bitcast(U32), axis=0)

            def gather_ki(b):
                pool.indirect_dma_start(out=kibuf[b % 2], out_offset=None, in_=kirows,
                                        in_offset=off(0, b)).then_inc(ki_in[b % 2], 16)

            def gather_k(u):
                pool.indirect_dma_start(out=kbuf[u % 2], out_offset=None, in_=krows,
                                        in_offset=off(1 + u % 2, u // 2)).then_inc(k_in[u % 2], 16)

            def gather_v(b):
                dst = (rT, sqT)[b % 2][:].rearrange("p c t -> p (c t)")[:, 0:RUN * 256]
                pool.indirect_dma_start(out=dst, out_offset=None, in_=vrows,
                                        in_offset=off(0, b)).then_inc(v_in[b % 2], 16)

            for b in range(2):
                gather_ki(b)
            pool.wait_ge(x_ready, 4 + 2 * KD)
            for u in range(2):
                gather_k(u)
            for b in range(2):
                gather_v(b)
            for t in range(2):
                pool.wait_ge(rel_used, 4 * (t + 1))
                pool.affine_select(out=sc[:, t, 0:P * (t + 1)], in_=sc[:, t, 0:P * (t + 1)], pattern=[[-1, P * (t + 1)]], compare_op=ALU.is_ge,
                                   fill=NEG, base=P * t, channel_multiplier=1).then_inc(sc_causal, 1)
            for b in range(2, TS):
                pool.wait_ge(ki_t, b - 1)
                gather_ki(b)
            for t in range(2):
                pool.wait_ge(bias_done, t + 1)
                pool.affine_select(out=work[:, t, 0:P * (t + 1)], in_=work[:, t, 0:P * (t + 1)], pattern=[[-1, P * (t + 1)]], compare_op=ALU.is_ge,
                                   fill=NEG, base=P * t, channel_multiplier=1).then_inc(bias_causal, 1)
            pool.wait_ge(score_done, 2)
            pool.affine_select(out=sc9, in_=sc9, pattern=[[-1, 8]], compare_op=ALU.is_equal, fill=NEG,
                               base=0, channel_multiplier=1).then_inc(new_masked, 1)
            for u in range(2, 2 * TS):
                pool.wait_ge(k_t, 2 * (u - 1))
                gather_k(u)
            for b in range(2, TS):
                pool.wait_ge(v_used, b - 1)
                gather_v(b)
            for a, v in enumerate((ln2_g, ln2_b)):
                pool.dma_start(cache[:, D * a:D * a + D], v[1:2, :].to_broadcast([P, D])).then_inc(gb_in, 16)

            pool.wait_ge(xt_copied, 6)
            pool.dma_start(x_rows[0:TP, :].rearrange("(t p) d -> p t d", p=P), xrow[:, 0:2, :]).then_inc(rows_stored, 16)
            pool.dma_start(x_rows[TP:T, :], xrow[0:8, 2, :]).then_inc(rows_stored, 16)

            def gather_x(now):
                pool.wait_ge(cur_ready, now)
                pool.sem_inc(gathers_due, 1)
                pool.indirect_dma_start(out=xg, out_offset=None, in_=x_rows,
                                        in_offset=bass.IndirectOffsetOnAxis(ap=curi[0:CAP, 0:1].bitcast(U32), axis=0)
                                        ).then_inc(xg_in, 16)

            pool.wait_ge(rows_cleared, 16)
            pool.wait_ge(rows_stored, 32)
            gather_x(1)
            pool.wait_ge(passes_ready, 1)
            n = pool.value_load(npass[0:1, 0:1], min_val=NE, max_val=ROUNDS * NE)
            with pool.Fori(0, n) as i:
                pool.wait_ge(group_done, G_MOE + (i - 1) * G_EXP + KD + 2)
                gather_x(i + 2)
                pool.wait_ge(group_free, G_MOE + (i + 1) * G_EXP)
                pool.dma_start(r_rows[bass.ds(i * CAP, CAP), :], orow).then_inc(rows_stored, 16)
            pool.wait_ge(rows_stored, 32 + 16 * n)
            pool.sem_inc(gathers_due, 1)
            pool.wait_ge(rowk_ready, 1)
            for t in range(3):
                m = P if t < 2 else 8
                for k in range(2):
                    pool.indirect_dma_start(out=res[0:m, t, k, :], out_offset=None, in_=r_rows,
                                            in_offset=bass.IndirectOffsetOnAxis(
                                                ap=rowk[0:m, t, k:k + 1].bitcast(U32), axis=0)).then_inc(res_in[t], 16)

        @block.tensor
        def _(pe):
            done = Count(group_done)
            loads = [Count(s) for s in slab_in]
            got = [0]

            def arrived(s, by=16):
                loads[s].k += by
                pe.wait_ge(slab_in[s], loads[s].base + loads[s].k)

            def bank():
                g = done.base + done.k
                if done.phase + done.k >= NB:
                    pe.wait_ge(group_free, g - (NB - 1))
                return ps[(done.phase + done.k) % NB]

            def group(lhs, rhs, n, m=P, ready=None):
                out = bank()[0:m, 0:T]
                for k in range(n):
                    if ready:
                        pe.wait_ge(*ready(k))
                    mm = pe.matmul(out, lhs(k), rhs(k), start=(k == 0), stop=(k == n - 1))
                done.inc(mm)

            def stats(c, n, src, sq, ready):
                if c == 0 and got[0]:
                    pe.wait_ge(var_done, got[0])
                pe.wait_ge(*ready)
                squares[0] += 1
                pe.wait_ge(sq_done, squares[0])
                pe.matmul(ps[4][:, 0:T], ones[:], src[:, c, :], start=(c == 0), stop=(c == n - 1))
                mm = pe.matmul(ps[5][:, 0:T], ones[:], sq[:, c, :], start=(c == 0), stop=(c == n - 1))
                if c == n - 1:
                    mm.then_inc(stats_done, 1)
                    got[0] += 1

            squares = [0]

            def proj_with_stats(slots, rhs, g0, by=16):
                for n, s in enumerate(slots):
                    arrived(s, by)
                    for j in range(4):
                        c = 4 * n + j
                        group(lambda k: slab(s, KD, 512)[:, k, P * j:P * j + P], rhs, KD)
                        if c:
                            stats(c - 1, KD, rT, sqT, (group_free, g0 + c))
                stats(KD - 1, KD, rT, sqT, (group_free, g0 + KD))

            x = lambda k: xT[:, k, :]
            y = lambda k: yT[:, k, :]

            pe.wait_ge(consts_in, 16)
            pe.wait_ge(x_in, 32)
            for c in range(KD):
                b = bank()
                for t in range(2):
                    pe.transpose(b[:, P * t:P * t + P], xtok[:, t, P * c:P * c + P], ident)
                done.inc(pe.transpose(b[:, TP:T], xstok[:, P * c:P * c + P], square[0:8, 0, 0:8]))
            pe.wait_ge(group_free, KD)
            for n, s in enumerate(S_EIN):
                arrived(s)
                for j in range(4):
                    group(lambda k: slab(s, KD, 512)[:, k, P * j:P * j + P], x, KD)
                if n == 1:
                    pe.wait_ge(even_in, 16 * 12)
                    pe.wait_ge(causal_w, 1)
                    pe.wait_ge(pool_consts, 8)
                    pe.transpose(ps[6][:, 0:NVEC], vecraw[:], square[0:NVEC, 0, 0:NVEC])
                    for c in range(4):
                        mm = pe.transpose(ps[6][:, 128 + 16 * c:144 + 16 * c], str_[:, P * c:P * c + P], square[0:16, 0, 0:16])
                    mm.then_inc(even_t, 1)
                    for g in range(4):
                        mm = pe.transpose(ps[7][:, P * g:P * g + P], wsr[:, g, :], ident)
                    mm.then_inc(even_t, 1)
                    for c in range(4):
                        stats(c, 4, hT[:, 16:20, :], sqT, (group_free, G_EIN + c + 1))
                if n == 3:
                    pe.wait_ge(x_ready, 4)
                    pe.wait_ge(even_tc, 2)
                    for t in range(2):
                        for c in range(4):
                            mm = pe.transpose(ps[6 + t][:, P * c:P * c + P], hT[:, 16 + c, P * t:P * t + P], ident)
                    mm.then_inc(vt_done, 1)
            pe.wait_ge(vt_copied, 1)
            for g in range(4):
                b = bank()
                for t in range(2):
                    pe.matmul(b[:, P * t:P * t + P], vtok[:, t, P * g:P * g + P], wsT[:, g, :], start=True, stop=False)
                    mm = pe.matmul(b[:, P * t:P * t + P], one8[0:1, :], sgb[:, P * g:P * g + P], start=False, stop=True)
                done.inc(mm)
            pe.wait_ge(z_done, 1)
            for c in range(4):
                mm = pe.transpose(ps[6][0:10, P * c:P * c + P], zlast[:, c, :], ident)
            mm.then_inc(z_t, 1)
            for c in range(4):
                mm = pe.transpose(ps[7][0:8, P * c:P * c + P], hT[:, 16 + c, TP:T], ident)
            mm.then_inc(z_t, 1)
            pe.wait_ge(group_free, G_EOUT)
            proj_with_stats(S_EOUT, y, G_EOUT)

            def up(s, xin):
                arrived(s, 32)
                for j in range(2):
                    for a, v in enumerate(up_views(s)):
                        first = (lambda k: (x_ready, 4 + k + 1)) if s == S_UP[0] and j == 0 and a == 0 else None
                        group(lambda k: v[:, k, P * j:P * j + P], xin, KD, ready=first)

            with pe.Fori(0, 2) as i:
                done.enter(i, 20)
                for s in S_UP:
                    loads[s].enter(i, 32)
                    up(s, x)
                    loads[s].leave(2)
                done.leave(2)
            up(S_UPLAST, x)
            for i in range(2):
                for pair in range(2):
                    pr = S_DOWN[2 * pair:2 * pair + 2]
                    for s in pr:
                        arrived(s)
                    for j in range(2):
                        c = 4 * i + 2 * pair + j
                        first = (lambda k: (group_free, G_UP + 2 * k + 2)) if c == 0 else None
                        group(lambda k: slab(pr[k // 11], 11, 256)[:, k % 11, P * j:P * j + P],
                              lambda k: hT[:, k, :], KF, ready=first)
                        if c:
                            stats(c - 1, KD, rT, sqT, (group_free, G_DOWN + c))
            stats(KD - 1, KD, rT, sqT, (group_free, G_DOWN + KD))

            pe.wait_ge(idx_in, 16 * 13)
            pe.wait_ge(var_done, got[0])
            turned = []

            def rotate(n, g):
                q = len(turned)
                pe.wait_ge(group_free, g + 1)
                if q >= 2:
                    pe.wait_ge(roped, q - 1)
                pe.matmul(ps[4 + q % 2][:, 0:T], rot, hT[:, n, :], start=True, stop=True).then_inc(rot_done, 1)
                turned.append(n)

            todo = []
            for s, n0, kind in zip(S_OIN, (QI, KI, KK, QQ, QQ + 4), ("std", "ki", "kv", "q", "q")):
                arrived(s, {"ki": 32, "q": 128}.get(kind, 16))
                if kind == "ki":
                    v = slab(s, KD, 136)
                    todo.append((KI, done.k))
                    group(lambda k: v[:, k, 0:P], x, KD)
                    group(lambda k: v[:, k, P:P + 8], x, KD, m=8)
                    continue
                for j in range(4):
                    now = (n0 + j, done.base + done.k)
                    first = (lambda k: (x_ready, 4 + KD + k + 1)) if n0 == QI and j == 0 else None
                    group(lambda k: slab(s, KD, 512)[:, k, P * j:P * j + P], x, KD, ready=first)
                    if todo:
                        rotate(*todo.pop(0))
                    if kind != "kv" or j < 2:
                        todo.append(now)
            for now in todo:
                rotate(*now)
            assert turned == ROPED, turned
            pe.wait_ge(roped, len(ROPED))
            for t in range(2):
                for c in range(4):
                    pe.transpose(ps[4 + t][:, P * c:P * c + P], hT[:, KK + c, P * t:P * t + P], ident)
            for c in range(4):
                pe.transpose(ps[6][0:8, P * c:P * c + P], hT[:, KK + c, TP:T], ident)
            for t in range(2):
                pe.transpose(ps[7][:, 64 * t:64 * t + 64], hT[0:64, KI, P * t:P * t + P], square[0:64, 0, 0:64])
                pe.transpose(ps[7][:, 192 + 8 * t:200 + 8 * t], wiT[:, P * t:P * t + P], square[0:8, 0, 0:8])
            pe.transpose(ps[7][0:8, 128:192], hT[0:64, KI, TP:T], square[0:64, 0, 0:64]).then_inc(tok_t, 1)

            pe.wait_ge(tok_copied, 5)
            pe.matmul(ps[7][:, 0:32].rearrange("p (c b) -> p c b", c=4), swap, hT[:, QI:QI + 4, TP:T],
                      start=True, stop=True).then_inc(swapped, 1)
            pe.wait_ge(wib_in, 1)
            pe.matmul(ps[7][:, 64:128], one8[:], dwi, start=True, stop=True).then_inc(swapped, 1)

            for u in range(4):
                t, c0 = u // 2, 2 * (u % 2)
                L = P * (t + 1)
                for half in range(2):
                    if u >= 2:
                        pe.wait_ge(rel_done, 2 * (u - 2) + half + 1)
                    for c in range(2):
                        mm = pe.matmul(ps[2 * (u % 2) + half][:, 256 * c:256 * c + L],
                                       hT[64 * half:64 * half + 64, QI + c0 + c, P * t:P * t + P],
                                       hT[64 * half:64 * half + 64, KI, 0:L], start=True, stop=True)
                    mm.then_inc(dots_done, 1)

            def logits(u):
                t, c0 = u // 4, 2 * (u % 4)
                L = P * (t + 1)
                for half in range(2):
                    if u:
                        pe.wait_ge(lg_read, 2 * (u - 1) + half + 1)
                    for c in range(2):
                        mm = pe.matmul(ps[half][:, 256 * c:256 * c + L],
                                       hT[64 * half:64 * half + 64, QQ + c0 + c, P * t:P * t + P],
                                       hT[64 * half:64 * half + 64, KK + c0 // 4, 0:L], start=True, stop=True)
                    mm.then_inc(lg_done, 1)

            def values(u):
                t, c0 = u // 4, 2 * (u % 4)
                nb = t + 1
                for half in range(2):
                    v = 2 * u + half
                    pe.wait_ge(prob_done, v + 1)
                    if v >= 2:
                        pe.wait_ge(pt_copied, v - 1)
                    for c in range(2):
                        for k in range(nb):
                            mm = pe.transpose(ps[4 + v % 2][:, P * (c * nb + k):P * (c * nb + k) + P],
                                              S[u % 2][:, half, c, P * k:P * k + P], ident)
                    mm.then_inc(pt_done, 1)
                for half in range(2):
                    v = 2 * u + half
                    pe.wait_ge(pt_copied, v + 1)
                    if u and half == 0:
                        pe.wait_ge(o_copied, u)
                    head = 2 * (c0 // 4) + half
                    for c in range(2):
                        for k in range(nb):
                            mm = pe.matmul(ps[6][64 * half:64 * half + 64, P * c:P * c + P],
                                           ktv[:, k, 256 + 64 * head:320 + 64 * head],
                                           PT[v % 2][:, P * (c * nb + k):P * (c * nb + k) + P],
                                           start=(k == 0), stop=(k == nb - 1))
                    mm.then_inc(o_done, 1)

            def ki_transposes(b):
                pe.wait_ge(ki_in[b % 2], 16 * (b // 2 + 1))
                if b >= 2:
                    pe.wait_ge(ki_copied, b - 1)
                for c in range(4):
                    mm = pe.transpose(ps[4 + b % 2][:, P * c:P * c + P], kibuf[b % 2][:, P * c:P * c + P], ident)
                mm.then_inc(ki_t, 1)

            ki_transposes(0)
            pe.wait_ge(qi_ready, 2)
            for b in range(TS):
                if b + 1 < TS:
                    ki_transposes(b + 1)
                pe.wait_ge(ki_copied, b + 1)
                for c in range(4):
                    mm = pe.matmul(ps[6][:, 64 * b + 16 * c:64 * b + 16 * c + 16], kiT[b % 2][:, P * c:P * c + P],
                                   qiB[:, b, :], start=True, stop=True)
                mm.then_inc(ki_mm, 1)
            pe.matmul(ps[7][0:8, 256:320], hT[0:64, KI, TP:T], qiB[0:64, :, 0:8],
                      start=True, stop=True).then_inc(sdots, 1)

            def k_transposes(u):
                b, hf = u // 2, u % 2
                pe.wait_ge(k_in[hf], 16 * (b + 1))
                for j in range(2):
                    if u >= 1:
                        pe.wait_ge(k_copied, 2 * (u - 1) + j + 1)
                    else:
                        pe.wait_ge(rel_done, 8)
                    for r in range(4):
                        mm = pe.transpose(ps[j][:, P * r:P * r + P],
                                          kbuf[hf][:, 256 * r + P * j:256 * r + P * j + P], ident)
                    mm.then_inc(k_t, 1)

            pe.wait_ge(qbd_done, 1)
            k_transposes(0)
            for u in range(2 * TS):
                b, hf = u // 2, u % 2
                if u + 1 < 2 * TS:
                    k_transposes(u + 1)
                if u == 0:
                    pe.wait_ge(score_done, 1)
                    for a in range(2):
                        for r in range(4):
                            pe.transpose(ps[4 + a][0:8, P * r:P * r + P], score[:, :, 2 * r + a], ident)
                    pe.wait_ge(new_masked, 1)
                    pe.transpose(ps[7][0:8, 0:8], sc9, square[0:8, 0, 0:8]).then_inc(row_t, 1)
                for j in range(2):
                    pe.wait_ge(k_copied, 2 * u + j + 1)
                    o = D * j + P * b
                    mm = pe.matmul(ps[2 + hf][:, :], qwide[:, o:o + P], KT[u % 2][:, j, :],
                                   start=(b == 0 and j == 0), stop=(b == TS - 1 and j == 1))
                mm.then_inc(k_mm, 1)
            for j in range(2):
                mm = pe.matmul(ps[6][:, 0:8], qfull[:, j, :], hT[:, KK + j, TP:T], start=(j == 0), stop=(j == 1))
            mm.then_inc(slg_done, 1)
            logits(0)
            pe.wait_ge(slg_copied, 3)
            pe.wait_ge(row_masked, 1)
            rv = row[:, 0:1024].rearrange("b (s r) -> b r s", r=8)
            for a in range(2):
                pe.matmul(ps[2 + a][:, :], pick[:], rv[:, 4 * a:4 * a + 4, :], start=True, stop=True)
            pe.matmul(ps[7][:, 0:8], pick[:], row[:, 1024:1032], start=True, stop=True).then_inc(mask_wide, 1)
            pe.wait_ge(sprob_done, 1)
            for a in range(2):
                for r in range(4):
                    pe.transpose(ps[2 + a][:, P * r:P * r + P], SS[:, 512 * a + P * r:512 * a + P * r + P], ident)
            pe.transpose(ps[7][0:8, 0:P], SS[:, 1024:1032], ident).then_inc(spt_done, 1)

            def sample_values(b):
                if b == 0:
                    pe.wait_ge(spt_copied, 3)
                if b >= 2:
                    pe.wait_ge(om_done, b - 1)
                pe.wait_ge(v_in[b % 2], 16 * (b // 2 + 1))
                vb = (rT, sqT)[b % 2][:].rearrange("p c t -> p (c t)")
                out = ps[2 + b % 2][0:16, 0:256]
                for r in range(RUN):
                    pe.matmul(out, PTs[:, r, 16 * b:16 * b + 16], vb[:, 256 * r:256 * r + 256],
                              start=(r == 0), stop=False)
                pe.matmul(out, PTs[0:8, 8, 16 * b:16 * b + 16], kvs[0:8, 256:512],
                          start=False, stop=True).then_inc(v_used, 1)

            def sample_heads(b):
                pe.wait_ge(om_done, b + 1)
                for j in range(2):
                    mm = pe.matmul(ps[7][:, 8 * b + 4 * j:8 * b + 4 * j + 4], om[b % 2][:, P * j:P * j + P],
                                   heads[:, 256:260], start=True, stop=True)
                mm.then_inc(so_t, 1)

            for u in range(8):
                if u < 7:
                    logits(u + 1)
                sample_values(u)
                if u:
                    sample_heads(u - 1)
                values(u)
            sample_heads(TS - 1)

            pe.wait_ge(so_done, 1)
            proj_with_stats(S_OOUT, y, G_OOUT, by=64)
            for t in range(3):
                m = P if t < 2 else 8
                out = ps[6][0:m, 8 * t:8 * t + 8]
                for k in range(KD):
                    if t == 0:
                        pe.wait_ge(x_ready, 4 + 2 * KD + k + 1)
                    pe.matmul(out, xT[:, k, P * t:P * t + m], wrt[:, k, :], start=(k == 0), stop=False)
                mm = pe.matmul(out, one8[0:1, 0:m], wrb[:], start=False, stop=True)
                mm.then_inc(route_done, 1)
            for t in range(3):
                m = P if t < 2 else 8
                for a in range(2):
                    q = 2 * t + a
                    if q >= 2:
                        pe.wait_ge(xt_copied, q - 1)
                    else:
                        pe.wait_ge(var_done, got[0])
                    for c in range(4):
                        mm = pe.transpose(ps[4 + q % 2][0:m, P * c:P * c + P], xT[:, 4 * a + c, P * t:P * t + m], ident)
                    mm.then_inc(xt_t, 1)
            pe.wait_ge(chosen, 1)
            for t in range(4):
                m = 8 if t == 2 else P
                out = ps[7][0:m, 8 * t:8 * t + 8]
                last = min(t, 2)
                for k in range(last + 1):
                    mk = P if k < 2 else 8
                    w = before if k == t else all1
                    mm = pe.matmul(out, w[0:mk, 0:m], choice[0:mk, 2, k, :], start=(k == 0), stop=(k == last))
            mm.then_inc(counted, 1)
            def places(r):
                for e in range(NE):
                    out = ps[(6, 7, 6)[r]][0:CAP, 2 * e:2 * e + 2]
                    for n, t in enumerate(TILES[r]):
                        m = P if t < 2 else 8
                        if e == 0:
                            pe.wait_ge(sel_ready, SELS[r] + n + 1)
                        mm = pe.matmul(out, sel[0:m, t, e, :], tg[0:m, t, e, :], start=(n == 0), stop=(t == 2))
                mm.then_inc(sel_done, 1)

            places(0)
            pe.wait_ge(passes_ready, 1)
            n = pe.value_load(npass[0:1, 0:1], min_val=NE, max_val=ROUNDS * NE)
            with pe.If(n > NE):
                places(1)
                places(2)

            def gathered():
                for a in range(2):
                    b = bank()
                    for c in range(4):
                        mm = pe.transpose(b[:, CAP * c:CAP * c + CAP], xg[:, P * (4 * a + c):P * (4 * a + c) + P],
                                          square[0:CAP, 0, 0:CAP])
                    done.inc(mm)

            pe.wait_ge(xg_in, 16)
            gathered()
            with pe.Fori(0, n) as i:
                done.enter(i, G_EXP)
                for s in range(NSLOT):
                    loads[s].enter(i, 32 if s < 4 else 16)
                pe.wait_ge(group_free, done.base)
                for s in range(4):
                    arrived(s, 32)
                    for j in range(2):
                        b = bank()
                        for a, v in enumerate(up_views(s)):
                            for k in range(KD):
                                mm = pe.matmul(b[:, CAP * a:CAP * a + CAP], v[:, k, P * j:P * j + P], xgT[:, k, :],
                                               start=(k == 0), stop=(k == KD - 1))
                        done.inc(mm)
                pe.wait_ge(xg_in, 16 * (i + 2))
                gathered()
                pe.wait_ge(group_free, done.base + KD)
                for s in (4, 5):
                    arrived(s)
                    b = bank()
                    for k in range(KD):
                        mm = pe.matmul(b[0:CAP, :], hg[:, k, :], slab(s, KD, 512)[:, k, :],
                                       start=(k == 0), stop=(k == KD - 1))
                    done.inc(mm)
                for s in range(NSLOT):
                    loads[s].leave(n)
                done.leave(n)

        @block.scalar
        def _(act):
            norms, cen = [0], [0]

            def squares(n, src, ready):
                for c in range(n):
                    act.wait_ge(ready[0], ready[1] + c + 1)
                    act.activation(sqT[:, c, :], src[:, c, :], ACT.Square).then_inc(sq_done, 1)

            def norm(n, dst, src, g, b):
                norms[0] += 1
                act.wait_ge(var_done, norms[0])
                act.activation(rstd[:], var[:], ACT.Sqrt, bias=eps[:, 0:1]).then_inc(std_done, 1)
                for c in range(n):
                    cen[0] += 1
                    act.wait_ge(centred, cen[0])
                    act.activation(dst[:, c, :], src[:, c, :], ACT.Identity, scale=vec[:, g + c:g + c + 1],
                                   bias=vec[:, b + c:b + c + 1]).then_inc(x_ready, 1)

            def silus(n, g0, first):
                for m in range(n):
                    act.wait_ge(group_done, g0 + 2 * m + 1)
                    act.wait_ge(group_free, g0 + 2 * m - 2)
                    act.activation(silu[:, m % 2, :], ps[(first + 2 * m) % NB][:, 0:T], ACT.Silu).then_inc(silu_done, 1)

            vT = hT[:, 16:20, :]
            squares(4, vT, (group_free, G_EIN))
            act.wait_ge(even_tc, 2)
            act.wait_ge(pool_consts, 8)
            norm(4, vT, vT, V_SG, V_SB)
            squares(KD, rT, (group_free, G_EOUT))
            norm(KD, xT, rT, V_LN1G, V_LN1B)
            with act.Fori(0, 2) as i:
                silus(10, G_UP + 20 * i, G_UP % NB)
            silus(2, G_UP + 40, G_UP % NB)
            squares(KD, rT, (group_free, G_DOWN))
            norm(KD, xT, rT, V_LN2G, V_LN2B)
            act.wait_ge(zeros_ready, 1)
            act.dma_start(r_rows[NE * CAP:ROUNDS * NE * CAP, :].rearrange("(p a) (c q) -> p (a c) q", p=P, q=512),
                          silu[:].rearrange("p a t -> p (a t)")[:, 0:512].unsqueeze(1)
                          .to_broadcast([P, (ROUNDS - 1) * NE * CAP * 2 // P, 512])
                          ).then_inc(rows_cleared, 16)

            act.wait_ge(tok_t, 1)
            act.copy(ktv[:, 0, :], ps[4][:, :]).then_inc(tok_copied, 1)
            act.copy(kvs[:], ps[6][0:8, :]).then_inc(tok_copied, 1)
            for u in range(4):
                L = P * (u // 2 + 1)
                for half in range(2):
                    v = 2 * u + half
                    act.wait_ge(dots_done, v + 1)
                    if v >= 2:
                        act.wait_ge(rel_used, v - 1)
                    src = ps[2 * (u % 2) + half][:, :].rearrange("p (c s) -> p c s", c=2)[:, :, 0:L]
                    act.activation(rel[half][:, :, 0:L], src, ACT.Relu, scale=0.125).then_inc(rel_done, 1)

            def exps(u):
                L = P * (u // 4 + 1)
                for half in range(2):
                    act.wait_ge(lg_read, 2 * u + half + 1)
                    for c in range(2):
                        col = 4 * (u % 2) + 2 * half + c
                        row_ = S[u % 2][:, half, c, 0:L]
                        ins = act.activation(row_, row_, ACT.Exp, bias=stat[:, col:col + 1],
                                             accum_out=stat[:, 8 + col:9 + col])
                    ins.then_inc(exp_done, 1)

            def probs_by_key(u):
                n = 256 * (u // 4 + 1)
                for half in range(2):
                    v = 2 * u + half
                    act.wait_ge(pt_done, v + 1)
                    if v >= 2:
                        act.wait_ge(o_done, v - 1)
                    act.copy(PT[v % 2][:, 0:n], ps[4 + v % 2][:, 0:n]).then_inc(pt_copied, 1)

            for b in range(TS):
                act.wait_ge(ki_t, b + 1)
                if b >= 2:
                    act.wait_ge(ki_mm, b - 1)
                act.copy(kiT[b % 2], ps[4 + b % 2][:, :]).then_inc(ki_copied, 1)
            act.wait_ge(ki_mm, TS)
            act.wait_ge(sdots, 1)
            act.activation(srel[:, 0:512], ps[6][:, :], ACT.Relu, scale=0.125).then_inc(srel_done, 1)
            act.activation(srel[0:8, 512:576], ps[7][0:8, 256:320], ACT.Relu, scale=0.125).then_inc(srel_done, 1)
            for u in range(2 * TS):
                for j in range(2):
                    act.wait_ge(k_t, 2 * u + j + 1)
                    if u >= 2:
                        act.wait_ge(k_mm, u - 1)
                    act.copy(KT[u % 2][:, j, :], ps[j][:, :]).then_inc(k_copied, 1)
            act.wait_ge(slg_done, 1)
            for a in range(2):
                act.mul(SS[:, 512 * a:512 * a + 512], ps[2 + a][:, :], 0.125).then_inc(slg_copied, 1)
            act.mul(SS[:, 1024:1032], ps[6][:, 0:8], 0.125).then_inc(slg_copied, 1)
            act.wait_ge(smax_done, 1)
            act.activation(SS, SS, ACT.Exp, bias=st8[:, 0:1], accum_out=st8[:, 1:2]).then_inc(sexp_done, 1)
            act.wait_ge(even_stored, 16 * 3)
            act.wait_ge(state_stored, 16)
            exps(0)
            act.wait_ge(spt_done, 1)
            for a in range(2):
                act.copy(PTs[:, 4 * a:4 * a + 4, :].rearrange("p r q -> p (r q)"), ps[2 + a][:, :]).then_inc(spt_copied, 1)
            act.copy(PTs[0:8, 8, :], ps[7][0:8, 0:P]).then_inc(spt_copied, 1)
            for u in range(8):
                if u < 7:
                    exps(u + 1)
                probs_by_key(u)
            squares(KD, rT, (group_free, G_OOUT))
            norm(KD, xT, rT, V_LN1G + 8, V_LN1B + 8)
            for t in range(3):
                m = P if t < 2 else 8
                for a in range(2):
                    q = 2 * t + a
                    act.wait_ge(xt_t, q + 1)
                    act.copy(xrow[0:m, t, 512 * a:512 * a + 512], ps[4 + q % 2][0:m, :]).then_inc(xt_copied, 1)
                    if q == 1:
                        act.wait_ge(route_in, 1)
                        act.activation(gate[:, 1, :], gate[:, 0, :], ACT.Exp).then_inc(gate_e, 1)
            act.wait_ge(passes_ready, 1)
            act.wait_ge(rows_cleared, 16)
            n = act.value_load(npass[0:1, 0:1], min_val=NE, max_val=ROUNDS * NE)
            with act.Fori(0, n) as i:
                for m in range(KD):
                    act.wait_ge(group_done, G_MOE + i * G_EXP + m + 1)
                    act.wait_ge(group_free, G_MOE + i * G_EXP + m - 1)
                    act.activation(silug[:, m % 2, :], ps[(G_MOE + m) % NB][:, 0:CAP], ACT.Silu).then_inc(silu_done, 1)
            for t in range(3):
                m = P if t < 2 else 8
                act.wait_ge(fvar, t + 1)
                act.activation(fin[0:m, t, 14:15], fin[0:m, t, 13:14], ACT.Sqrt, bias=eps[0:m, 0:1]).then_inc(fstd, 1)

        @block.vector
        def _(dve):
            V = nc.vector
            chain = Count(dchain)
            free = Count(group_free)
            norms = [0]

            def mark(ins):
                return chain.inc(ins)

            def link(ins):
                dve.wait_ge(dchain, chain.inc(ins))

            def filled(ahead=0):
                dve.wait_ge(group_done, free.base + free.k + 1 + ahead)
                return ps[(free.phase + free.k + ahead) % NB]

            def residual(n):
                for c in range(n):
                    free.inc(V.scalar_tensor_tensor(out=rT[:, c, :], in0=xT[:, c, :], scalar=ALPHA,
                                                    in1=filled()[:, 0:T], op0=ALU.mult, op1=ALU.add))

            def norm(n, src):
                norms[0] += 1
                scale = float(KD // n)
                dve.wait_ge(stats_done, norms[0])
                link(V.tensor_scalar(mean[:], ps[4][:, 0:T], scale, None, ALU.mult))
                link(V.tensor_tensor(var[:], mean[:], mean[:], ALU.mult))
                V.scalar_tensor_tensor(out=var[:], in0=ps[5][:, 0:T], scalar=scale, in1=var[:],
                                       op0=ALU.mult, op1=ALU.subtract).then_inc(var_done, 1)
                dve.wait_ge(std_done, norms[0])
                link(V.reciprocal(rstd[:], rstd[:]))
                at = [mark(V.tensor_tensor(src[:, 0, :], src[:, 0, :], mean[:], ALU.subtract))]
                for c in range(n):
                    if c + 1 < n:
                        at.append(mark(V.tensor_tensor(src[:, c + 1, :], src[:, c + 1, :], mean[:], ALU.subtract)))
                    dve.wait_ge(dchain, at[c])
                    V.tensor_tensor(src[:, c, :], src[:, c, :], rstd[:], ALU.mult).then_inc(centred, 1)

            V.memset(lgr[:], 0.0)
            V.memset(place[:], 0.0)
            V.memset(fin[:], 1.0)
            V.memset(tokg[:], 0.0)
            for c in range(KD):
                free.inc(V.tensor_copy(xT[:, c, :], filled()[:, 0:T]))
            dve.wait_ge(group_free, KD)
            V.memset(zext[:, :, 0:2], 0.0)
            for c in range(4):
                free.inc(V.tensor_copy(hT[:, 16 + c, :], filled()[:, 0:T]))
            for c in range(4):
                free.inc(V.tensor_copy(hT[:, 4 + c, :], filled()[:, 0:T]))
            dve.wait_ge(even_t, 1)
            V.tensor_copy(vec[:], ps[6][:, 0:NVEC])
            V.tensor_copy(stT, ps[6][:, 128:192].rearrange("p (c n) -> p c n", c=4)).then_inc(even_tc, 1)
            dve.wait_ge(even_t, 2)
            V.tensor_copy(wsT, ps[7][:, :].rearrange("p (g i) -> p g i", g=4)).then_inc(even_tc, 1)
            norm(4, hT[:, 16:20, :])
            dve.wait_ge(idx_in, 16 * 13)
            link(V.tensor_copy(idxf[:], idx[:, 0, :]))
            link(V.tensor_scalar(idxf[:], idxf[:], float(PAGE // RUN), sg[:, 0:1], ALU.mult, ALU.add))
            V.tensor_copy(idx[:, 0, :], idxf[:])
            V.tensor_scalar(idx[:, 1, :], idxf[:], 2.0, None, ALU.mult)
            V.tensor_scalar(idx[:, 2, :], idxf[:], 2.0, 1.0, ALU.mult, ALU.add).then_inc(idx_done, 1)

            dve.wait_ge(even_tc, 2)
            dve.wait_ge(group_free, free.k)
            w_ = lambda j, c: vec[:, V_CW + 4 * j + c:V_CW + 4 * j + c + 1]
            for c in range(4):
                b = filled()
                mark(V.tensor_tensor(zext[:, c, 2:258], b[:, 0:TP], hT[:, 4 + c, 0:TP], ALU.mult))
                free.inc(V.tensor_tensor(zlast[:, c, 2:10], b[:, TP:T], hT[:, 4 + c, TP:T], ALU.mult))
                dve.wait_ge(group_free, free.k)
                mark(V.tensor_scalar(cst, zext[:, c, 2:258], w_(2, c), None, ALU.mult))
                link(V.tensor_scalar(css, zlast[:, c, 2:10], w_(2, c), None, ALU.mult))
                mark(V.scalar_tensor_tensor(out=cst, in0=zext[:, c, 1:257], scalar=w_(1, c), in1=cst,
                                            op0=ALU.mult, op1=ALU.add))
                link(V.scalar_tensor_tensor(out=css, in0=stT[:, c, 1:16:2], scalar=w_(1, c), in1=css,
                                            op0=ALU.mult, op1=ALU.add))
                mark(V.scalar_tensor_tensor(out=hT[:, 8 + c, 0:TP], in0=zext[:, c, 0:256], scalar=w_(0, c), in1=cst,
                                            op0=ALU.mult, op1=ALU.add))
                link(V.scalar_tensor_tensor(out=hT[:, 8 + c, TP:T], in0=stT[:, c, 0:16:2], scalar=w_(0, c), in1=css,
                                            op0=ALU.mult, op1=ALU.add))
            V.tensor_copy(zlast[:, :, 0:2], zext[:, :, 256:258]).then_inc(z_done, 1)
            for c in range(4):
                free.inc(V.tensor_copy(hT[:, 12 + c, :], filled()[:, 0:T]))
            dve.wait_ge(vt_done, 1)
            for t in range(2):
                ins = V.tensor_copy(vtok[:, t, :], ps[6 + t][:, :])
            ins.then_inc(vt_copied, 1)
            for c in range(4):
                free.inc(V.tensor_tensor(yT[:, c, :], filled()[:, 0:T], hT[:, 8 + c, :], ALU.mult))
            dve.wait_ge(x_ready, 4)
            for g in range(4):
                b = filled()
                V.tensor_tensor(yT[:, 4 + g, 0:TP], b[:, 0:TP], hT[:, 12 + g, 0:TP], ALU.mult)
                link(V.tensor_scalar(css, hT[:, 16 + g, TP:T], w00[:, 0, g:g + 1], w00[:, 1, g:g + 1],
                                     ALU.mult, ALU.add))
                free.inc(V.tensor_tensor(yT[:, 4 + g, TP:T], css, hT[:, 12 + g, TP:T], ALU.mult))
                dve.wait_ge(group_free, free.k)
            dve.wait_ge(z_t, 1)
            V.tensor_copy(zrow, ps[6][0:10, :]).then_inc(z_copied, 1)
            dve.wait_ge(z_t, 2)
            V.tensor_copy(vrow, ps[7][0:8, :]).then_inc(z_copied, 1)
            residual(KD)
            norm(KD, rT)

            def hidden(m, dst):
                filled(1)
                b = ps[(free.phase + free.k + 1) % NB]
                free.inc(V.tensor_tensor(dst, silu[:, m % 2, :], b[:, 0:T], ALU.mult), 2)

            silus = Count(silu_done)
            with dve.Fori(0, 2) as i:
                free.enter(i, 20)
                silus.enter(i, 10)
                for m in range(10):
                    silus.k += 1
                    dve.wait_ge(silu_done, silus.base + silus.k)
                    hidden(m, hT[:, bass.ds(i * 10 + m, 1), :].rearrange("p a t -> p (a t)"))
                silus.leave(2)
                free.leave(2)
            for m in range(2):
                silus.k += 1
                dve.wait_ge(silu_done, silus.base + silus.k)
                hidden(m, hT[:, 20 + m, :])
            residual(KD)
            norm(KD, rT)

            V.memset(silu[:], 0.0).then_inc(zeros_ready, 1)

            ropes = [0]

            def turn():
                q = ropes[0]
                n = ROPED[q]
                dve.wait_ge(rot_done, q + 1)
                mark(V.tensor_tensor(mean[:], hT[:, n, :], rope[:, 0, :], ALU.mult))
                link(V.tensor_tensor(var[:], ps[4 + q % 2][:, 0:T], rope[:, 1, :], ALU.mult))
                V.tensor_tensor(hT[:, n, :], mean[:], var[:], ALU.add).then_inc(roped, 1)
                dve.wait_ge(roped, q + 1)
                ropes[0] += 1

            waiting = 0
            for n0, kind in ((QI, "std"), (KI, "ki"), (KK, "kv"), (QQ, "q"), (QQ + 4, "q")):
                if kind == "ki":
                    free.inc(V.tensor_copy(hT[:, KI, :], filled()[:, 0:T]))
                    free.inc(V.tensor_scalar(wiT[:], filled()[0:8, 0:T], 8.0 ** -0.5, None, ALU.mult))
                    waiting += 1
                    continue
                for j in range(4):
                    free.inc(V.tensor_copy(hT[:, n0 + j, :], filled()[:, 0:T]))
                    if waiting:
                        turn()
                        waiting -= 1
                    if kind != "kv" or j < 2:
                        waiting += 1
            while waiting:
                turn()
                waiting -= 1
            dve.wait_ge(tok_t, 1)
            V.tensor_copy(ktv[:, 1, :], ps[5][:, :]).then_inc(tok_copied, 1)
            V.tensor_copy(kit[0:8, 2, :], ps[7][0:8, 128:192])
            V.tensor_copy(kit[:, 0:2, :], ps[7][:, 0:128].rearrange("p (t d) -> p t d", t=2)).then_inc(tok_copied, 1)
            V.tensor_copy(wit[:], ps[7][:, 192:208].rearrange("p (t h) -> p t h", t=2)).then_inc(tok_copied, 1)
            dve.wait_ge(tok_copied, 5)
            lo, hi = slice(0, 64), slice(64, P)
            V.tensor_tensor(dwi.rearrange("h (b g) -> h b g", b=8),
                            wiT[:, TP:T].unsqueeze(2).to_broadcast([8, 8, 8]),
                            square[0:8, 0:1, 0:8].to_broadcast([8, 8, 8]), ALU.mult).then_inc(wib_in, 1)
            link(V.memset(qiB[:], 0.0))
            dve.wait_ge(swapped, 2)
            qv = qiB[:].rearrange("p b (a c e) -> p a e c b", a=2, e=2)
            raw = hT[:, QI:QI + 4, TP:T]
            swp = ps[7][:, 0:32].rearrange("p (c b) -> p c b", c=4)
            V.tensor_copy(qv[lo, 0, 0], raw[lo])
            V.tensor_copy(qv[hi, 1, 1], raw[hi])
            V.tensor_copy(qv[lo, 0, 1], swp[lo])
            V.tensor_copy(qv[hi, 1, 0], swp[hi]).then_inc(qi_ready, 1)
            V.tensor_copy(wib, ps[7][:, 64:128]).then_inc(qi_ready, 1)
            mark(V.memset(qwide, 0.0))
            link(V.memset(mean[:], 0.0))
            for j in range(2):
                q = hT[:, QQ + 4 * j:QQ + 4 * j + 4, TP:T].rearrange("p x b -> p b x")
                wide_ = slot[3][:, D * j:D * j + 9 * P].rearrange("p (b w) -> p b w", w=P + 16)
                full = qfull[:, j, :].rearrange("p (b w) -> p b w", b=8)
                for half, rows in ((0, lo), (1, hi)):
                    at = slice(8 * j + 4 * half, 8 * j + 4 * half + 4)
                    V.tensor_copy(wide_[rows, :, at], q[rows])
                    ins = V.tensor_copy(full[rows, :, at], q[rows])
            ins.then_inc(qbd_done, 1)
            for u in range(4):
                t, c0 = u // 2, 2 * (u % 2)
                L = P * (t + 1)
                for half in range(2):
                    v = 2 * u + half
                    dve.wait_ge(rel_done, v + 1)
                    for c in range(2):
                        wgt = wit[:, t, 2 * (c0 + c) + half:2 * (c0 + c) + half + 1]
                        src = rel[half][:, c, 0:L]
                        if u % 2 == 0 and half == 0 and c == 0:
                            ins = V.tensor_scalar(sc[:, t, 0:L], src, wgt, None, ALU.mult)
                        else:
                            ins = V.scalar_tensor_tensor(out=sc[:, t, 0:L], in0=src, scalar=wgt, in1=sc[:, t, 0:L],
                                                         op0=ALU.mult, op1=ALU.add)
                        if c == 0:
                            link(ins)
                    ins.then_inc(rel_used, 1)
                    dve.wait_ge(rel_used, v + 1)

            def select(src, dst, mx, k):
                for _ in range(k // 8):
                    link(V.max(out=mx, in_=src))
                    link(V.match_replace(out=dst, in_to_replace=mx, in_values=src, imm_value=TAKEN))
                    src = dst

            for t in range(2):
                L = P * (t + 1)
                dve.wait_ge(sc_causal, t + 1)
                select(sc[:, t, 0:L], work[:, t, 0:L], mx8p[:], TOPK_P)
                V.tensor_scalar(work[:, t, 0:L], work[:, t, 0:L], TAKEN / 2, NEG, ALU.is_gt,
                                ALU.mult).then_inc(bias_done, 1)

            def masked_logits(u):
                t = u // 4
                L = P * (t + 1)
                dve.wait_ge(bias_causal, t + 1)
                if u >= 2:
                    dve.wait_ge(pt_done, 2 * (u - 1))
                for half in range(2):
                    dve.wait_ge(lg_done, 2 * u + half + 1)
                    dst = S[u % 2][:, half, :, 0:L]
                    col = 4 * (u % 2) + 2 * half
                    link(V.scalar_tensor_tensor(
                        out=dst, in0=ps[half][:, :].rearrange("p (c s) -> p c s", c=2)[:, :, 0:L],
                        scalar=0.125, in1=work[:, t:t + 1, 0:L].to_broadcast([P, 2, L]), op0=ALU.mult, op1=ALU.add))
                    link(V.tensor_reduce(out=stat[:, col:col + 2], in_=dst, axis=AX, op=ALU.max))
                    V.tensor_scalar(stat[:, col:col + 2], stat[:, col:col + 2], -1.0, None,
                                    ALU.mult).then_inc(lg_read, 1)

            def probs(u):
                L = P * (u // 4 + 1)
                for half in range(2):
                    dve.wait_ge(exp_done, 2 * u + half + 1)
                    col = 4 * (u % 2) + 2 * half
                    link(V.reciprocal(stat[:, 16 + col:18 + col], stat[:, 8 + col:10 + col]))
                    for c in range(2):
                        row_ = S[u % 2][:, half, c, 0:L]
                        ins = V.tensor_scalar(row_, row_, stat[:, 16 + col + c:17 + col + c], None, ALU.mult)
                    ins.then_inc(prob_done, 1)

            def heads_out(u):
                t, c0 = u // 4, 2 * (u % 4)
                dve.wait_ge(o_done, 2 * (u + 1))
                V.tensor_copy(yT[:, c0:c0 + 2, P * t:P * t + P],
                              ps[6][:, 0:256].rearrange("p (c q) -> p c q", c=2)).then_inc(o_copied, 1)

            dve.wait_ge(srel_done, 2)
            v = srel[:, 0:512]
            link(V.tensor_tensor(v.rearrange("p (b r h) -> p b r h", b=8, r=8),
                                 v.rearrange("p (b r h) -> p b r h", b=8, r=8),
                                 wib.rearrange("p (b h) -> p b h", b=8).unsqueeze(2).to_broadcast([P, 8, 8, 8]),
                                 ALU.mult))
            V.tensor_reduce(out=score.rearrange("p b r -> p (b r)"), in_=v.rearrange("p (q h) -> p q h", h=8),
                            axis=AX, op=ALU.add).then_inc(score_done, 1)
            v = srel[0:8, 512:576]
            link(V.tensor_tensor(v, v, wib[0:8, :], ALU.mult))
            V.tensor_reduce(out=sc9, in_=v.rearrange("p (b h) -> p b h", b=8), axis=AX,
                            op=ALU.add).then_inc(score_done, 1)
            dve.wait_ge(row_t, 1)
            rv = row[:, 0:1024].rearrange("b (p r a) -> b a r p", r=4, a=2)
            for a in range(2):
                mark(V.tensor_copy(rv[:, a], ps[4 + a][0:8, :].rearrange("b (r p) -> b r p", r=4)))
            link(V.tensor_copy(row[:, 1024:1032], ps[7][0:8, 0:8]))
            select(row, row, mx8, TOPK_S)
            V.tensor_scalar(row, row, TAKEN / 2, None, ALU.is_gt).then_inc(row_masked, 1)
            dve.wait_ge(mask_wide, 1)
            for a in range(2):
                mark(V.scalar_tensor_tensor(out=SS[:, 512 * a:512 * a + 512], in0=ps[2 + a][:, :], scalar=NEG,
                                            in1=SS[:, 512 * a:512 * a + 512], op0=ALU.mult, op1=ALU.add))
            link(V.scalar_tensor_tensor(out=SS[:, 1024:1032], in0=ps[7][:, 0:8], scalar=NEG,
                                        in1=SS[:, 1024:1032], op0=ALU.mult, op1=ALU.add))
            link(V.reduce_max(st8[:, 2:3], SS, AX))
            V.tensor_scalar(st8[:, 0:1], st8[:, 2:3], -1.0, None, ALU.mult).then_inc(smax_done, 1)
            masked_logits(0)
            dve.wait_ge(sexp_done, 1)
            link(V.reciprocal(st8[:, 3:4], st8[:, 1:2]))
            V.tensor_scalar(SS, SS, st8[:, 3:4], None, ALU.mult).then_inc(sprob_done, 1)
            dve.wait_ge(heads_in, 16)
            for u in range(8):
                if u < 7:
                    masked_logits(u + 1)
                probs(u)
                if u:
                    heads_out(u - 1)
                dve.wait_ge(v_used, u + 1)
                V.tensor_tensor(om[u % 2], ps[2 + u % 2][0:16, 0:256], heads[:, 0:256], ALU.mult).then_inc(om_done, 1)
            heads_out(7)
            dve.wait_ge(so_t, TS)
            V.tensor_copy(yT[:, :, TP:T], ps[7][:, 0:64].rearrange("p (b c) -> p c b", b=8)).then_inc(so_done, 1)
            residual(KD)
            norm(KD, rT)

            dve.wait_ge(route_done, 3)
            V.tensor_copy(lgr[:, 0:2, :], ps[6][:, 0:16].rearrange("p (t e) -> p t e", t=2))
            link(V.tensor_copy(lgr[0:8, 2, :], ps[6][0:8, 16:24]))
            for t in range(3):
                mark(V.max(out=top[:, t, :], in_=lgr[:, t, :]))
            dve.wait_ge(dchain, chain.k)
            V.tensor_tensor(gate[:, 0, :], top[:, :, 1], top[:, :, 0], ALU.subtract).then_inc(route_in, 1)
            for t in range(3):
                mark(V.max_index(mxi[:, t, :], top[:, t, :], lgr[:, t, :]))
            dve.wait_ge(dchain, chain.k)
            link(V.tensor_copy(topi[:], mxi[:]))
            wide = lambda a: a.unsqueeze(2).to_broadcast([P, 3, 8])
            io = iota8[:].unsqueeze(1).to_broadcast([P, 3, 8])
            for k in range(2):
                mark(V.tensor_tensor(choice[:, k], io, wide(topi[:, :, k]), ALU.is_equal))
            dve.wait_ge(dchain, chain.k)
            V.tensor_tensor(choice[:, 2], choice[:, 0], choice[:, 1], ALU.add).then_inc(chosen, 1)
            dve.wait_ge(gate_e, 1)
            link(V.tensor_scalar(gate[:, 2, :], gate[:, 1, :], 1.0, None, ALU.add))
            link(V.reciprocal(gate[:, 2, :], gate[:, 2, :]))
            link(V.tensor_tensor(gate[:, 3, :], gate[:, 2, :], gate[:, 1, :], ALU.mult))
            mark(V.tensor_tensor(tmp8[:], choice[:, 0], wide(gate[:, 2, :]), ALU.mult))
            link(V.tensor_tensor(tmp8b[:], choice[:, 1], wide(gate[:, 3, :]), ALU.mult))
            mark(V.tensor_tensor(tg[:, :, :, 1], tmp8[:], tmp8b[:], ALU.add))
            dve.wait_ge(counted, 1)
            mark(V.scalar_tensor_tensor(out=place[:, 0:2, :], in0=ps[7][:, 0:16].rearrange("p (t e) -> p t e", t=2),
                                        scalar=1.0, in1=choice[:, 2, 0:2, :], op0=ALU.add, op1=ALU.mult))
            mark(V.scalar_tensor_tensor(out=place[0:8, 2, :], in0=ps[7][0:8, 16:24],
                                        scalar=1.0, in1=choice[0:8, 2, 2, :], op0=ALU.add, op1=ALU.mult))
            link(V.reduce_max(cnt[:, 0:1], ps[7][:, 24:32], AX))

            def sel_round(r):
                if r:
                    dve.wait_ge(sel_done, r)
                for t in TILES[r]:
                    m = P if t < 2 else 8
                    V.tensor_tensor(sel[0:m, t], iotac[0:m, CAP * r:CAP * r + CAP].unsqueeze(1).to_broadcast([m, NE, CAP]),
                                    place[0:m, t, :].unsqueeze(2).to_broadcast([m, NE, CAP]),
                                    ALU.is_equal).then_inc(sel_ready, 1)

            def places(r):
                dve.wait_ge(sel_done, r + 1)
                V.tensor_copy(tokg[0:CAP, NE * r:NE * r + NE, :],
                              ps[(6, 7, 6)[r]][0:CAP, 0:2 * NE].rearrange("p (e a) -> p e a", a=2)).then_inc(tokg_done, 1)
                dve.wait_ge(tokg_done, r + 1)

            def current(i):
                V.tensor_copy(curi[0:CAP, :], tokg[0:CAP, bass.ds(i, 1), 0]).then_inc(cur_ready, 1)

            sel_round(0)
            mark(V.tensor_scalar(cnt[:, 1:2], cnt[:, 0:1], float(CAP), float(NE), ALU.is_gt, ALU.mult))
            link(V.tensor_scalar(cnt[:, 2:3], cnt[:, 0:1], 2.0 * CAP, float(NE), ALU.is_gt, ALU.mult))
            link(V.scalar_tensor_tensor(out=cnt[:, 3:4], in0=cnt[:, 1:2], scalar=float(NE), in1=cnt[:, 2:3],
                                        op0=ALU.add, op1=ALU.add))
            V.tensor_copy(npass[:], cnt[0:1, 3:4]).then_inc(passes_ready, 1)
            places(0)
            current(0)
            dve.wait_ge(passes_ready, 1)
            n = dve.value_load(npass[0:1, 0:1], min_val=NE, max_val=ROUNDS * NE)
            with dve.If(n > NE):
                sel_round(1)
                places(1)
                sel_round(2)
                places(2)
            over = float(NE * CAP - CAP)
            mark(V.tensor_scalar(tmp8[:], place[:], CAP + 1.0, over, ALU.is_ge, ALU.mult))
            link(V.tensor_scalar(tmp8b[:], place[:], 2.0 * CAP + 1.0, over, ALU.is_ge, ALU.mult))
            link(V.tensor_tensor(tmp8[:], tmp8[:], tmp8b[:], ALU.add))
            link(V.scalar_tensor_tensor(out=tmp8[:], in0=place[:], scalar=-1.0, in1=tmp8[:], op0=ALU.add, op1=ALU.add))
            link(V.scalar_tensor_tensor(out=tmp8[:], in0=io, scalar=float(CAP), in1=tmp8[:], op0=ALU.mult, op1=ALU.add))
            for k in range(2):
                link(V.tensor_tensor(tmp8b[:], tmp8[:], choice[:, k], ALU.mult))
                link(V.tensor_reduce(out=rowf[:, k, :], in_=tmp8b[:], axis=AX, op=ALU.add))
                ins = V.tensor_copy(rowk[:, :, k], rowf[:, k, :])
            ins.then_inc(rowk_ready, 1)

            def gathered():
                for a in range(2):
                    free.inc(V.tensor_copy(xgT[:, 4 * a:4 * a + 4, :],
                                           filled()[:, 0:4 * CAP].rearrange("p (c s) -> p c s", c=4)))

            gathered()
            dve.wait_ge(group_free, free.k)
            with dve.Fori(0, n) as i:
                free.enter(i, G_EXP)
                silus.enter(i, KD)
                chain.enter(i, 1)
                link(V.tensor_copy(curg[0:CAP, :], tokg[0:CAP, bass.ds(i, 1), :].rearrange("p a b -> p (a b)")))
                current(i + 1)
                for m in range(KD):
                    silus.k += 1
                    dve.wait_ge(silu_done, silus.base + silus.k)
                    free.inc(V.tensor_tensor(hg[:, m, :], silug[:, m % 2, :],
                                             filled()[:, CAP:2 * CAP], ALU.mult))
                gathered()
                dve.wait_ge(rows_stored, 32 + 16 * i)
                for a in range(2):
                    b = filled()
                    free.inc(V.tensor_scalar(orow[:, 512 * a:512 * a + 512], b[0:CAP, :], curg[0:CAP, 1:2], None,
                                             ALU.mult))
                dve.wait_ge(group_free, free.base + free.k)
                chain.leave(n)
                silus.leave(n)
                free.leave(n)

            tail = Count(tchain)
            then = lambda ins: dve.wait_ge(tchain, tail.inc(ins))
            dve.wait_ge(gb_in, 32)
            def centre(t):
                m = P if t < 2 else 8
                a, b = res[0:m, t, 0, :], res[0:m, t, 1, :]
                dve.wait_ge(res_in[t], 32)
                then(V.scalar_tensor_tensor(out=a, in0=xrow[0:m, t, :], scalar=ALPHA, in1=a, op0=ALU.mult, op1=ALU.add))
                then(V.tensor_tensor(a, a, b, ALU.add))
                for h in range(2):
                    ins = V.bn_stats(fin[0:m, t, 6 * h:6 * h + 6], a[:, 512 * h:512 * h + 512])
                then(ins)
                V.bn_aggr(fin[0:m, t, 12:14], fin[0:m, t, 0:12]).then_inc(fvar, 1)
                dve.wait_ge(fvar, t + 1)
                then(V.scalar_tensor_tensor(out=a, in0=a, scalar=fin[0:m, t, 12:13], in1=cache[0:m, 0:D],
                                            op0=ALU.subtract, op1=ALU.mult))

            def scale(t):
                m = P if t < 2 else 8
                a = res[0:m, t, 0, :]
                dve.wait_ge(fstd, t + 1)
                then(V.reciprocal(fin[0:m, t, 15:16], fin[0:m, t, 14:15]))
                V.scalar_tensor_tensor(out=a, in0=a, scalar=fin[0:m, t, 15:16], in1=cache[0:m, D:2 * D],
                                       op0=ALU.mult, op1=ALU.add).then_inc(final_ready, 1)

            for t in range(3):
                centre(t)
                scale(t)


def constants():
    square = np.zeros((5, P, P), np.float32)
    square[0] = np.eye(P)
    for h in (0, 64):
        for i in range(8):
            square[1, h + i + 8, h + i] = -1.0
            square[1, h + i, h + i + 8] = 1.0
    square[2] = np.roll(np.eye(P), 64, axis=0)
    square[3] = np.triu(np.ones((P, P)), 1)
    square[4] = 1.0
    inv = np.float32(500000.0) ** (-np.arange(8, dtype=np.float32) / np.float32(8))
    pos = np.concatenate([np.arange(TP), np.full(TS, PAST)]).astype(np.float32)
    ang = (pos[:, None] * inv[None, :].astype(np.float32)).astype(np.float32)
    rope = np.zeros((2, P, T), np.float32)
    rope[0] = 1.0
    for h in (0, 64):
        for i in range(16):
            rope[0, h + i] = np.cos(ang[:, i % 8].astype(np.float64))
            rope[1, h + i] = np.sin(ang[:, i % 8].astype(np.float64))
    pick = np.zeros((9, P), np.float32)
    pick[np.arange(P) // 16, np.arange(P)] = 1.0
    pick[8] = np.arange(P) % (PAGE // RUN)
    heads = np.zeros((16, 260), np.float32)
    for h in range(16):
        heads[h, 64 * (h // 4):64 * (h // 4) + 64] = 1.0
        heads[h, 256 + h % 4] = 1.0
    return {"c_square": square, "c_rope": rope, "c_pick": pick, "c_heads": heads}


INPUTS = ["x_prompt", "x_sample", "cache_k", "cache_v", "cache_kidx", "state_conv", "page_table",
          "ln1_g", "ln1_b", "ln2_g", "ln2_b", "w_in_even", "conv_w", "sgu_ln_g", "sgu_ln_b", "sgu_w", "sgu_b",
          "w_out_even", "ffn_w1", "ffn_w3", "ffn_w2", "w_in_odd", "w_out_odd", "router_w", "router_b",
          "moe_w1", "moe_w3", "moe_w2"]
OUTPUTS = [(1, TP, D), (TS, 1, D), (1, 1, TP, 4, 64), (1, 1, TP, 4, 64), (1, 1, TP, 64), (1, 1, 2, CH),
           (1, TS, 1, 4, 64), (1, TS, 1, 4, 64), (1, TS, 1, 64), (1, TS, 2, CH), (1, TS, 1, CH)]


def kernel(**inputs):
    import concourse.bacc as bacc
    from concourse.bass_utils import run_bass_kernel_spmd

    nc = bacc.Bacc("TRN2", target_bir_lowering=False, num_devices=1)
    arrays = {name: np.ascontiguousarray(inputs[name]) for name in INPUTS}
    arrays.update(constants())
    args = [nc.dram_tensor(name, a.shape, mybir.dt.from_np(a.dtype), kind="ExternalInput").ap()
            for name, a in arrays.items()]
    scratch = [nc.dram_tensor(name, shape, F32, kind="Internal").ap()
               for name, shape in (("x_rows", (T, D)), ("r_rows", (ROUNDS * NE * CAP, D)))]
    args += scratch
    args += [nc.dram_tensor(f"out_{i}", shape, F32, kind="ExternalOutput").ap() for i, shape in enumerate(OUTPUTS)]
    build(nc, *args)
    got = run_bass_kernel_spmd(nc, [arrays], core_ids=[0])
    return tuple(got.results[0][f"out_{i}"] for i in range(len(OUTPUTS)))
```
